# Optimizing a Trainium2 kernel written in Bass

```python
import math
import jax, jax.numpy as jnp
from jax import lax
import numpy as np

D_MODEL = 1024
BATCH = 1
SEQ = 512
DEPTH = 2

MEM_LEN = 256
D_MIX = D_MODEL
GLA_WIDTH = 3 * D_MIX // 8
GLA_HEADS = 4
GLA_DV = GLA_WIDTH // GLA_HEADS
GLA_DK = GLA_DV // 2
GLA_RANK = 16
GLA_TAU = 16.0
GLA_CHUNK = 64
DSA_WIDTH = 3 * D_MIX // 8
DSA_DH = 64
DSA_HEADS = DSA_WIDTH // DSA_DH
IDX_HEADS = 8
IDX_DIM = 64
TOPK_MAX = 256
Q_BLOCK = 128
CONV_CH = D_MIX - GLA_WIDTH - DSA_WIDTH
CONV_WIDTH = 31
NUM_BUCKETS = 32
MAX_DISTANCE = 128
X_HEADS = 4
X_DH = 64
N_GROUPS = 4
EXPERTS_PER_GROUP = 4
N_EXPERTS = N_GROUPS * EXPERTS_PER_GROUP
TOPK_EXPERTS = 2
D_EXPERT = 512
NORM_EPS = 1e-6
IN_SIZES = (GLA_HEADS * GLA_DK, GLA_HEADS * GLA_DK, GLA_WIDTH, GLA_RANK, GLA_WIDTH,
            DSA_WIDTH, DSA_WIDTH, DSA_WIDTH, IDX_HEADS * IDX_DIM, IDX_DIM, IDX_HEADS,
            2 * CONV_CH)
D_IN = sum(IN_SIZES)

kernel_name = "hybrid_gla_dsa_conformer_hmoe"

def rms_norm(x, g):
    xf = x.astype(jnp.float32)
    y = xf * lax.rsqrt(jnp.mean(xf * xf, axis=-1, keepdims=True) + NORM_EPS)
    return (y * g.astype(jnp.float32)).astype(x.dtype)

def t5_bucket(dist):
    max_exact = NUM_BUCKETS // 2
    d = jnp.maximum(dist, 1).astype(jnp.float32)
    large = max_exact + (jnp.log(d / max_exact) / math.log(MAX_DISTANCE / max_exact)
                         * (NUM_BUCKETS - max_exact)).astype(jnp.int32)
    large = jnp.minimum(large, NUM_BUCKETS - 1)
    return jnp.where(dist < max_exact, dist, large)

def gla_chunked(q, k, v, log_a):
    B, S, H, DK = q.shape
    DV = v.shape[-1]
    n = S // GLA_CHUNK

    def to_chunks(t):
        return t.astype(jnp.float32).reshape(B, n, GLA_CHUNK, H, t.shape[-1]).transpose(1, 0, 3, 2, 4)

    qc, kc, vc, ac = to_chunks(q * (DK ** -0.5)), to_chunks(k), to_chunks(v), to_chunks(log_a)
    causal = jnp.tril(jnp.ones((GLA_CHUNK, GLA_CHUNK), dtype=bool))

    def step(state, inp):
        qi, ki, vi, ai = inp
        b = jnp.cumsum(ai, axis=-2)
        diff = b[:, :, :, None, :] - b[:, :, None, :, :]
        decay = jnp.exp(jnp.where(causal[:, :, None], diff, -jnp.inf))
        attn = jnp.einsum('bhtd,bhsd,bhtsd->bhts', qi, ki, decay)
        o = (jnp.einsum('bhts,bhsv->bhtv', attn, vi)
             + jnp.einsum('bhtd,bhdv->bhtv', qi * jnp.exp(b), state))
        b_last = b[:, :, -1:, :]
        state = (jnp.exp(b_last[:, :, 0, :])[..., None] * state
                 + jnp.einsum('bhsd,bhsv->bhdv', ki * jnp.exp(b_last - b), vi))
        return state, o

    state0 = jnp.zeros((B, H, DK, DV), jnp.float32)
    _, o = lax.scan(step, state0, (qc, kc, vc, ac))
    return o.transpose(1, 0, 3, 2, 4).reshape(B, S, H, DV)

def dsa_attention(q, k, v, q_idx, k_idx, w_idx, rel_bias, topk):
    B, S, H, DH = q.shape
    n_blk = S // Q_BLOCK
    kf = k.reshape(B, S, H * DH)
    vf = v.reshape(B, S, H * DH)
    key_pos = jnp.arange(S)
    k_idx_f = k_idx.astype(jnp.float32)

    def block(i):
        start = i * Q_BLOCK
        qi = lax.dynamic_slice_in_dim(q, start, Q_BLOCK, axis=1)
        qx = lax.dynamic_slice_in_dim(q_idx, start, Q_BLOCK, axis=1).astype(jnp.float32)
        wx = lax.dynamic_slice_in_dim(w_idx, start, Q_BLOCK, axis=1).astype(jnp.float32)
        tpos = start + jnp.arange(Q_BLOCK)
        dots = jnp.einsum('bthd,bsd->bths', qx, k_idx_f) * (IDX_DIM ** -0.5)
        score = jnp.einsum('bths,bth->bts', jax.nn.relu(dots), wx)
        score = jnp.where(key_pos[None, :] <= tpos[:, None], score, -jnp.inf)
        _, sel = lax.top_k(score, topk)
        valid = sel <= tpos[None, :, None]
        ksel = jax.vmap(lambda kb, ib: kb[ib])(kf, sel).reshape(B, Q_BLOCK, topk, H, DH)
        vsel = jax.vmap(lambda vb, ib: vb[ib])(vf, sel).reshape(B, Q_BLOCK, topk, H, DH)
        logits = jnp.einsum('bthd,btkhd->bhtk', qi, ksel).astype(jnp.float32) * (DH ** -0.5)
        bucket = t5_bucket(jnp.maximum(tpos[None, :, None] - sel, 0))
        logits = logits + rel_bias[bucket].astype(jnp.float32).transpose(0, 3, 1, 2)
        logits = jnp.where(valid[:, None], logits, -jnp.inf)
        p = jax.nn.softmax(logits, axis=-1)
        return jnp.einsum('bhtk,btkhd->bthd', p.astype(vsel.dtype), vsel)

    out = lax.map(block, jnp.arange(n_blk))
    return out.transpose(1, 0, 2, 3, 4).reshape(B, S, H, DH)

def conformer_conv(u, conv_w, conv_b, ln_g, ln_b):
    a, g = jnp.split(u, 2, axis=-1)
    h = a * jax.nn.sigmoid(g)
    h = lax.conv_general_dilated(h, conv_w[:, None, :].astype(h.dtype), window_strides=(1,),
                                 padding=[(CONV_WIDTH - 1, 0)],
                                 dimension_numbers=('NWC', 'WIO', 'NWC'),
                                 feature_group_count=CONV_CH) + conv_b
    hf = h.astype(jnp.float32)
    mu = jnp.mean(hf, axis=-1, keepdims=True)
    var = jnp.mean(jnp.square(hf - mu), axis=-1, keepdims=True)
    y = (hf - mu) * lax.rsqrt(var + NORM_EPS) * ln_g.astype(jnp.float32) + ln_b.astype(jnp.float32)
    return jax.nn.silu(y).astype(u.dtype)

def memory_cross_attention(h, m, w_cq, w_ckv, qn, kn, w_co):
    B, S, _ = h.shape
    M = m.shape[1]
    q = rms_norm((h @ w_cq).reshape(B, S, X_HEADS, X_DH), qn)
    kv = (m @ w_ckv).reshape(B, M, 2, X_HEADS, X_DH)
    k = rms_norm(kv[:, :, 0], kn)
    v = kv[:, :, 1]
    logits = jnp.einsum('bshd,bmhd->bhsm', q, k).astype(jnp.float32) * (X_DH ** -0.5)
    p = jax.nn.softmax(logits, axis=-1)
    o = jnp.einsum('bhsm,bmhd->bshd', p.astype(v.dtype), v).reshape(B, S, X_HEADS * X_DH)
    return o @ w_co

def hierarchical_moe(h, w_rg, b_rg, w_re, b_re, w_gate, w_up, w_down):
    B, S, D = h.shape
    t = h.reshape(B * S, D)
    g_logits = (t @ w_rg + b_rg).astype(jnp.float32)
    g_prob = jax.nn.softmax(g_logits, axis=-1)
    g_sel = jnp.argmax(g_logits, axis=-1)
    g_w = jnp.take_along_axis(g_prob, g_sel[:, None], axis=1)[:, 0]
    e_logits = (t @ w_re + b_re).astype(jnp.float32).reshape(-1, N_GROUPS, EXPERTS_PER_GROUP)
    e_logits = jnp.take_along_axis(e_logits, g_sel[:, None, None], axis=1)[:, 0]
    top_w, top_i = lax.top_k(jax.nn.softmax(e_logits, axis=-1), TOPK_EXPERTS)
    top_w = top_w / jnp.sum(top_w, axis=-1, keepdims=True)
    expert_id = g_sel[:, None] * EXPERTS_PER_GROUP + top_i
    gates = jnp.einsum('tk,tke->te', top_w, jax.nn.one_hot(expert_id, N_EXPERTS, dtype=jnp.float32))
    gates = (gates * g_w[:, None]).astype(t.dtype)
    y = jnp.zeros_like(t)
    for e in range(N_EXPERTS):
        he = jax.nn.silu(t @ w_gate[e]) * (t @ w_up[e])
        y = y + gates[:, e:e + 1] * (he @ w_down[e])
    return y.reshape(B, S, D)

def setup_inputs(seed: int = 0) -> dict:
    key = jax.random.key(seed)
    keys = jax.random.split(key, 32)
    counter = [0]

    def nrm(shape, scale):
        k = keys[counter[0]]
        counter[0] += 1
        return scale * jax.random.normal(k, shape, jnp.float32)

    L = DEPTH
    return {
        "x": nrm((BATCH, SEQ, D_MODEL), 1.0),
        "mem": nrm((BATCH, MEM_LEN, D_MODEL), 1.0),
        "rel_bias": nrm((NUM_BUCKETS, DSA_HEADS), 0.2),
        "norm_mix": 1.0 + nrm((L, D_MODEL), 0.02),
        "w_in": nrm((L, D_MODEL, D_IN), D_MODEL ** -0.5),
        "gla_wa2": nrm((L, GLA_RANK, GLA_HEADS * GLA_DK), GLA_RANK ** -0.5),
        "gla_ba": nrm((L, GLA_HEADS * GLA_DK), 0.1),
        "gla_onorm": 1.0 + nrm((L, GLA_DV), 0.02),
        "dsa_qnorm": 1.0 + nrm((L, DSA_DH), 0.02),
        "dsa_knorm": 1.0 + nrm((L, DSA_DH), 0.02),
        "conv_w": nrm((L, CONV_WIDTH, CONV_CH), CONV_WIDTH ** -0.5),
        "conv_b": nrm((L, CONV_CH), 0.02),
        "conv_ln_g": 1.0 + nrm((L, CONV_CH), 0.02),
        "conv_ln_b": nrm((L, CONV_CH), 0.02),
        "w_out": nrm((L, D_MIX, D_MODEL), D_MIX ** -0.5),
        "norm_x": 1.0 + nrm((L, D_MODEL), 0.02),
        "norm_mem": 1.0 + nrm((L, D_MODEL), 0.02),
        "w_cq": nrm((L, D_MODEL, X_HEADS * X_DH), D_MODEL ** -0.5),
        "w_ckv": nrm((L, D_MODEL, 2 * X_HEADS * X_DH), D_MODEL ** -0.5),
        "x_qnorm": 1.0 + nrm((L, X_DH), 0.02),
        "x_knorm": 1.0 + nrm((L, X_DH), 0.02),
        "w_co": nrm((L, X_HEADS * X_DH, D_MODEL), (X_HEADS * X_DH) ** -0.5),
        "norm_ffn": 1.0 + nrm((L, D_MODEL), 0.02),
        "w_rg": nrm((L, D_MODEL, N_GROUPS), D_MODEL ** -0.5),
        "b_rg": nrm((L, N_GROUPS), 0.01),
        "w_re": nrm((L, D_MODEL, N_EXPERTS), D_MODEL ** -0.5),
        "b_re": nrm((L, N_EXPERTS), 0.01),
        "w_gate": nrm((L, N_EXPERTS, D_MODEL, D_EXPERT), D_MODEL ** -0.5),
        "w_up": nrm((L, N_EXPERTS, D_MODEL, D_EXPERT), D_MODEL ** -0.5),
        "w_down": nrm((L, N_EXPERTS, D_EXPERT, D_MODEL), D_EXPERT ** -0.5),
    }

def reference(x, mem, rel_bias, norm_mix, w_in, gla_wa2, gla_ba, gla_onorm, dsa_qnorm, dsa_knorm,
              conv_w, conv_b, conv_ln_g, conv_ln_b, w_out, norm_x, norm_mem, w_cq, w_ckv,
              x_qnorm, x_knorm, w_co, norm_ffn, w_rg, b_rg, w_re, b_re, w_gate, w_up, w_down):
    B, S, _ = x.shape
    topk = min(TOPK_MAX, S // 4)
    split_at = [int(o) for o in np.cumsum(IN_SIZES)[:-1]]
    for l in range(DEPTH):
        h = rms_norm(x, norm_mix[l])
        z = h @ w_in[l]
        (g_q, g_k, g_v, g_lr, g_r, d_q, d_k, d_v, i_q, i_k, i_w, c_u) = jnp.split(z, split_at, axis=-1)
        log_a = jax.nn.log_sigmoid((g_lr @ gla_wa2[l] + gla_ba[l]).astype(jnp.float32)) / GLA_TAU
        o_gla = gla_chunked(g_q.reshape(B, S, GLA_HEADS, GLA_DK), g_k.reshape(B, S, GLA_HEADS, GLA_DK),
                            g_v.reshape(B, S, GLA_HEADS, GLA_DV), log_a.reshape(B, S, GLA_HEADS, GLA_DK))
        o_gla = rms_norm(o_gla.astype(x.dtype), gla_onorm[l]) * jax.nn.silu(g_r.reshape(B, S, GLA_HEADS, GLA_DV))
        dq = rms_norm(d_q.reshape(B, S, DSA_HEADS, DSA_DH), dsa_qnorm[l])
        dk = rms_norm(d_k.reshape(B, S, DSA_HEADS, DSA_DH), dsa_knorm[l])
        o_dsa = dsa_attention(dq, dk, d_v.reshape(B, S, DSA_HEADS, DSA_DH),
                              i_q.reshape(B, S, IDX_HEADS, IDX_DIM), i_k, i_w * (IDX_HEADS ** -0.5),
                              rel_bias, topk)
        o_conv = conformer_conv(c_u, conv_w[l], conv_b[l], conv_ln_g[l], conv_ln_b[l])
        mix = jnp.concatenate([o_gla.reshape(B, S, GLA_WIDTH), o_dsa.reshape(B, S, DSA_WIDTH), o_conv], axis=-1)
        x = x + mix @ w_out[l]
        x = x + memory_cross_attention(rms_norm(x, norm_x[l]), rms_norm(mem, norm_mem[l]),
                                       w_cq[l], w_ckv[l], x_qnorm[l], x_knorm[l], w_co[l])
        x = x + hierarchical_moe(rms_norm(x, norm_ffn[l]), w_rg[l], b_rg[l], w_re[l], b_re[l],
                                 w_gate[l], w_up[l], w_down[l])
    return x


_drawn_inputs = setup_inputs


def setup_inputs(seed=0):
    import zlib

    import numpy as np

    out = dict(_drawn_inputs(seed))
    spreads = {}
    factors = {'gla_onorm': 2.736,
     'dsa_qnorm': 5.034,
     'dsa_knorm': 6.51,
     'norm_x': 5.073,
     'norm_mem': 4.184,
     'x_qnorm': 6.075,
     'x_knorm': 4.65,
     'b_rg': 4.029,
     'b_re': 3.148}
    for name, (base, spread) in spreads.items():
        noise = np.random.default_rng([zlib.crc32(name.encode()), seed]).standard_normal(out[name].shape)
        drawn = base * np.exp(spread * noise) if base else spread * noise
        out[name] = __import__('jax').numpy.asarray(drawn.astype(out[name].dtype))
    for name, factor in factors.items():
        out[name] = (out[name] * factor).astype(out[name].dtype)
    return out
```

```python
from contextlib import ExitStack

import concourse.bass as bass
from concourse import mybir
import numpy as np

F32 = mybir.dt.float32
I32 = mybir.dt.int32
U32 = mybir.dt.uint32
U8 = mybir.dt.uint8
ALU = mybir.AluOpType
ACT = mybir.ActivationFunctionType
AX = mybir.AxisListType.X

P = 128
D, S, L, M = 1024, 512, 2, 256
KD = D // P
NT = S // P
GH, GK, GV, RANK = 4, 48, 96, 16
AH, AD = 6, 64
IH, ID = 8, 64
TOPK = S // 4
CC, CW = 256, 31
XH, XD = 4, 64
NB, MAXD = 32, 128
NG, EG, E, F = 4, 4, 16, 512
PAIRS = 2 * S
MAXB = E + (PAIRS - E) // P
NBC = MAXB + 1
EPS = 1e-6
SLOT = KD * 512
NSLOT = 3
NEG, TAKEN, FAR = -3.0e38, -3.4e38, -1.0e30
HALVES = [1, 2, 4, 8, 16, 32, 64]
NLEV = len(HALVES)

SIZES = dict(gq=GH * GK, gk=GH * GK, gv=GH * GV, lr=RANK, gr=GH * GV, dq=AH * AD, dk=AH * AD, dv=AH * AD,
             iq=IH * ID, ik=ID, iw=IH, ca=CC, cg=CC)
COL, _at = {}, 0
for _n, _w in SIZES.items():
    COL[_n] = _at
    _at += _w

CHUNKS = [
    [(0, COL["ik"], ID), (ID, COL["ik"], ID), (2 * ID, COL["iw"], IH), (2 * ID + IH, COL["lr"], RANK)],
    [(0, COL["iq"], IH * ID)],
    [(0, COL["ca"], 2 * CC)],
    [(0, COL["dq"], AH * AD)],
    [(0, COL["dk"], AH * AD)],
    [(0, COL["dv"], AH * AD)],
    [(64 * h, COL["gq"] + GK * h, 64) for h in range(GH)] + [(256 + 64 * h, COL["gk"] + GK * h, 64) for h in range(GH)],
    [(0, COL["gv"], GH * GV)],
    [(0, COL["gr"], GH * GV)],
]
LOADS = [sum(len(c) for c in CHUNKS[:i + 1]) for i in range(len(CHUNKS))]


def host_constants():
    p, c = np.arange(P)[:, None], np.arange(P)[None, :]
    ident = (p == c).astype(np.float32)
    same_head = (p // 64 == c // 64).astype(np.float32)
    before = (p < c).astype(np.float32)
    iota = np.broadcast_to(c, (P, P)).astype(np.float32)
    dist = 255 - np.arange(384)
    d = np.maximum(dist, 1).astype(np.float32)
    large = NB // 2 + (np.log(d / np.float32(NB // 2)) / np.float32(np.log(MAXD / (NB // 2))) * (NB // 2)).astype(np.int32)
    bucket = np.where(dist < NB // 2, dist, np.minimum(large, NB - 1))
    onehot = (bucket[None, :] == np.arange(NB)[:, None]) & (dist >= 0)[None, :]
    onehot = onehot.astype(np.float32)
    steps = np.ones((P, S), np.float32)
    steps[:, ::P] = 0.0
    tok = (p + P * np.arange(NT)[None, :]).astype(np.float32)
    cf = np.concatenate([ident, same_head, before, iota, tok, steps], 1)
    masks = []
    for h in HALVES:
        masks.append((p // (2 * h) == c // (2 * h)) & ((c // h) % 2 == 1) & ((p // h) % 2 == 0))
    masks.append(p == c)
    return cf, onehot, np.stack(masks, 1).reshape(P, -1).astype(np.float32)


def program(nc, A, out):
    ctx = ExitStack()
    with ctx:
        def sb(name, shape, dt=F32):
            return ctx.enter_context(nc.sbuf_tensor(name, shape, dt))

        def sem(name):
            s = ctx.enter_context(nc.semaphore(name))
            (pool_dma_sems if name.startswith("pd_") else sems).append(s)
            return s

        def view(t, off, *shape, rows=P):
            n = int(np.prod(shape))
            ap = t[0:rows, off:off + n]
            names = "abcd"[:len(shape)]
            if len(shape) > 1:
                ap = ap.rearrange(f"p ({' '.join(names)}) -> p {' '.join(names)}",
                                  **{names[i]: shape[i] for i in range(1, len(shape))})
            return ap

        sems, pool_dma_sems = [], []

        arena = sb("arena", [P, 6 * SLOT])
        scratch = sb("scratch", [P, 7680])
        x = sb("x", [P, NT, D])
        hT = sb("hT", [P, KD, S])
        cf = sb("cf", [P, 4 * P + NT + S])
        cmask = sb("cmask", [P, (NLEV + 1) * P], U8)
        ones = sb("ones", [P, P])
        toep = sb("toep", [P, AH, 2 * P])
        bfar = sb("bfar", [P, AH])
        mixg = sb("mixg", [P, GH, S])
        mixr = sb("mixr", [P, 5, S])
        sel = sb("sel", [P, NT, S])
        iw = sb("iw", [P, NT, IH])
        sq = sb("sq", [P, 2, S])
        rs = sb("rs", [P, 2, S])
        ik2 = sq[:, 1, :]
        par = sb("par", [P, 64])
        convw = sb("convw", [P, 2, CW + 1])
        wa2 = sb("wa2", [RANK, 2, P])
        m8 = sb("m8", [P, 8])
        small = sb("small", [P, 64])
        epst = sb("epst", [P, 1])
        zero = sb("zero", [P, 256])
        ebl = sb("ebl", [P, 2, NT])
        slots = sb("slots", [P, 2 * NBC])
        slot_tok = sb("slot_tok", [P, NBC], U32)
        pair_slot = sb("pair_slot", [P, NT, 2], U32)
        blk = sb("blk", [1, 128])
        idx = sb("idx", [P, 2, 1], U32)
        gate = sb("gate", [P, 2])
        blki = sb("blki", [1, 32], I32)

        ident, same_head = cf[:, 0:P], cf[:, P:2 * P]
        before, iota = cf[:, 2 * P:3 * P], cf[:, 3 * P:4 * P]
        tok = cf[:, 4 * P:4 * P + NT]
        steps = cf[:, 4 * P + NT:]
        onehot = view(arena, 6144, 384, rows=NB)
        masks = cmask[:, :].rearrange("p (l t) -> p l t", t=P)

        def slot(i):
            return view(arena, i * SLOT, KD, 512)

        up = 3 * SLOT
        gq, gk, b = (view(arena, up + 1024 * i, 2, S) for i in range(3))
        st = view(arena, up + 1024, 3, 2, 2 * GV)
        gv = view(arena, up + 3072, NT, GH * GV)
        gr = view(arena, up + 4608, GH, S, rows=GV)
        AT = view(arena, up + 6656, NT, GH, P)
        qexp, kdec = view(arena, up + 8704, 2, S), view(arena, up + 9728, 2, S)
        kdecT = view(arena, up + 10752, NT, 2, P)
        lrT = view(arena, up + 11776, S, rows=RANK)
        cin = view(arena, up + 8704, 2, S + CW - 1)
        csig = view(arena, up + 8704 + 2 * (S + CW - 1), 2, S)
        xn = view(scratch, 0, 2, D)
        relu = view(scratch, 0, 4, S)
        ld, lq, lk = (view(scratch, 1024 * i, 2, S) for i in range(3))
        lg, bm, pT = (view(scratch, 1024 * i, 2, S) for i in range(3))
        dq, dk = view(scratch, 3072, 3, S), view(scratch, 4608, 3, S)
        dv = view(scratch, 6144, NT, AH * AD)
        iq = mixg[:, :, :]
        wog = view(arena, 0, GH, D, rows=GV)
        wor = view(arena, GH * D, 5, D)
        wckv = view(arena, up, KD, 512)
        wcq = view(arena, up + 4096, KD, 256)
        wco = view(arena, up + 6144, 2, D)
        memT = view(arena, up + 8192, KD, M)
        ckT = view(arena, up + 10240, 2, M)
        cv = view(arena, up + 10752, 2, XH * XD)
        cqT = view(arena, up + 11264, 2, S)
        mem = view(scratch, 2048, 2, D)
        clg, cpT = view(scratch, 4096, 2, M), view(scratch, 4608, 2, 2, P)
        coT = view(scratch, 5120, 2, S)
        oneP, oneB = view(scratch, 6144, 2, P), view(scratch, 6400, 2, 2 * NBC)
        selw = sel[:, :, :].rearrange("p n s -> p (n s)")
        rout = view(selw, 0, NT, 224)
        wr = view(selw, 1024, KD, NG + E)
        wg, wu = [view(arena, (3 * i) * SLOT, KD, F) for i in (0, 1)], [view(arena, (3 * i + 1) * SLOT, KD, F) for i in (0, 1)]
        wd = [view(arena, (3 * i + 2) * SLOT, F // P, D) for i in (0, 1)]
        xg, xgT = view(scratch, 0, 2, D), view(scratch, 2048, 2, KD, P)
        he, heT = view(scratch, 4096, 2, F), view(scratch, 5120, F // P, P)
        yb = view(scratch, 5632, 2, D)
        ya = hT[:, :, :].rearrange("p c t -> p (c t)").rearrange("p (n d) -> p n d", d=D)

        ps = [ctx.enter_context(nc.psum_tensor(f"ps{i}", [P, 512], F32)) for i in range(8)]

        skew = nc.dram_tensor("skew", [P * AH * 384 + 384], F32, kind="Internal").ap()
        hrows = nc.dram_tensor("hrows", [S, D], F32, kind="Internal").ap()
        yrows = nc.dram_tensor("yrows", [MAXB * P, D], F32, kind="Internal").ap()

        PC = dict(gmix=0, gx=8, gmem=16, gffn=24, ba=32, onorm=34, dqn=35, dkn=36, clg=37, clb=39, cqn=41, ckn=42, cb=43)
        NPC = 45
        prow = rs[0:NPC, 1, 0:P]

        def pc(name, i=0, rows=P):
            return par[0:rows, PC[name] + i:PC[name] + i + 1]

        s_const, s_x0, s_cv = sem("constants_in"), sem("x_in"), sem("c_dve")
        s_zt = sem("zero_tile")
        s_skw, s_toep, s_far = sem("skew_written"), sem("toep_in"), sem("far_bias")
        s_w = [sem(f"w_in_slot{i}") for i in range(NSLOT)]
        s_par, s_wa2, s_cwr = sem("params_in"), sem("wa2_in"), sem("conv_taps_in")
        cv_, ca_, cp_ = sem("dve_chain"), sem("act_chain"), sem("pool_chain")
        sN = {n: sem(n) for n in (
            "prow_zero", "par_t", "root_done", "xn_ready", "tr_done", "hT_ready", "proj_done", "proj_out", "dots_done", "relu_done",
            "relu_used", "causal_done", "conv_done", "sq_ready", "sum_done", "sums_root", "normed", "a_done", "sig_abs",
            "sig_ln", "b_ready", "lev_d", "lev_e", "lev_q", "lev_k", "lev_mm", "lev_cp", "at_zero", "eb_done", "el_done",
            "qexp_done", "kdec_done", "kt_done", "kt_out", "upd_done", "state_done", "o_done", "osq", "osum", "oroot",
            "odone", "mean_done", "cen_done", "csq", "var_done", "croot", "cnorm", "lg_done", "bm_done", "lg_out",
            "exp_done", "p_norm", "pt_done", "pt_out", "pv_done", "cw_t", "cw_out", "sel_done", "op_done", "x_mid",
            "xm_root", "xm_xn", "xm_tr", "xm_hT", "mm_root", "mm_xn", "mm_tr", "mm_T", "cp_done", "cp_out", "cn_sq",
            "cn_sum", "cn_root", "cn_done", "cl_done", "c_nm", "c_exp", "c_norm", "c_pt", "c_pto", "c_pv", "c_o",
            "co_done", "x_cross", "f_root", "f_xn", "f_tr", "f_hT", "r_done", "r_lin", "r_exp", "r_hot", "r_rank",
            "r_one", "r_slots", "blk_tr", "blk_xgT", "blk_silu", "blk_h", "blk_htr", "blk_hT", "blk_y", "blk_yo",
            "w_free", "x_free", "mem_in", "wo_in", "wckv_in", "wcq_in", "wco_in", "wr_in", "rb_in", "idx",
            "h_free", "y_read", "blk_gate", "blk_up", "y_added", "er_done",)}
        s_wg, s_wu, s_wd = ([sem(f"{n}{i}") for i in (0, 1)] for n in ("gate_in", "up_in", "down_in"))
        s_ga = [sem(f"pd_rows{i}") for i in (0, 1)]
        s_yg = [sem(f"pd_ygather{i}") for i in range(4)]
        s_hr = [sem(f"hrows_stored{i}") for i in range(NT)]
        s_ys = [sem(f"y_stored{i}") for i in (0, 1)]
        s_out = sem("out_stored")
        s_zero = ctx.enter_context(nc.semaphore("yrows_zeroed"))

        def pair_rows(h, n):
            return slice(64 * (h % 2), 64 * (h % 2) + n)

        count = {}

        def engine(eng, own):
            def do(ins, mark=None, wait=True):
                s = sN[mark] if mark else own
                count[s] = count.get(s, 0) + 1
                ins.then_inc(s, 1)
                if wait:
                    eng.wait_ge(s, count[s])
            return do

        with nc.Block() as block:
            @block.sync
            def _(sp):
                sp.dma_start(cf[:, :], A["cf"]).then_inc(s_const, 16)
                sp.dma_start(view(arena, 7168, (NLEV + 1) * P), A["cmask"]).then_inc(s_const, 16)
                sp.dma_start(onehot, A["onehot"]).then_inc(s_const, 16)
                sp.dma_start(small[0:NB, 0:AH], A["rel_bias"]).then_inc(s_const, 16)
                sp.dma_start(x[:, :, :], A["x"][0].rearrange("(n p) d -> p n d", p=P)).then_inc(s_x0, 16)
                sp.wait_ge(s_far, 2 + AH)
                sp.dma_start(skew[0:P * AH * 384].rearrange("(p h j) -> p h j", h=AH, j=384),
                             view(arena, 0, AH, 384)).then_inc(s_skw, 16)
                sp.wait_ge(s_skw, 16)
                sp.dma_start(toep[:, :, :], bass.AP(tensor=skew.tensor, offset=P - 1,
                                                    ap=[[AH * 384 - 1, P], [384, AH], [1, 2 * P]])).then_inc(s_toep, 16)
                sp.wait_ge(s_toep, 16)
                sp.wait_ge(s_x0, 16)

            @block.scalar
            def _(act):
                act.wait_ge(s_zt, 1)
                act.dma_start(yrows.rearrange("(p n) (c d) -> p (n c) d", p=P, d=256),
                              zero[:, :].unsqueeze(1).to_broadcast([P, MAXB * D // 256, 256])).then_inc(s_zero, 16)

            @block.vector
            def _(dve):
                nc.vector.memset(zero[:, :], 0.0).then_inc(s_zt, 1)
                nc.vector.memset(ones[:, :], 1.0).then_inc(s_cv, 1)
                nc.vector.memset(epst[:, :], EPS).then_inc(s_cv, 1)
                nc.vector.memset(wa2[:, :, :], 0.0).then_inc(s_cv, 1)
                dve.wait_ge(s_const, 64)
                dve.wait_ge(s_cv, 3)
                for h in range(AH):
                    nc.vector.tensor_scalar(view(arena, 4096 + P * h, P, rows=NB), ones[0:NB, :], small[0:NB, h:h + 1],
                                            None, ALU.mult).then_inc(s_cv, 1)
                for h in range(AH):
                    dve.wait_ge(cv_, h + 1)
                    nc.vector.tensor_copy(view(arena, 384 * h, 384), ps[h % 2][:, 0:384]).then_inc(s_far, 1)
                dve.wait_ge(cp_, 1)
                nc.vector.tensor_copy(bfar[:, :], ps[2][:, 0:AH]).then_inc(s_far, 1)
                nc.vector.tensor_copy(cmask[:, :], view(arena, 7168, (NLEV + 1) * P)).then_inc(s_far, 1)

            @block.tensor
            def _(pe):
                pe.wait_ge(s_const, 64)
                for h in range(AH):
                    pe.wait_ge(s_cv, 4 + h)
                    if h >= 2:
                        pe.wait_ge(s_far, h - 1)
                    nc.tensor.matmul(ps[h % 2][:, 0:384], view(arena, 4096 + P * h, P, rows=NB), onehot,
                                     start=True, stop=True).then_inc(cv_, 1)
                for h in range(AH):
                    last = nc.tensor.matmul(ps[2][:, h:h + 1], view(arena, 4096 + P * h, P, rows=NB), onehot[:, 0:1],
                                            start=True, stop=True)
                last.then_inc(cp_, 1)

        with nc.Fori(0, L) as l:
            with nc.Block() as block:
                @block.sync
                def _(sp):
                    for s in sems:
                        sp.sem_clear(s)

                @block.gpsimd
                def _(gp):
                    gp.dma_reset()
                    for s in pool_dma_sems:
                        gp.sem_clear(s)

            def layer(name):
                return A[name][bass.ds(l, 1)]

            PARAMS = [("gmix", "norm_mix", KD, P, 0), ("gx", "norm_x", KD, P, 0), ("gmem", "norm_mem", KD, P, 0),
                      ("gffn", "norm_ffn", KD, P, 0), ("onorm", "gla_onorm", 1, GV, 0),
                      ("clg", "conv_ln_g", 2, P, 0), ("clb", "conv_ln_b", 2, P, 0), ("cb", "conv_b", 2, P, 0)]
            HEADP = [("dqn", "dsa_qnorm"), ("dkn", "dsa_knorm"), ("cqn", "x_qnorm"), ("ckn", "x_knorm")]
            NPAR = len(PARAMS) + 2 * len(HEADP) + GH

            JOBS = [(0, 0, P, "T", "ik", 0), (0, 2 * ID + IH, RANK, "T", "lr", 0)]
            JOBS += [(0, 2 * ID, IH, "tok", "iw", i) for i in range(NT)]
            JOBS += [(1, P * i, P, "T", "iq", i) for i in range(4)]
            JOBS += [(2, P * i, P, "T", "ca", i) for i in range(2)] + [(2, CC + P * i, P, "T", "cg", i) for i in range(2)]
            JOBS += [(3, P * i, P, "T", "dq", i) for i in range(3)] + [(4, P * i, P, "T", "dk", i) for i in range(3)]
            JOBS += [(5, 0, AH * AD, "tok", "dv", i) for i in range(NT)]
            JOBS += [(6, P * i, P, "T", "gq", i) for i in range(2)] + [(6, 2 * P + P * i, P, "T", "gk", i) for i in range(2)]
            JOBS += [(7, 0, GH * GV, "tok", "gv", i) for i in range(NT)]
            JOBS += [(8, GV * i, GV, "T", "gr", i) for i in range(GH)]
            NJ = len(JOBS)

            def done(name):
                return max(n for n, j in enumerate(JOBS) if j[4] == name) + 1

            DEST = dict(ik=lambda i: ik2[:, :], lr=lambda i: lrT, iw=lambda i: iw[:, i, :], iq=lambda i: iq[:, i, :],
                        ca=lambda i: cin[:, i, CW - 1:], cg=lambda i: csig[:, i, :], dq=lambda i: dq[:, i, :],
                        dk=lambda i: dk[:, i, :], dv=lambda i: dv[:, i, :], gq=lambda i: gq[:, i, :],
                        gk=lambda i: gk[:, i, :], gv=lambda i: gv[:, i, :], gr=lambda i: gr[:, i, :])
            AFTER_IDX = done("iq")
            STEPS = [(i, h) for i in range(NT) for h in range(AH)]
            DOTS = [(i, h) for i in range(NT) for h in range(IH)]

            def merge(dve, do, v, c):
                dve.wait_ge(sN["lev_mm"], NT * v + c + 1)
                if v == 0 and c == 0:
                    dve.wait_ge(sN["at_zero"], 1)
                m = masks[:, v, :].unsqueeze(1).unsqueeze(1).to_broadcast([P, 2, 2, P])
                c0 = c - c % 2
                do(nc.vector.copy_predicated(AT[:, c0:c0 + 2, c % 2:GH:2, :], m,
                                             ps[4 + c][:, :].rearrange("p (c h t) -> p c h t", c=2, t=P)), "lev_cp")

            with nc.Block() as block:
                @block.sync
                def _(sp):
                    sp.wait_ge(sN["prow_zero"], 1)
                    for name, src, n, w, _ in PARAMS:
                        sp.dma_start(prow[PC[name]:PC[name] + n, 0:w], layer(src).rearrange("o (c p) -> (o c) p", p=w))\
                          .then_inc(s_par, 16)
                    for name, src in HEADP:
                        for half in (0, 64):
                            sp.dma_start(prow[PC[name]:PC[name] + 1, half:half + 64], layer(src)).then_inc(s_par, 16)
                    for h in range(GH):
                        sp.dma_start(prow[PC["ba"] + h // 2:PC["ba"] + h // 2 + 1, 64 * (h % 2):64 * (h % 2) + GK],
                                     layer("gla_ba")[:, GK * h:GK * h + GK]).then_inc(s_par, 16)
                    w_in = A["w_in"][bass.ds(l, 1)].rearrange("o (c p) n -> p (o c) n", p=P)
                    for n, parts in enumerate(CHUNKS):
                        if n >= NSLOT:
                            sp.wait_ge(sN["proj_done"], max(m for m, j in enumerate(JOBS) if j[0] == n - NSLOT) + 1)
                        for dst, col, width in parts:
                            sp.dma_start(slot(n % NSLOT)[:, :, dst:dst + width], w_in[:, :, col:col + width])\
                              .then_inc(s_w[n % NSLOT], 16)
                        if n == 0:
                            for h in range(GH):
                                sp.dma_start(wa2[:, h // 2, 64 * (h % 2):64 * (h % 2) + GK],
                                             layer("gla_wa2")[:, :, GK * h:GK * h + GK].rearrange("o r c -> (o r) c"))\
                                  .then_inc(s_wa2, 16)
                            sp.dma_start(rs[0:CW, 0, 0:CC], layer("conv_w").rearrange("o j c -> (o j) c")).then_inc(s_cwr, 16)

                @block.tensor
                def _(pe):
                    pe.wait_ge(s_par, 16 * NPAR)
                    nc.tensor.transpose(ps[7][:, 0:NPC], prow, ident[0:NPC, 0:NPC]).then_inc(sN["par_t"], 1)
                    for t in range(NT):
                        pe.wait_ge(sN["xn_ready"], t + 1)
                        for q in range(2):
                            n = 2 * t + q
                            if n >= 2:
                                pe.wait_ge(sN["hT_ready"], n - 1)
                            for c in range(4):
                                last = nc.tensor.transpose(ps[4 + q][:, P * c:P * c + P],
                                                           xn[:, t % 2, P * (4 * q + c):P * (4 * q + c) + P], ident)
                            last.then_inc(sN["tr_done"], 1)
                    pe.wait_ge(sN["hT_ready"], 8)

                    pe.wait_ge(s_cwr, 16)
                    for i in range(2):
                        last = nc.tensor.transpose(ps[6][:, CW * i:CW * i + CW], rs[0:CW, 0, P * i:P * i + P], ident[0:CW, 0:CW])
                    last.then_inc(sN["cw_t"], 1)

                    def project(n):
                        chunk, col, width, kind, name, i = JOBS[n]
                        k = chunk % NSLOT
                        first = JOBS.index(next(j for j in JOBS if j[0] == chunk))
                        if n == first:
                            parts = sum(len(CHUNKS[c]) for c in range(k, chunk + 1, NSLOT))
                            pe.wait_ge(s_w[k], 16 * parts)
                        if n >= 4:
                            pe.wait_ge(sN["proj_out"], n - 3)
                        w = slot(k)
                        for c in range(KD):
                            if kind == "T":
                                last = nc.tensor.matmul(ps[n % 4][0:width, :], w[:, c, col:col + width], hT[:, c, :],
                                                        start=(c == 0), stop=(c == KD - 1))
                            else:
                                last = nc.tensor.matmul(ps[n % 4][:, 0:width], hT[:, c, P * i:P * i + P],
                                                        w[:, c, col:col + width], start=(c == 0), stop=(c == KD - 1))
                        last.then_inc(sN["proj_done"], 1)

                    for n in range(AFTER_IDX):
                        project(n)
                    pe.wait_ge(sN["proj_out"], AFTER_IDX)
                    pe.wait_ge(sN["cw_out"], 1)
                    for n, (i, h) in enumerate(DOTS):
                        if n >= 4:
                            pe.wait_ge(sN["relu_done"], n - 3)
                        r = pair_rows(h, ID)
                        nc.tensor.matmul(ps[4 + n % 4][:, 0:P * (i + 1)], iq[r, h // 2, P * i:P * i + P],
                                         ik2[r, 0:P * (i + 1)], start=True, stop=True).then_inc(sN["dots_done"], 1)
                    for n in range(AFTER_IDX, NJ):
                        project(n)

                    pe.wait_ge(sN["relu_done"], len(DOTS))
                    for n in range(6):
                        pe.wait_ge(sN["sq_ready"], n + 1)
                        if n >= 2:
                            pe.wait_ge(sN["sums_root"], n - 1)
                        nc.tensor.matmul(ps[4 + n % 2][:, :], same_head, sq[:, n % 2, :], start=True, stop=True)\
                          .then_inc(sN["sum_done"], 1)
                    pe.wait_ge(s_wa2, 16 * GH)
                    for i in range(2):
                        nc.tensor.matmul(ps[6 + i][:, :], wa2[:, i, :], lrT, start=True, stop=True).then_inc(sN["a_done"], 1)
                    pe.wait_ge(sN["b_ready"], 2)
                    pe.wait_ge(sN["sums_root"], 6)
                    for v in range(NLEV + 1):
                        if v < NLEV:
                            pe.wait_ge(sN["lev_q"], v + 1)
                            pe.wait_ge(sN["lev_k"], v + 1)
                        qq, kk = (lq, lk) if v < NLEV else (gq, gk)
                        for m in range(4):
                            if v >= 1:
                                pe.wait_ge(sN["lev_cp"], 4 * (v - 1) + m + 1)
                            for c in (m - m % 2, m - m % 2 + 1):
                                for h in (m % 2, m % 2 + 2):
                                    r = pair_rows(h, GK)
                                    at = 2 * P * (c % 2) + P * (h // 2)
                                    last = nc.tensor.matmul(ps[4 + m][:, at:at + P], kk[r, h // 2, P * c:P * c + P],
                                                            qq[r, h // 2, P * c:P * c + P], start=True, stop=True)
                            last.then_inc(sN["lev_mm"], 1)
                    pe.wait_ge(sN["kdec_done"], 1)
                    pe.wait_ge(sN["lev_cp"], NT * (NLEV + 1))
                    for i in range(2):
                        for c in range(NT):
                            last = nc.tensor.transpose(ps[4 + i][:, P * c:P * c + P], kdec[:, i, P * c:P * c + P], ident)
                        last.then_inc(sN["kt_done"], 1)
                    pe.wait_ge(sN["kt_out"], 2)
                    pe.wait_ge(sN["proj_out"], NJ)
                    for c in range(3):
                        for i in range(2):
                            last = nc.tensor.matmul(ps[5 + c][:, 192 * i:192 * i + 192], kdecT[:, c, i, :],
                                                    gv[:, c, 192 * i:192 * i + 192], start=True, stop=True)
                        last.then_inc(sN["upd_done"], 1)
                    pe.wait_ge(sN["qexp_done"], 1)
                    for c in range(NT):
                        if c >= 1:
                            pe.wait_ge(sN["state_done"], c)
                        for h in range(GH):
                            r = pair_rows(h, GK)
                            o = ps[h][0:GV, P * c:P * c + P]
                            last = nc.tensor.matmul(o, gv[:, c, GV * h:GV * h + GV], AT[:, c, h, :], start=True, stop=(c == 0))
                            if c:
                                last = nc.tensor.matmul(o, st[r, c - 1, h // 2, GV * (h % 2):GV * (h % 2) + GV],
                                                        qexp[r, h // 2, P * c:P * c + P], start=False, stop=True)
                    last.then_inc(sN["o_done"], 1)
                    for h in range(GH):
                        pe.wait_ge(sN["osq"], h + 1)
                        if h == 0:
                            pe.wait_ge(sN["state_done"], 3)
                        if h >= 2:
                            pe.wait_ge(sN["oroot"], h - 1)
                        nc.tensor.matmul(ps[4 + h % 2][0:GV, :], ones[0:GV, 0:GV], sq[0:GV, h % 2, :], start=True, stop=True)\
                          .then_inc(sN["osum"], 1)
                    pe.wait_ge(sN["conv_done"], 1)
                    for i in range(2):
                        last = nc.tensor.matmul(ps[6][:, :], ones[:, :], mixr[:, 3 + i, :], start=(i == 0), stop=(i == 1))
                    last.then_inc(sN["mean_done"], 1)
                    pe.wait_ge(sN["csq"], 2)
                    for i in range(2):
                        last = nc.tensor.matmul(ps[7][:, :], ones[:, :], sq[:, i, :], start=(i == 0), stop=(i == 1))
                    last.then_inc(sN["var_done"], 1)
                    pe.wait_ge(sN["normed"], 6)
                    pe.wait_ge(sN["oroot"], 4)
                    pe.wait_ge(sN["croot"], 1)
                    pe.wait_ge(sN["odone"], 4)

                    def logits(n):
                        i, h = STEPS[n]
                        r = pair_rows(h, AD)
                        if n >= 2:
                            pe.wait_ge(sN["lg_out"], n - 1)
                        nc.tensor.matmul(ps[4 + n % 2][:, 0:P * (i + 1)], dq[r, h // 2, P * i:P * i + P],
                                         dk[r, h // 2, 0:P * (i + 1)], start=True, stop=True).then_inc(sN["lg_done"], 1)

                    def turn(n):
                        i, h = STEPS[n]
                        pe.wait_ge(sN["p_norm"], n + 1)
                        if n >= 2:
                            pe.wait_ge(sN["pt_out"], n - 1)
                        for j in range(i + 1):
                            last = nc.tensor.transpose(ps[6 + n % 2][:, P * j:P * j + P], lg[:, n % 2, P * j:P * j + P], ident)
                        last.then_inc(sN["pt_done"], 1)

                    def values(n):
                        i, h = STEPS[n]
                        pe.wait_ge(sN["pt_out"], n + 1)
                        for j in range(i + 1):
                            last = nc.tensor.matmul(ps[h // 2][pair_rows(h, AD), P * i:P * i + P],
                                                    dv[:, j, AD * h:AD * h + AD], pT[:, n % 2, P * j:P * j + P],
                                                    start=(j == 0), stop=(j == i))
                        last.then_inc(sN["pv_done"], 1)

                    logits(0)
                    logits(1)
                    for n in range(len(STEPS)):
                        turn(n)
                        if n + 2 < len(STEPS):
                            logits(n + 2)
                        if n >= 1:
                            values(n - 1)
                    values(len(STEPS) - 1)

                @block.scalar
                def _(act):
                    do = engine(act, ca_)
                    for t in range(NT):
                        if t >= 2:
                            act.wait_ge(sN["tr_done"], 2 * (t - 1))
                        do(nc.scalar.activation(xn[:, t % 2, :], x[:, t, :], ACT.Square, accum_out=small[:, t:t + 1]))
                        do(nc.scalar.activation(small[:, 4 + t:5 + t], small[:, t:t + 1], ACT.Sqrt, bias=epst[:, :],
                                                scale=1.0 / D), "root_done")

                    FUNC = dict(gr=ACT.Silu, cg=ACT.Sigmoid)

                    def evacuate(n):
                        chunk, col, width, kind, name, i = JOBS[n]
                        act.wait_ge(sN["proj_done"], n + 1)
                        if name == "gq" and i == 0:
                            act.wait_ge(sN["at_zero"], 1)
                        src = ps[n % 4][0:width, :] if kind == "T" else ps[n % 4][:, 0:width]
                        scale = GK ** -0.5 if name == "gq" else IH ** -0.5 if name == "iw" else 1.0
                        nc.scalar.activation(DEST[name](i), src, FUNC.get(name, ACT.Copy), scale=scale)\
                          .then_inc(sN["proj_out"], 1)

                    for n in range(AFTER_IDX):
                        evacuate(n)
                    for n, (i, h) in enumerate(DOTS):
                        act.wait_ge(sN["dots_done"], n + 1)
                        if n >= 4:
                            act.wait_ge(sN["relu_used"], n - 3)
                        nc.scalar.activation(relu[:, n % 4, 0:P * (i + 1)], ps[4 + n % 4][:, 0:P * (i + 1)], ACT.Relu,
                                             scale=ID ** -0.5).then_inc(sN["relu_done"], 1)
                    for n in range(AFTER_IDX, NJ):
                        evacuate(n)
                    act.wait_ge(sN["proj_out"], NJ)
                    for n in range(6):
                        t = (dq if n < 3 else dk)[:, n % 3, :]
                        if n >= 2:
                            act.wait_ge(sN["sum_done"], n - 1)
                        do(nc.scalar.activation(sq[:, n % 2, :], t, ACT.Square), "sq_ready", wait=False)
                        act.wait_ge(sN["sum_done"], n + 1)
                        if n >= 2:
                            act.wait_ge(sN["normed"], n - 1)
                        do(nc.scalar.activation(rs[:, n % 2, :], ps[4 + n % 2][:, :], ACT.Sqrt, bias=epst[:, :], scale=1.0 / AD),
                           "sums_root", wait=False)
                    for i in range(2):
                        act.wait_ge(sN["a_done"], i + 1)
                        act.wait_ge(sN["sig_abs"], i + 1)
                        do(nc.scalar.activation(ld[:, i, :], b[:, i, :], ACT.Abs))
                        do(nc.scalar.activation(ld[:, i, :], ld[:, i, :], ACT.Exp, scale=-1.0))
                        do(nc.scalar.activation(ld[:, i, :], ld[:, i, :], ACT.Ln, bias=ones[:, 0:1]), "sig_ln")
                    for v in range(NLEV):
                        act.wait_ge(sN["lev_d"], v + 1)
                        do(nc.scalar.activation(ld, ld, ACT.Abs))
                        do(nc.scalar.activation(ld, ld, ACT.Exp, scale=-1.0), "lev_e")
                    act.wait_ge(sN["lev_q"], NLEV)
                    act.wait_ge(sN["lev_k"], NLEV)
                    do(nc.scalar.activation(ld, b, ACT.Exp), "eb_done")
                    act.wait_ge(sN["el_done"], 1)
                    do(nc.scalar.activation(lq, lq, ACT.Exp, scale=-1.0), "er_done")
                    for i in range(2):
                        act.wait_ge(sN["kt_done"], i + 1)
                        do(nc.scalar.activation(kdecT[:, :, i, :], ps[4 + i][:, :].rearrange("p (c d) -> p c d", d=P), ACT.Copy),
                           "kt_out", wait=False)
                    act.wait_ge(sN["o_done"], 1)
                    for h in range(GH):
                        if h >= 2:
                            act.wait_ge(sN["osum"], h - 1)
                        do(nc.scalar.activation(sq[0:GV, h % 2, :], ps[h][0:GV, :], ACT.Square), "osq", wait=False)
                        act.wait_ge(sN["osum"], h + 1)
                        if h >= 2:
                            act.wait_ge(sN["odone"], h - 1)
                        do(nc.scalar.activation(rs[0:GV, h % 2, :], ps[4 + h % 2][0:GV, :], ACT.Sqrt, bias=epst[0:GV, :],
                                                scale=1.0 / GV), "oroot", wait=False)
                    for i in range(2):
                        act.wait_ge(sN["cen_done"], i + 1)
                        do(nc.scalar.activation(sq[:, i, :], mixr[:, 3 + i, :], ACT.Square), "csq", wait=False)
                    act.wait_ge(sN["var_done"], 1)
                    act.wait_ge(sN["odone"], 4)
                    do(nc.scalar.activation(rs[:, 0, :], ps[7][:, :], ACT.Sqrt, bias=epst[:, :], scale=1.0 / CC), "croot")
                    act.wait_ge(sN["cnorm"], 2)
                    for i in range(2):
                        do(nc.scalar.activation(mixr[:, 3 + i, :], mixr[:, 3 + i, :], ACT.Silu, scale=pc("clg", i),
                                                bias=pc("clb", i)), wait=False)

                    def exps(n):
                        i, h = STEPS[n]
                        act.wait_ge(sN["lg_out"], n + 1)
                        s = lg[:, n % 2, 0:P * (i + 1)]
                        nc.scalar.activation(s, s, ACT.Exp, bias=small[:, 8 + n % 2:9 + n % 2],
                                             accum_out=small[:, 10 + n % 2:11 + n % 2]).then_inc(sN["exp_done"], 1)

                    def turned(n):
                        i, h = STEPS[n]
                        act.wait_ge(sN["pt_done"], n + 1)
                        if n >= 2:
                            act.wait_ge(sN["pv_done"], n - 1)
                        nc.scalar.activation(pT[:, n % 2, 0:P * (i + 1)], ps[6 + n % 2][:, 0:P * (i + 1)], ACT.Copy)\
                          .then_inc(sN["pt_out"], 1)

                    exps(0)
                    for n in range(len(STEPS)):
                        if n + 1 < len(STEPS):
                            exps(n + 1)
                        turned(n)

                @block.vector
                def _(dve):
                    do = engine(dve, cv_)
                    do(nc.vector.memset(prow, 0.0), "prow_zero")
                    dve.wait_ge(sN["par_t"], 1)
                    do(nc.vector.tensor_copy(par[:, 0:NPC], ps[7][:, 0:NPC]))
                    for t in range(NT):
                        dve.wait_ge(sN["root_done"], t + 1)
                        do(nc.vector.reciprocal(small[:, 12 + t:13 + t], small[:, 4 + t:5 + t]))
                        do(nc.vector.tensor_scalar(xn[:, t % 2, :], x[:, t, :], small[:, 12 + t:13 + t], None, ALU.mult), "xn_ready")
                        for q in range(2):
                            dve.wait_ge(sN["tr_done"], 2 * t + q + 1)
                            g = par[:, PC["gmix"] + 4 * q:PC["gmix"] + 4 * q + 4].unsqueeze(2).to_broadcast([P, 4, P])
                            do(nc.vector.tensor_tensor(hT[:, 4 * q:4 * q + 4, P * t:P * t + P],
                                                       ps[4 + q][:, :].rearrange("p (c t) -> p c t", t=P), g, ALU.mult), "hT_ready",
                               wait=False)
                    dve.wait_ge(sN["cw_t"], 1)
                    do(nc.vector.tensor_copy(convw[:, :, 0:CW], ps[6][:, 0:2 * CW].rearrange("p (i j) -> p i j", j=CW)), "cw_out")
                    dve.wait_ge(sN["proj_out"], done("iw"))
                    for n, (i, h) in enumerate(DOTS):
                        s = sel[:, i, 0:P * (i + 1)]
                        dve.wait_ge(sN["relu_done"], n + 1)
                        r, w = relu[:, n % 4, 0:P * (i + 1)], iw[:, i, h:h + 1]
                        if h == 0:
                            ins = nc.vector.tensor_scalar(s, r, w, None, ALU.mult)
                        else:
                            ins = nc.vector.scalar_tensor_tensor(s, r, w, s, ALU.mult, ALU.add)
                        do(ins, "relu_used")
                    for i in range(NT):
                        dve.wait_ge(sN["causal_done"], i + 1)
                        s = sel[:, i, 0:P * (i + 1)]
                        if i == 0:
                            do(nc.vector.tensor_scalar(s, s, 0.9 * NEG, FAR, ALU.is_lt, ALU.mult))
                            continue
                        for _ in range(TOPK // 8):
                            do(nc.vector.max(m8[:, :], s))
                            do(nc.vector.match_replace(s, m8[:, :], s, TAKEN))
                        do(nc.vector.tensor_scalar(s, s, 0.5 * (NEG + TAKEN), FAR, ALU.is_gt, ALU.mult))
                    do(nc.vector.memset(small[:, 60:61], 0.0), "sel_done")
                    do(nc.vector.memset(cin[:, :, 0:CW - 1], 0.0))
                    dve.wait_ge(sN["proj_out"], done("cg"))
                    for i in range(2):
                        do(nc.vector.tensor_tensor(cin[:, i, CW - 1:], cin[:, i, CW - 1:], csig[:, i, :], ALU.mult))
                        o = mixr[:, 3 + i, :]
                        do(nc.vector.tensor_scalar(o, cin[:, i, 0:S], convw[:, i, 0:1], pc("cb", i), ALU.mult, ALU.add))
                        for j in range(1, CW):
                            do(nc.vector.scalar_tensor_tensor(o, cin[:, i, j:j + S], convw[:, i, j:j + 1], o, ALU.mult, ALU.add))
                    do(nc.vector.memset(small[:, 60:61], 0.0), "conv_done")
                    for n in range(6):
                        t = (dq if n < 3 else dk)[:, n % 3, :]
                        dve.wait_ge(sN["sums_root"], n + 1)
                        do(nc.vector.reciprocal(rs[:, n % 2, :], rs[:, n % 2, :]))
                        do(nc.vector.scalar_tensor_tensor(t, t, pc("dqn" if n < 3 else "dkn"), rs[:, n % 2, :], ALU.mult, ALU.mult),
                           "normed")
                    for i in range(2):
                        dve.wait_ge(sN["a_done"], i + 1)
                        do(nc.vector.tensor_scalar(b[:, i, :], ps[6 + i][:, :], pc("ba", i), None, ALU.add), "sig_abs")
                    for i in range(2):
                        dve.wait_ge(sN["sig_ln"], i + 1)
                        do(nc.vector.scalar_tensor_tensor(b[:, i, :], b[:, i, :], 0.0, ld[:, i, :], ALU.min, ALU.subtract))
                        do(nc.vector.tensor_scalar(b[:, i, :], b[:, i, :], 1.0 / 16.0, None, ALU.mult))
                        do(nc.vector.tensor_tensor_scan(lq[:, i, :], steps, b[:, i, :], 0.0, ALU.mult, ALU.add))
                        do(nc.vector.tensor_copy(b[:, i, :], lq[:, i, :]), "b_ready")
                    for v, half in enumerate(HALVES):
                        if v >= 1:
                            dve.wait_ge(sN["lev_k"], v)
                        bv = b.rearrange("p i t -> p (i t)").rearrange("p (n w) -> p n w", w=2 * half)
                        dvw = ld.rearrange("p i t -> p (i t)").rearrange("p (n w) -> p n w", w=2 * half)
                        do(nc.vector.tensor_tensor(dvw, bv, bv[:, :, half - 1:half].to_broadcast([P, 2 * S // (2 * half), 2 * half]),
                                                   ALU.subtract), "lev_d")
                        if v >= 1:
                            for c in range(NT):
                                merge(dve, do, v - 1, c)
                        dve.wait_ge(sN["lev_e"], v + 1)
                        do(nc.vector.tensor_tensor(lq, gq, ld, ALU.mult), "lev_q")
                    for v in (NLEV - 1, NLEV):
                        for c in range(NT):
                            merge(dve, do, v, c)
                    bc = b.rearrange("p i t -> p (i t)").rearrange("p (n w) -> p n w", w=P)
                    do(nc.vector.tensor_tensor(lq.rearrange("p i t -> p (i t)").rearrange("p (n w) -> p n w", w=P), bc,
                                               bc[:, :, P - 1:P].to_broadcast([P, 2 * NT, P]), ALU.subtract), "el_done")
                    dve.wait_ge(sN["eb_done"], 1)
                    do(nc.vector.tensor_tensor(qexp, gq, ld, ALU.mult), "qexp_done")
                    do(nc.vector.tensor_copy(ebl[:, :, :], ld.rearrange("p i (c t) -> p i c t", t=P)[:, :, :, P - 1]))
                    dve.wait_ge(sN["er_done"], 1)
                    do(nc.vector.tensor_tensor(kdec, gk, lq, ALU.mult), "kdec_done")
                    for c in range(3):
                        dve.wait_ge(sN["upd_done"], c + 1)
                        for i in range(2):
                            u = ps[5 + c][:, 192 * i:192 * i + 192]
                            if c == 0:
                                ins = nc.vector.tensor_copy(st[:, 0, i, :], u)
                            else:
                                ins = nc.vector.scalar_tensor_tensor(st[:, c, i, :], st[:, c - 1, i, :], ebl[:, i, c:c + 1], u,
                                                                     ALU.mult, ALU.add)
                            do(ins, "state_done" if i else None)
                    for h in range(GH):
                        dve.wait_ge(sN["oroot"], h + 1)
                        r = rs[0:GV, h % 2, :]
                        do(nc.vector.reciprocal(r, r))
                        do(nc.vector.scalar_tensor_tensor(r, ps[h][0:GV, :], pc("onorm", 0, GV), r, ALU.mult, ALU.mult))
                        do(nc.vector.tensor_tensor(mixg[0:GV, h, :], r, gr[:, h, :], ALU.mult), "odone")
                    dve.wait_ge(sN["mean_done"], 1)
                    for i in range(2):
                        do(nc.vector.scalar_tensor_tensor(mixr[:, 3 + i, :], ps[6][:, :], -1.0 / CC, mixr[:, 3 + i, :], ALU.mult,
                                                          ALU.add), "cen_done")
                    dve.wait_ge(sN["croot"], 1)
                    do(nc.vector.reciprocal(rs[:, 1, :], rs[:, 0, :]))
                    for i in range(2):
                        do(nc.vector.tensor_tensor(mixr[:, 3 + i, :], mixr[:, 3 + i, :], rs[:, 1, :], ALU.mult), "cnorm")

                    def masked(n):
                        i, h = STEPS[n]
                        w = P * (i + 1)
                        dve.wait_ge(sN["lg_done"], n + 1)
                        dve.wait_ge(sN["bm_done"], n + 1)
                        if n >= 2:
                            dve.wait_ge(sN["pt_done"], n - 1)
                        s = lg[:, n % 2, 0:w]
                        do(nc.vector.scalar_tensor_tensor(s, ps[4 + n % 2][:, 0:w], AD ** -0.5, bm[:, n % 2, 0:w], ALU.mult, ALU.add))
                        do(nc.vector.reduce_max(small[:, 16 + n % 2:17 + n % 2], s, AX))
                        do(nc.vector.tensor_scalar(small[:, 8 + n % 2:9 + n % 2], small[:, 16 + n % 2:17 + n % 2], -1.0, None,
                                                   ALU.mult), "lg_out")

                    def normalise(n):
                        i, h = STEPS[n]
                        s = lg[:, n % 2, 0:P * (i + 1)]
                        dve.wait_ge(sN["exp_done"], n + 1)
                        do(nc.vector.reciprocal(small[:, 18:19], small[:, 10 + n % 2:11 + n % 2]))
                        do(nc.vector.tensor_scalar(s, s, small[:, 18:19], None, ALU.mult), "p_norm")

                    masked(0)
                    for n in range(len(STEPS)):
                        if n + 1 < len(STEPS):
                            masked(n + 1)
                        normalise(n)
                    dve.wait_ge(sN["pv_done"], len(STEPS))
                    for i in range(3):
                        do(nc.vector.tensor_copy(mixr[:, i, :], ps[i][:, :]))

                @block.gpsimd
                def _(gp):
                    do = engine(gp, cp_)
                    do(nc.gpsimd.memset(AT, 0.0), "at_zero")
                    for i in range(NT):
                        gp.wait_ge(sN["relu_used"], IH * (i + 1))
                        s = sel[:, i, P * i:P * i + P]
                        do(nc.gpsimd.affine_select(out=s, in_=s, pattern=[[-1, P]], compare_op=ALU.is_ge, fill=NEG, base=0,
                                                   channel_multiplier=1), "causal_done")
                    for v in range(NLEV):
                        gp.wait_ge(sN["lev_e"], v + 1)
                        if v >= 1:
                            gp.wait_ge(sN["lev_mm"], NT * v)
                        else:
                            gp.wait_ge(sN["proj_out"], NJ)
                        do(nc.gpsimd.tensor_tensor(lk, gk, ld, ALU.mult), "lev_k")
                    gp.wait_ge(sN["sel_done"], 1)
                    gp.wait_ge(sN["kdec_done"], 1)
                    gp.wait_ge(sN["lev_mm"], NT * NLEV)
                    for n, (i, h) in enumerate(STEPS):
                        if n >= 2:
                            gp.wait_ge(sN["lg_out"], n - 1)
                        near = 2 if i else 1
                        w0 = P * (i + 1 - near)
                        if w0:
                            do(nc.gpsimd.tensor_scalar(bm[:, n % 2, 0:w0], sel[:, i, 0:w0], bfar[:, h:h + 1], None, ALU.add))
                        do(nc.gpsimd.tensor_tensor(bm[:, n % 2, w0:P * (i + 1)], sel[:, i, w0:P * (i + 1)],
                                                   toep[:, h, 2 * P - P * near:2 * P], ALU.add), "bm_done")

            XSTEPS = [(t, h) for t in range(NT) for h in range(XH)]
            HALF = [(t, q) for t in range(NT) for q in range(2)]

            def rows_squared(act, do, rows, nt, root, freed):
                for t in range(nt):
                    freed(act, t)
                    do(nc.scalar.activation(xn[:, t % 2, :], rows[:, t, :], ACT.Square, accum_out=small[:, t:t + 1]))
                    do(nc.scalar.activation(small[:, 4 + t:5 + t], small[:, t:t + 1], ACT.Sqrt, bias=epst[:, :], scale=1.0 / D), root)

            def rows_turned(pe, nt, ready, bank, tr, out):
                for t in range(nt):
                    pe.wait_ge(sN[ready], t + 1)
                    for q in range(2):
                        n = 2 * t + q
                        if n >= 2:
                            pe.wait_ge(sN[out], n - 1)
                        for c in range(4):
                            last = nc.tensor.transpose(ps[bank + q][:, P * c:P * c + P],
                                                       xn[:, t % 2, P * (4 * q + c):P * (4 * q + c) + P], ident)
                        last.then_inc(sN[tr], 1)

            def rows_normed(dve, do, rows, nt, root, ready, tr, bank, gain, dest, out, freed=None):
                for t in range(nt):
                    dve.wait_ge(sN[root], t + 1)
                    do(nc.vector.reciprocal(small[:, 12 + t:13 + t], small[:, 4 + t:5 + t]))
                    do(nc.vector.tensor_scalar(xn[:, t % 2, :], rows[:, t, :], small[:, 12 + t:13 + t], None, ALU.mult), ready)
                    for q in range(2):
                        dve.wait_ge(sN[tr], 2 * t + q + 1)
                        g = par[:, PC[gain] + 4 * q:PC[gain] + 4 * q + 4].unsqueeze(2).to_broadcast([P, 4, P])
                        do(nc.vector.tensor_tensor(dest[:, 4 * q:4 * q + 4, P * t:P * t + P],
                                                   ps[bank + q][:, :].rearrange("p (c t) -> p c t", t=P), g, ALU.mult), out)

            with nc.Block() as block:
                @block.sync
                def _(sp):
                    w = A["w_out"][bass.ds(l, 1)]
                    sp.dma_start(mem, A["mem"][0].rearrange("(n p) d -> p n d", p=P)).then_inc(sN["mem_in"], 16)
                    sp.dma_start(wog, w[:, 0:GH * GV, :].rearrange("o (h v) n -> v (o h) n", v=GV)).then_inc(sN["wo_in"], 16)
                    sp.dma_start(wor, w[:, GH * GV:D, :].rearrange("o (c p) n -> p (o c) n", p=P)).then_inc(sN["wo_in"], 16)
                    sp.dma_start(wckv, layer("w_ckv").rearrange("o (c p) n -> p (o c) n", p=P)).then_inc(sN["wckv_in"], 16)
                    sp.dma_start(wcq, layer("w_cq").rearrange("o (c p) n -> p (o c) n", p=P)).then_inc(sN["wcq_in"], 16)
                    sp.dma_start(wco, layer("w_co").rearrange("o (c p) n -> p (o c) n", p=P)).then_inc(sN["wco_in"], 16)
                    sp.dma_start(wr[:, :, 0:NG], layer("w_rg").rearrange("o (c p) n -> p (o c) n", p=P)).then_inc(sN["wr_in"], 16)
                    sp.dma_start(wr[:, :, NG:NG + E], layer("w_re").rearrange("o (c p) n -> p (o c) n", p=P)).then_inc(sN["wr_in"], 16)
                    sp.dma_start(blk[:, 0:NG], layer("b_rg")).then_inc(sN["rb_in"], 16)
                    sp.dma_start(blk[:, NG:NG + E], layer("b_re")).then_inc(sN["rb_in"], 16)
                    for t in range(NT):
                        sp.wait_ge(sN["f_xn"], t + 1)
                        sp.dma_start(hrows[P * t:P * t + P, :], xn[:, t % 2, :]).then_inc(s_hr[t], 16)
                    for t in range(NT):
                        sp.wait_ge(s_hr[t], 16)

                @block.tensor
                def _(pe):
                    rows_turned(pe, 2, "mm_xn", 2, "mm_tr", "mm_T")
                    pe.wait_ge(sN["wo_in"], 32)
                    for n, (t, q) in enumerate(HALF):
                        if n >= 2:
                            pe.wait_ge(sN["x_mid"], n - 1)
                        for c in range(GH + 5):
                            if c < GH:
                                a, w = mixg[0:GV, c, P * t:P * t + P], wog[:, c, 512 * q:512 * q + 512]
                            else:
                                a, w = mixr[:, c - GH, P * t:P * t + P], wor[:, c - GH, 512 * q:512 * q + 512]
                            last = nc.tensor.matmul(ps[n % 2][:, :], a, w, start=(c == 0), stop=(c == GH + 4))
                        last.then_inc(sN["op_done"], 1)
                    pe.wait_ge(sN["mm_T"], 4)
                    pe.wait_ge(sN["wckv_in"], 16)
                    for i in range(2):
                        for c in range(KD):
                            last = nc.tensor.matmul(ps[4][:, M * i:M * i + M], wckv[:, c, P * i:P * i + P], memT[:, c, :],
                                                    start=(c == 0), stop=(c == KD - 1))
                    last.then_inc(sN["cp_done"], 1)
                    for i in range(2):
                        for c in range(KD):
                            last = nc.tensor.matmul(ps[5][:, 256 * i:256 * i + 256], memT[:, c, P * i:P * i + P],
                                                    wckv[:, c, 256:512], start=(c == 0), stop=(c == KD - 1))
                    last.then_inc(sN["cp_done"], 1)
                    rows_turned(pe, NT, "xm_xn", 6, "xm_tr", "xm_hT")
                    pe.wait_ge(sN["xm_hT"], 8)
                    pe.wait_ge(sN["wcq_in"], 16)
                    for i in range(2):
                        for c in range(KD):
                            last = nc.tensor.matmul(ps[2 + i][:, :], wcq[:, c, P * i:P * i + P], hT[:, c, :],
                                                    start=(c == 0), stop=(c == KD - 1))
                        last.then_inc(sN["cp_done"], 1)
                    pe.wait_ge(sN["x_mid"], 8)
                    for n in range(3):
                        pe.wait_ge(sN["cn_sq"], n + 1)
                        if n >= 2:
                            pe.wait_ge(sN["cn_root"], n - 1)
                        nc.tensor.matmul(ps[n % 2][:, :], same_head, sq[:, n % 2, :], start=True, stop=True)\
                          .then_inc(sN["cn_sum"], 1)
                    pe.wait_ge(sN["cn_done"], 3)

                    def logits(n):
                        t, h = XSTEPS[n]
                        r = pair_rows(h, XD)
                        if n >= 2:
                            pe.wait_ge(sN["c_exp"], n - 1)
                        nc.tensor.matmul(ps[4 + n % 2][:, 0:M], cqT[r, h // 2, P * t:P * t + P], ckT[r, h // 2, :],
                                         start=True, stop=True).then_inc(sN["cl_done"], 1)

                    def values(n):
                        t, h = XSTEPS[n]
                        pe.wait_ge(sN["c_pto"], n + 1)
                        for j in range(2):
                            last = nc.tensor.matmul(ps[h // 2][pair_rows(h, XD), P * t:P * t + P],
                                                    cv[:, j, XD * h:XD * h + XD], cpT[:, n % 2, j, :], start=(j == 0), stop=(j == 1))
                        last.then_inc(sN["c_pv"], 1)

                    pe.wait_ge(sN["cp_out"], 1)
                    logits(0)
                    logits(1)
                    for n in range(len(XSTEPS)):
                        pe.wait_ge(sN["c_norm"], n + 1)
                        if n >= 2:
                            pe.wait_ge(sN["c_pto"], n - 1)
                        for j in range(2):
                            last = nc.tensor.transpose(ps[6 + n % 2][:, P * j:P * j + P], clg[:, n % 2, P * j:P * j + P], ident)
                        last.then_inc(sN["c_pt"], 1)
                        if n + 2 < len(XSTEPS):
                            logits(n + 2)
                        if n >= 1:
                            values(n - 1)
                    values(len(XSTEPS) - 1)
                    pe.wait_ge(sN["c_o"], 2)
                    pe.wait_ge(sN["wco_in"], 16)
                    for n, (t, q) in enumerate(HALF):
                        if n >= 2:
                            pe.wait_ge(sN["x_cross"], n - 1)
                        for c in range(2):
                            last = nc.tensor.matmul(ps[2 + n % 2][:, :], coT[:, c, P * t:P * t + P], wco[:, c, 512 * q:512 * q + 512],
                                                    start=(c == 0), stop=(c == 1))
                        last.then_inc(sN["co_done"], 1)
                    rows_turned(pe, NT, "f_xn", 6, "f_tr", "f_hT")
                    pe.wait_ge(sN["f_hT"], 8)
                    pe.wait_ge(sN["wr_in"], 32)
                    pe.wait_ge(sN["rb_in"], 32)
                    for t in range(NT):
                        o = ps[4][:, 32 * t:32 * t + NG + E]
                        for c in range(KD):
                            nc.tensor.matmul(o, hT[:, c, P * t:P * t + P], wr[:, c, :], start=(c == 0), stop=False)
                        last = nc.tensor.matmul(o, ones[0:1, :], blk[:, 0:NG + E], start=False, stop=True)
                    last.then_inc(sN["r_done"], 1)
                    pe.wait_ge(sN["r_hot"], 1)
                    for t in range(NT):
                        for j in range(t):
                            nc.tensor.matmul(ps[5][:, E * t:E * t + E], ones[:, :], rout[:, j, 80:96], start=(j == 0), stop=False)
                        nc.tensor.matmul(ps[5][:, E * t:E * t + E], before, rout[:, t, 80:96], start=(t == 0), stop=True)
                    for t in range(NT):
                        last = nc.tensor.matmul(ps[5][:, 64:64 + E], ones[:, :], rout[:, t, 80:96], start=(t == 0), stop=(t == NT - 1))
                    last.then_inc(sN["r_rank"], 1)
                    for n in range(2 * NT):
                        pe.wait_ge(sN["r_one"], n + 1)
                        last = nc.tensor.matmul(ps[4][:, 256:256 + 2 * NBC], oneP[:, n % 2, :], oneB[:, n % 2, :],
                                                start=(n == 0), stop=(n == 2 * NT - 1))
                        last.then_inc(sN["r_slots"], 1)

                @block.scalar
                def _(act):
                    do = engine(act, ca_)
                    act.wait_ge(sN["mem_in"], 16)
                    rows_squared(act, do, mem, 2, "mm_root", lambda e, t: None)

                    def freed_x(e, t):
                        e.wait_ge(sN["x_mid"], 2 * t + 2)
                        e.wait_ge(sN["mm_tr"], 4)
                        if t >= 2:
                            e.wait_ge(sN["xm_tr"], 2 * (t - 1))

                    rows_squared(act, do, x, NT, "xm_root", freed_x)
                    act.wait_ge(sN["cp_done"], 2)
                    do(nc.scalar.activation(cv, ps[5][:, :].rearrange("p (i n) -> p i n", i=2), ACT.Copy), "cp_out", wait=False)
                    for n in range(3):
                        src = ps[4] if n == 0 else ps[1 + n]
                        act.wait_ge(sN["cp_done"], 1 if n == 0 else n + 2)
                        if n >= 2:
                            act.wait_ge(sN["cn_sum"], n - 1)
                        do(nc.scalar.activation(sq[:, n % 2, :], src[:, :], ACT.Square), "cn_sq", wait=False)
                        act.wait_ge(sN["cn_sum"], n + 1)
                        if n >= 2:
                            act.wait_ge(sN["cn_done"], n - 1)
                        do(nc.scalar.activation(rs[:, n % 2, :], ps[n % 2][:, :], ACT.Sqrt, bias=epst[:, :], scale=1.0 / XD),
                           "cn_root", wait=False)

                    def exps(n):
                        act.wait_ge(sN["c_nm"], n + 1)
                        if n >= 2:
                            act.wait_ge(sN["c_pt"], n - 1)
                        nc.scalar.activation(clg[:, n % 2, :], ps[4 + n % 2][:, 0:M], ACT.Exp, bias=small[:, 20 + n % 2:21 + n % 2],
                                             scale=XD ** -0.5, accum_out=small[:, 22 + n % 2:23 + n % 2]).then_inc(sN["c_exp"], 1)

                    exps(0)
                    for n in range(len(XSTEPS)):
                        if n + 1 < len(XSTEPS):
                            exps(n + 1)
                        act.wait_ge(sN["c_pt"], n + 1)
                        if n >= 2:
                            act.wait_ge(sN["c_pv"], n - 1)
                        nc.scalar.activation(cpT[:, n % 2, :, :], ps[6 + n % 2][:, 0:2 * P].rearrange("p (j t) -> p j t", t=P),
                                             ACT.Copy).then_inc(sN["c_pto"], 1)
                    act.wait_ge(sN["c_pv"], len(XSTEPS))
                    for i in range(2):
                        do(nc.scalar.activation(coT[:, i, :], ps[i][:, :], ACT.Copy), "c_o", wait=False)

                    def freed_f(e, t):
                        e.wait_ge(sN["x_cross"], 2 * t + 2)
                        if t >= 2:
                            e.wait_ge(sN["f_tr"], 2 * (t - 1))
                            e.wait_ge(s_hr[t - 2], 16)

                    rows_squared(act, do, x, NT, "f_root", freed_f)
                    act.wait_ge(sN["r_lin"], 1)
                    do(nc.scalar.activation(rout[:, :, 24:28], rout[:, :, 24:28], ACT.Exp), "r_exp")
                    act.wait_ge(sN["r_lin"], 2)
                    do(nc.scalar.activation(rout[:, :, 44:45], rout[:, :, 44:45], ACT.Exp), "r_exp")

                @block.vector
                def _(dve):
                    do = engine(dve, cv_)
                    V = nc.vector
                    rows_normed(dve, do, mem, 2, "mm_root", "mm_xn", "mm_tr", 2, "gmem", memT, "mm_T")
                    for n, (t, q) in enumerate(HALF):
                        dve.wait_ge(sN["op_done"], n + 1)
                        xt = x[:, t, 512 * q:512 * q + 512]
                        do(V.tensor_tensor(xt, xt, ps[n % 2][:, :], ALU.add), "x_mid")
                    rows_normed(dve, do, x, NT, "xm_root", "xm_xn", "xm_tr", 6, "gx", hT, "xm_hT")
                    for n in range(3):
                        src, dst = (ps[4], ckT.rearrange("p i m -> p (i m)")) if n == 0 else (ps[1 + n], cqT[:, n - 1, :])
                        dve.wait_ge(sN["cn_root"], n + 1)
                        do(V.reciprocal(rs[:, n % 2, :], rs[:, n % 2, :]))
                        do(V.scalar_tensor_tensor(dst, src[:, :], pc("cqn" if n else "ckn"), rs[:, n % 2, :], ALU.mult, ALU.mult),
                           "cn_done")

                    def row_max(n):
                        dve.wait_ge(sN["cl_done"], n + 1)
                        do(V.reduce_max(small[:, 24:25], ps[4 + n % 2][:, 0:M], AX))
                        do(V.tensor_scalar(small[:, 20 + n % 2:21 + n % 2], small[:, 24:25], -XD ** -0.5, None, ALU.mult), "c_nm")

                    row_max(0)
                    for n in range(len(XSTEPS)):
                        if n + 1 < len(XSTEPS):
                            row_max(n + 1)
                        dve.wait_ge(sN["c_exp"], n + 1)
                        do(V.reciprocal(small[:, 25:26], small[:, 22 + n % 2:23 + n % 2]))
                        do(V.tensor_scalar(clg[:, n % 2, :], clg[:, n % 2, :], small[:, 25:26], None, ALU.mult), "c_norm")
                    for n, (t, q) in enumerate(HALF):
                        dve.wait_ge(sN["co_done"], n + 1)
                        xt = x[:, t, 512 * q:512 * q + 512]
                        do(V.tensor_tensor(xt, xt, ps[2 + n % 2][:, :], ALU.add), "x_cross")
                    rows_normed(dve, do, x, NT, "f_root", "f_xn", "f_tr", 6, "gffn", hT, "f_hT")

                    def R(a, b):
                        return rout[:, :, a:b]

                    def spread(ap, n):
                        return ap.to_broadcast([P, NT, n])

                    def first_largest(v, hot, m):
                        do(V.reduce_max(m, v, AX))
                        do(V.tensor_tensor(R(48, 52), v, spread(m, 4), ALU.is_equal))
                        do(V.tensor_tensor(R(48, 52), R(48, 52), rout[:, :, 220:224], ALU.mult))
                        do(V.reduce_max(R(52, 53), R(48, 52), AX))
                        do(V.tensor_tensor(hot, R(48, 52), spread(R(52, 53), 4), ALU.is_equal))

                    for t in range(NT):
                        do(V.tensor_scalar(rout[:, t, 220:224], iota[:, 0:4], -1.0, 8.0, ALU.mult, ALU.add))
                    dve.wait_ge(sN["r_done"], 1)
                    do(V.tensor_copy(R(0, NG + E), ps[4][:, 0:P].rearrange("p (t n) -> p t n", n=32)[:, :, 0:NG + E]))
                    first_largest(R(0, 4), R(20, 24), R(40, 41))
                    do(V.tensor_tensor(R(24, 28), R(0, 4), spread(R(40, 41), 4), ALU.subtract), "r_lin")
                    el4 = R(4, 20).rearrange("p t (g e) -> p t g e", e=EG)
                    w16 = R(112, 128).rearrange("p t (g e) -> p t g e", e=EG)
                    do(V.tensor_tensor(w16, el4, R(20, 24).unsqueeze(3).to_broadcast([P, NT, NG, EG]), ALU.mult))
                    do(V.tensor_reduce(R(28, 32), w16.rearrange("p t g e -> p t e g"), AX, ALU.add))
                    first_largest(R(28, 32), R(32, 36), R(42, 43))
                    do(V.scalar_tensor_tensor(R(54, 58), R(32, 36), NEG, R(28, 32), ALU.mult, ALU.add))
                    first_largest(R(54, 58), R(36, 40), R(43, 44))
                    do(V.tensor_tensor(R(44, 45), R(43, 44), R(42, 43), ALU.subtract), "r_lin")
                    dve.wait_ge(sN["r_exp"], 1)
                    do(V.reduce_sum(R(41, 42), R(24, 28), AX))
                    dve.wait_ge(sN["r_exp"], 2)
                    do(V.tensor_scalar(R(58, 59), R(44, 45), 1.0, None, ALU.add))
                    do(V.tensor_tensor(R(58, 59), R(58, 59), R(41, 42), ALU.mult))
                    do(V.reciprocal(R(136, 137), R(58, 59)))
                    do(V.tensor_tensor(R(137, 138), R(136, 137), R(44, 45), ALU.mult))
                    for k in range(2):
                        hot = R(140 + 16 * k, 156 + 16 * k).rearrange("p t (g e) -> p t g e", e=EG)
                        do(V.tensor_tensor(hot, R(20, 24).unsqueeze(3).to_broadcast([P, NT, NG, EG]),
                                           R(32 + 4 * k, 36 + 4 * k).unsqueeze(2).to_broadcast([P, NT, NG, EG]), ALU.mult))
                    do(V.tensor_tensor(R(80, 96), R(140, 156), R(156, 172), ALU.add), "r_hot")
                    dve.wait_ge(sN["r_rank"], 1)
                    cnt, nbk, cum, exc = (rout[:, 0, 172:188], rout[:, 1, 172:188], rout[:, 2, 172:188], rout[:, 3, 172:188])
                    do(V.tensor_copy(cnt, ps[5][:, 64:64 + E]))
                    do(V.tensor_copy(R(96, 112), ps[5][:, 0:64].rearrange("p (t e) -> p t e", e=E)))
                    do(V.tensor_scalar(nbk, cnt, 0.0, None, ALU.is_gt))
                    for k in range(1, S // P):
                        do(V.scalar_tensor_tensor(nbk, cnt, float(P * k), nbk, ALU.is_gt, ALU.add))
                    do(V.tensor_tensor_scan(cum, ones[:, 0:E], nbk, 0.0, ALU.mult, ALU.add))
                    do(V.tensor_tensor(exc, cum, nbk, ALU.subtract))
                    for k in range(2):
                        hot = R(140 + 16 * k, 156 + 16 * k)
                        do(V.tensor_tensor(R(112, 128), hot, R(96, 112), ALU.mult))
                        do(V.reduce_sum(R(128 + k, 129 + k), R(112, 128), AX))
                        do(V.tensor_tensor(R(112, 128), hot, exc.unsqueeze(1).to_broadcast([P, NT, E]), ALU.mult))
                        do(V.reduce_sum(R(130 + k, 131 + k), R(112, 128), AX))
                    do(V.tensor_scalar(R(132, 134), R(128, 130), float(P), None, ALU.is_ge))
                    for k in range(2, S // P):
                        do(V.scalar_tensor_tensor(R(132, 134), R(128, 130), float(P * k), R(132, 134), ALU.is_ge, ALU.add))
                    do(V.scalar_tensor_tensor(R(134, 136), R(132, 134), -float(P), R(128, 130), ALU.mult, ALU.add))
                    do(V.tensor_tensor(R(130, 132), R(130, 132), R(132, 134), ALU.add))
                    do(V.scalar_tensor_tensor(R(138, 140), R(130, 132), float(P), R(134, 136), ALU.mult, ALU.add))
                    do(V.tensor_copy(pair_slot[:, :, :], R(138, 140)))
                    for n in range(2 * NT):
                        t, k = n // 2, n % 2
                        if n >= 2:
                            dve.wait_ge(sN["r_slots"], n - 1)
                        do(V.tensor_scalar(oneP[:, n % 2, :], iota, rout[:, t, 134 + k:135 + k], None, ALU.is_equal))
                        do(V.tensor_scalar(oneB[:, n % 2, 0:NBC], iota[:, 0:NBC], rout[:, t, 130 + k:131 + k], tok[:, t:t + 1],
                                           ALU.is_equal, ALU.mult))
                        do(V.tensor_scalar(oneB[:, n % 2, NBC:2 * NBC], iota[:, 0:NBC], rout[:, t, 130 + k:131 + k],
                                           rout[:, t, 136 + k:137 + k], ALU.is_equal, ALU.mult), "r_one")
                    w = sq[0:1, 0, 0:NBC * E].rearrange("p (b e) -> p b e", e=E)
                    do(V.tensor_tensor(w, iota[0:1, 0:NBC].unsqueeze(2).to_broadcast([1, NBC, E]),
                                       cum[0:1, :].unsqueeze(1).to_broadcast([1, NBC, E]), ALU.is_ge))
                    do(V.reduce_sum(blk[:, 32:32 + NBC], w, AX))
                    do(V.tensor_scalar(blk[:, 32:32 + NBC], blk[:, 32:32 + NBC], float(E - 1), None, ALU.min))
                    tot = rout[0:1, 2, 187:188]
                    do(V.tensor_scalar(blk[:, 64:76], iota[0:1, 1:13], 2.0, tot, ALU.mult, ALU.is_le))
                    do(V.reduce_sum(blk[:, 32 + NBC:33 + NBC], blk[:, 64:76], AX))
                    do(V.scalar_tensor_tensor(blk[:, 33 + NBC:34 + NBC], blk[:, 32 + NBC:33 + NBC], -2.0, tot, ALU.mult, ALU.add))
                    do(V.tensor_copy(blki[:, 0:NBC + 2], blk[:, 32:34 + NBC]))
                    dve.wait_ge(sN["r_slots"], 2 * NT)
                    do(V.tensor_copy(slots[:, :], ps[4][:, 256:256 + 2 * NBC]))
                    do(V.tensor_copy(slot_tok[:, :], slots[:, 0:NBC]))

            def expert_blocks(eng, block_fn):
                pairs = eng.value_load(blki[0:1, NBC:NBC + 1], min_val=PAIRS // S // 2, max_val=MAXB // 2)
                odd = eng.value_load(blki[0:1, NBC + 1:NBC + 2], min_val=0, max_val=1)
                with eng.Fori(0, pairs) as j:
                    block_fn(j, 0)
                    block_fn(j, 1)
                with eng.If(odd > 0):
                    block_fn(pairs, 0)
                return pairs, odd

            with nc.Block() as block:
                @block.sync
                def _(sp):
                    sp.sem_inc(sN["w_free"], 2)
                    sp.sem_inc(s_ys[0], 16)
                    sp.sem_inc(s_ys[1], 16)

                    def body(j, u):
                        e = sp.value_load(blki[0:1, bass.ds(2 * j + u, 1)], min_val=0, max_val=E - 1)
                        sp.wait_ge(sN["w_free"], 2 * j + (u + 1))
                        for name, dst, s in (("w_gate", wg, s_wg), ("w_up", wu, s_wu), ("w_down", wd, s_wd)):
                            src = A[name][bass.ds(l, 1), bass.ds(e, 1)].rearrange("o e (c p) n -> p (o e c) n", p=P)
                            sp.dma_start(dst[u], src).then_inc(s[u], 16)

                    expert_blocks(sp, body)

                @block.gpsimd
                def _(gp):
                    gp.sem_inc(sN["x_free"], 1)

                    def gather(j, u, col):
                        nc.gpsimd.tensor_copy(idx[:, u, :], slot_tok[:, col]).then_inc(sN["idx"], 1)

                    nc.gpsimd.tensor_copy(idx[:, 0, :], slot_tok[:, 0:1]).then_inc(sN["idx"], 1)
                    gp.wait_ge(sN["idx"], 1)
                    gp.indirect_dma_start(out=xg[:, 0, :], out_offset=None, in_=hrows,
                                          in_offset=bass.IndirectOffsetOnAxis(ap=idx[:, 0, :], axis=0)).then_inc(s_ga[0], 16)

                    def body(j, u):
                        v = 1 - u
                        gp.wait_ge(sN["x_free"], 2 * j + (u + 1))
                        gp.nop(nofuse=True)
                        nc.gpsimd.tensor_copy(idx[:, v, :], slot_tok[:, bass.ds(2 * j + (u + 1), 1)]).then_inc(sN["idx"], 1)
                        gp.wait_ge(sN["idx"], 2 * j + (u + 2))
                        gp.nop(nofuse=True)
                        gp.indirect_dma_start(out=xg[:, v, :], out_offset=None, in_=hrows,
                                              in_offset=bass.IndirectOffsetOnAxis(ap=idx[:, v, :], axis=0)).then_inc(s_ga[v], 16)

                    expert_blocks(gp, body)

                @block.tensor
                def _(pe):
                    def turn(u, need):
                        pe.wait_ge(s_ga[u], need)
                        for q in range(2):
                            for c in range(4):
                                last = nc.tensor.transpose(ps[4 + q][:, P * c:P * c + P],
                                                           xg[:, u, P * (4 * q + c):P * (4 * q + c) + P], ident)
                            last.then_inc(sN["blk_tr" if q == 0 else "x_free"], 1)

                    turn(0, 16)

                    def body(j, u):
                        g1 = 2 * j + (u + 1)
                        for bank, w, s in ((0, wg, s_wg), (1, wu, s_wu)):
                            pe.wait_ge(s[u], 16 * j + 16)
                            if bank == 0:
                                pe.wait_ge(sN["blk_xgT"], g1)
                                pe.wait_ge(sN["h_free"], g1)
                            for c in range(KD):
                                last = nc.tensor.matmul(ps[bank][:, :], xgT[:, u, c, :], w[u][:, c, :],
                                                        start=(c == 0), stop=(c == KD - 1))
                            last.then_inc(sN["blk_gate" if bank == 0 else "blk_up"], 1)
                        turn(1 - u, 16 * j + (16 if u == 0 else 32))
                        pe.wait_ge(sN["blk_h"], g1)
                        for c in range(F // P):
                            last = nc.tensor.transpose(ps[6][:, P * c:P * c + P], he[:, u, P * c:P * c + P], ident)
                        last.then_inc(sN["blk_htr"], 1)
                        pe.wait_ge(sN["blk_hT"], g1)
                        pe.wait_ge(s_wd[u], 16 * j + 16)
                        pe.wait_ge(sN["y_read"], g1)
                        for q in range(2):
                            for c in range(F // P):
                                last = nc.tensor.matmul(ps[2 + q][:, :], heT[:, c, :], wd[u][:, c, 512 * q:512 * q + 512],
                                                        start=(c == 0), stop=(c == F // P - 1))
                            last.then_inc(sN["blk_y" if q == 0 else "w_free"], 1)

                    expert_blocks(pe, body)

                @block.scalar
                def _(act):
                    act.wait_ge(s_zero, 16)

                    def body(j, u):
                        g1 = 2 * j + (u + 1)
                        act.wait_ge(sN["blk_gate"], g1)
                        nc.scalar.activation(he[:, u, :], ps[0][:, :], ACT.Silu).then_inc(sN["blk_silu"], 1)
                        act.wait_ge(sN["blk_htr"], g1)
                        nc.scalar.activation(heT, ps[6][:, :].rearrange("p (c t) -> p c t", t=P), ACT.Copy).then_inc(sN["blk_hT"], 1)
                        act.wait_ge(sN["blk_yo"], 2 * g1)
                        act.dma_start(yrows[bass.ds(2 * P * j + P * u, P), :], yb[:, u, :]).then_inc(s_ys[u], 16)

                    pairs, odd = expert_blocks(act, body)
                    act.wait_ge(s_ys[0], 16 * (pairs + odd) + 16)
                    act.nop(nofuse=True)
                    act.wait_ge(s_ys[1], 16 * pairs + 16)
                    act.nop(nofuse=True)

                @block.vector
                def _(dve):
                    dve.sem_inc(sN["h_free"], 1)
                    dve.sem_inc(sN["y_read"], 1)

                    def channel_major(u):
                        for q in range(2):
                            g = par[:, PC["gffn"] + 4 * q:PC["gffn"] + 4 * q + 4].unsqueeze(2).to_broadcast([P, 4, P])
                            last = nc.vector.tensor_tensor(xgT[:, u, 4 * q:4 * q + 4, :],
                                                           ps[4 + q][:, :].rearrange("p (c t) -> p c t", t=P), g, ALU.mult)
                        last.then_inc(sN["blk_xgT"], 1)

                    dve.wait_ge(sN["x_free"], 2)
                    channel_major(0)

                    def body(j, u):
                        g1 = 2 * j + (u + 1)
                        dve.wait_ge(sN["x_free"], g1 + 2)
                        channel_major(1 - u)
                        dve.wait_ge(sN["blk_silu"], g1)
                        dve.wait_ge(sN["blk_up"], g1)
                        nc.vector.tensor_tensor(he[:, u, :], he[:, u, :], ps[1][:, :], ALU.mult).then_inc(sN["blk_h"], 1)
                        nc.vector.tensor_copy(gate[:, u:u + 1], slots[:, bass.ds(2 * j + (NBC + u), 1)]).then_inc(sN["h_free"], 1)
                        dve.wait_ge(sN["h_free"], g1 + 1)
                        dve.wait_ge(s_ys[u], 16 * j + 16)
                        dve.wait_ge(sN["w_free"], g1 + 2)
                        for q in range(2):
                            nc.vector.tensor_scalar(yb[:, u, 512 * q:512 * q + 512], ps[2 + q][:, :], gate[:, u:u + 1], None,
                                                    ALU.mult).then_inc(sN["blk_yo"], 1)
                        dve.wait_ge(sN["blk_yo"], 2 * g1)
                        dve.sem_inc(sN["y_read"], 1)

                    expert_blocks(dve, body)

            with nc.Block() as block:
                @block.gpsimd
                def _(gp):
                    for n in range(2 * NT):
                        t, k = n // 2, n % 2
                        if n >= 4:
                            gp.wait_ge(sN["y_added"], n - 3)
                        gp.indirect_dma_start(out=ya[:, n % 4, :], out_offset=None, in_=yrows,
                                              in_offset=bass.IndirectOffsetOnAxis(ap=pair_slot[:, t, k:k + 1], axis=0))\
                          .then_inc(s_yg[n % 4], 16)

                @block.vector
                def _(dve):
                    for n in range(2 * NT):
                        t, k = n // 2, n % 2
                        dve.wait_ge(s_yg[n % 4], 16 * (n // 4 + 1))
                        if k:
                            dve.wait_ge(sN["y_added"], n)
                        nc.vector.tensor_tensor(x[:, t, :], x[:, t, :], ya[:, n % 4, :], ALU.add).then_inc(sN["y_added"], 1)

        with nc.Block() as block:
            @block.sync
            def _(sp):
                sp.dma_start(out[0].rearrange("(n p) d -> p n d", p=P), x[:, :, :]).then_inc(s_out, 16)
                sp.wait_ge(s_out, 16)


_INS = ["x", "mem", "rel_bias", "norm_mix", "w_in", "gla_wa2", "gla_ba", "gla_onorm", "dsa_qnorm", "dsa_knorm", "conv_w",
        "conv_b", "conv_ln_g", "conv_ln_b", "w_out", "norm_x", "norm_mem", "w_cq", "w_ckv", "x_qnorm", "x_knorm", "w_co",
        "norm_ffn", "w_rg", "b_rg", "w_re", "b_re", "w_gate", "w_up", "w_down"]


def kernel(**inputs):
    import concourse.bacc as _bacc
    from concourse.bass_utils import run_bass_kernel_spmd as _run

    nc = _bacc.Bacc("TRN2", target_bir_lowering=False, num_devices=1)
    arrays, handles = {}, {}
    cf, onehot, cmask = host_constants()
    for name, a in [(n, inputs[n]) for n in _INS] + [("cf", cf), ("onehot", onehot), ("cmask", cmask)]:
        a = np.ascontiguousarray(a)
        arrays[f"in_{name}"] = a
        handles[name] = nc.dram_tensor(f"in_{name}", a.shape, mybir.dt.from_np(a.dtype), kind="ExternalInput").ap()
    out = nc.dram_tensor("out_0", (1, S, D), F32, kind="ExternalOutput").ap()
    program(nc, handles, out)
    r = _run(nc, [arrays], core_ids=[0])
    return r.results[0]["out_0"]
```

```python
from contextlib import ExitStack

import concourse.bass as bass
from concourse import mybir
import numpy as np

F32 = mybir.dt.float32
I32 = mybir.dt.int32
U32 = mybir.dt.uint32
U8 = mybir.dt.uint8
F32R = mybir.dt.float32r
ALU = mybir.AluOpType
ACT = mybir.ActivationFunctionType
AX = mybir.AxisListType.X

P = 128
D, S, L, M = 1024, 512, 2, 256
KD = D // P
NT = S // P
GH, GK, GV, RANK = 4, 48, 96, 16
AH, AD = 6, 64
IH, ID = 8, 64
TOPK = S // 4
CC, CW = 256, 31
XH, XD = 4, 64
NB, MAXD = 32, 128
NG, EG, E, F = 4, 4, 16, 512
PAIRS = 2 * S
MAXB = E + (PAIRS - E) // P
NBC = MAXB + 1
EPS = 1e-6
SLOT = KD * 512
NSLOT = 3
NEG, TAKEN, FAR = -3.0e38, -3.4e38, -1.0e30
HALVES = [1, 2, 4, 8, 16, 32, 64]
NLEV = len(HALVES)

SIZES = dict(gq=GH * GK, gk=GH * GK, gv=GH * GV, lr=RANK, gr=GH * GV, dq=AH * AD, dk=AH * AD, dv=AH * AD,
             iq=IH * ID, ik=ID, iw=IH, ca=CC, cg=CC)
COL, _at = {}, 0
for _n, _w in SIZES.items():
    COL[_n] = _at
    _at += _w

CHUNKS = [
    [(0, COL["ik"], ID), (ID, COL["ik"], ID), (2 * ID, COL["iw"], IH), (2 * ID + IH, COL["lr"], RANK)],
    [(0, COL["iq"], IH * ID)],
    [(0, COL["ca"], 2 * CC)],
    [(0, COL["dq"], AH * AD)],
    [(0, COL["dk"], AH * AD)],
    [(0, COL["dv"], AH * AD)],
    [(64 * h, COL["gq"] + GK * h, 64) for h in range(GH)] + [(256 + 64 * h, COL["gk"] + GK * h, 64) for h in range(GH)],
    [(0, COL["gv"], GH * GV)],
    [(0, COL["gr"], GH * GV)],
]
LOADS = [sum(len(c) for c in CHUNKS[:i + 1]) for i in range(len(CHUNKS))]


def host_constants():
    p, c = np.arange(P)[:, None], np.arange(P)[None, :]
    ident = (p == c).astype(np.float32)
    same_head = (p // 64 == c // 64).astype(np.float32)
    before = (p < c).astype(np.float32)
    iota = np.broadcast_to(c, (P, P)).astype(np.float32)
    dist = 255 - np.arange(384)
    d = np.maximum(dist, 1).astype(np.float32)
    large = NB // 2 + (np.log(d / np.float32(NB // 2)) / np.float32(np.log(MAXD / (NB // 2))) * (NB // 2)).astype(np.int32)
    bucket = np.where(dist < NB // 2, dist, np.minimum(large, NB - 1))
    onehot = (bucket[None, :] == np.arange(NB)[:, None]) & (dist >= 0)[None, :]
    onehot = onehot.astype(np.float32)
    steps = np.ones((P, S), np.float32)
    steps[:, ::P] = 0.0
    tok = (p + P * np.arange(NT)[None, :]).astype(np.float32)
    cf = np.concatenate([ident, same_head, before, iota, tok, steps], 1)
    masks = []
    for h in HALVES:
        masks.append((p // (2 * h) == c // (2 * h)) & ((c // h) % 2 == 1) & ((p // h) % 2 == 0))
    masks.append(p == c)
    return cf, onehot, np.stack(masks, 1).reshape(P, -1).astype(np.float32)


def program(nc, A, out):
    ctx = ExitStack()
    with ctx:
        def sb(name, shape, dt=F32):
            return ctx.enter_context(nc.sbuf_tensor(name, shape, dt))

        def sem(name):
            s = ctx.enter_context(nc.semaphore(name))
            (pool_dma_sems if name.startswith("pd_") else sems).append(s)
            return s

        def view(t, off, *shape, rows=P):
            n = int(np.prod(shape))
            ap = t[0:rows, off:off + n]
            names = "abcd"[:len(shape)]
            if len(shape) > 1:
                ap = ap.rearrange(f"p ({' '.join(names)}) -> p {' '.join(names)}",
                                  **{names[i]: shape[i] for i in range(1, len(shape))})
            return ap

        sems, pool_dma_sems = [], []

        x = sb("x", [P, NT, D])
        cf = sb("cf", [P, 4 * P + NT + S])
        cmask = sb("cmask", [P, (NLEV + 1) * P], U8)
        ones = sb("ones", [P, P])
        toep = sb("toep", [P, AH, 2 * P])
        bfar = sb("bfar", [P, AH])
        iw = sb("iw", [P, NT, IH])
        par = sb("par", [P, 64])
        convw = sb("convw", [P, 2, CW + 1])
        wa2 = sb("wa2", [RANK, 2, P])
        m8 = sb("m8", [P, 8])
        small = sb("small", [P, 64])
        epst = sb("epst", [P, 1])
        zero = sb("zero", [P, 256])
        ebl = sb("ebl", [P, 2, NT])
        slots = sb("slots", [P, 2 * NBC])
        slot_tok = sb("slot_tok", [P, NBC], U32)
        pair_slot = sb("pair_slot", [P, NT, 2], U32)
        blk = sb("blk", [1, 128])
        idx = sb("idx", [P, 1], U32)
        gate = sb("gate", [P, 1])
        blki = sb("blki", [1, 32], I32)

        ident, same_head = cf[:, 0:P], cf[:, P:2 * P]
        before, iota = cf[:, 2 * P:3 * P], cf[:, 3 * P:4 * P]
        tok = cf[:, 4 * P:4 * P + NT]
        steps = cf[:, 4 * P + NT:]
        masks = cmask[:, :].rearrange("p (l t) -> p l t", t=P)

        ps = [ctx.enter_context(nc.psum_tensor(f"ps{i}", [P, 512], F32)) for i in range(8)]

        skew = nc.dram_tensor("skew", [P * AH * 384 + 384], F32, kind="Internal").ap()
        hrows = nc.dram_tensor("hrows", [S, D], F32, kind="Internal").ap()
        yrows = nc.dram_tensor("yrows", [MAXB * P, D], F32, kind="Internal").ap()

        PC = dict(gmix=0, gx=8, gmem=16, gffn=24, ba=32, onorm=34, dqn=35, dkn=36, clg=37, clb=39, cqn=41, ckn=42, cb=43)
        NPC = 45

        def pc(name, i=0, rows=P):
            return par[0:rows, PC[name] + i:PC[name] + i + 1]

        s_const, s_x0, s_cv = sem("constants_in"), sem("x_in"), sem("c_dve")
        s_zt = sem("zero_tile")
        s_skw, s_toep, s_far = sem("skew_written"), sem("toep_in"), sem("far_bias")
        s_w = [sem(f"w_in_slot{i}") for i in range(NSLOT)]
        s_par, s_wa2, s_cwr = sem("params_in"), sem("wa2_in"), sem("conv_taps_in")
        cv_, ca_, cp_ = sem("dve_chain"), sem("act_chain"), sem("pool_chain")
        sN = {n: sem(n) for n in (
            "prow_zero", "par_t", "root_done", "xn_ready", "tr_done", "hT_ready", "proj_done", "proj_out", "dots_done",
            "relu_done", "relu_used", "causal_done", "conv_done", "sq_ready", "sum_done", "sums_root", "normed",
            "a_done", "sig_abs", "sig_ln", "b_ready", "lev_d", "lev_e", "lev_q", "lev_k", "lev_mm", "lev_cp", "at_zero",
            "eb_done", "el_done", "qexp_done", "kdec_done", "kt_done", "kt_out", "upd_done", "state_done", "o_done",
            "osq", "osum", "oroot", "odone", "mean_done", "cen_done", "csq", "var_done", "croot", "cnorm", "lg_done",
            "bm_done", "lg_out", "exp_done", "p_norm", "pt_done", "pt_out", "pv_done", "cw_t", "cw_out", "sel_done",
            "op_done", "x_mid", "xm_root", "xm_xn", "xm_tr", "xm_hT", "mm_root", "mm_xn", "mm_tr", "mm_T", "cp_done",
            "cp_out", "cn_sq", "cn_sum", "cn_root", "cn_done", "cl_done", "c_nm", "c_exp", "c_norm", "c_pt", "c_pto",
            "c_pv", "c_o", "co_done", "x_cross", "f_root", "f_xn", "f_tr", "f_hT", "r_done", "r_lin", "r_exp", "r_hot",
            "r_rank", "r_one", "r_slots", "blk_tr", "blk_silu", "blk_h", "blk_htr", "x_free", "mem_in", "wo_in",
            "wckv_in", "wcq_in", "wco_in", "wr_in", "rb_in", "idx", "y_read", "y_added", "er_done", "blk_xh", "blk_xl",
            "blk_hh", "blk_hl", "gate_in",)}
        s_raw, s_head, s_split, s_used = ([sem(f"{n}_{q}") for q in ("gate", "up", "down")]
                                          for n in ("raw_in", "head_done", "rest_done", "products_done"))
        s_ga = sem("pd_rows")
        s_yg = [sem(f"pd_ygather{i}") for i in range(4)]
        s_hr = [sem(f"hrows_stored{i}") for i in range(NT)]
        s_ys = sem("y_rows_stored")
        s_out = sem("out_stored")
        s_zero = ctx.enter_context(nc.semaphore("yrows_zeroed"))

        def pair_rows(h, n):
            return slice(64 * (h % 2), 64 * (h % 2) + n)

        count = {}

        def engine(eng, own):
            def do(ins, mark=None, wait=True):
                s = sN[mark] if mark else own
                count[s] = count.get(s, 0) + 1
                ins.then_inc(s, 1)
                if wait:
                    eng.wait_ge(s, count[s])
            return do

        once = ExitStack()
        arena = once.enter_context(nc.sbuf_tensor("tables", [P, 8192], F32))
        onehot = view(arena, 6144, 384, rows=NB)
        with nc.Block() as block:
            @block.sync
            def _(sp):
                sp.dma_start(cf[:, :], A["cf"]).then_inc(s_const, 16)
                sp.dma_start(view(arena, 7168, (NLEV + 1) * P), A["cmask"]).then_inc(s_const, 16)
                sp.dma_start(onehot, A["onehot"]).then_inc(s_const, 16)
                sp.dma_start(small[0:NB, 0:AH], A["rel_bias"]).then_inc(s_const, 16)
                sp.dma_start(x[:, :, :], A["x"][0].rearrange("(n p) d -> p n d", p=P)).then_inc(s_x0, 16)
                sp.wait_ge(s_far, 2 + AH)
                sp.dma_start(skew[0:P * AH * 384].rearrange("(p h j) -> p h j", h=AH, j=384),
                             view(arena, 0, AH, 384)).then_inc(s_skw, 16)
                sp.wait_ge(s_skw, 16)
                sp.dma_start(toep[:, :, :], bass.AP(tensor=skew.tensor, offset=P - 1,
                                                    ap=[[AH * 384 - 1, P], [384, AH], [1, 2 * P]])).then_inc(s_toep, 16)
                sp.wait_ge(s_toep, 16)
                sp.wait_ge(s_x0, 16)

            @block.scalar
            def _(act):
                act.wait_ge(s_zt, 1)
                act.dma_start(yrows.rearrange("(p n) (c d) -> p (n c) d", p=P, d=256),
                              zero[:, :].unsqueeze(1).to_broadcast([P, MAXB * D // 256, 256])).then_inc(s_zero, 16)

            @block.vector
            def _(dve):
                nc.vector.memset(zero[:, :], 0.0).then_inc(s_zt, 1)
                nc.vector.memset(ones[:, :], 1.0).then_inc(s_cv, 1)
                nc.vector.memset(epst[:, :], EPS).then_inc(s_cv, 1)
                nc.vector.memset(wa2[:, :, :], 0.0).then_inc(s_cv, 1)
                dve.wait_ge(s_const, 64)
                dve.wait_ge(s_cv, 3)
                for h in range(AH):
                    nc.vector.tensor_scalar(view(arena, 4096 + P * h, P, rows=NB), ones[0:NB, :], small[0:NB, h:h + 1],
                                            None, ALU.mult).then_inc(s_cv, 1)
                for h in range(AH):
                    dve.wait_ge(cv_, h + 1)
                    nc.vector.tensor_copy(view(arena, 384 * h, 384), ps[h % 2][:, 0:384]).then_inc(s_far, 1)
                dve.wait_ge(cp_, 1)
                nc.vector.tensor_copy(bfar[:, :], ps[2][:, 0:AH]).then_inc(s_far, 1)
                nc.vector.tensor_copy(cmask[:, :], view(arena, 7168, (NLEV + 1) * P)).then_inc(s_far, 1)

            @block.tensor
            def _(pe):
                pe.wait_ge(s_const, 64)
                for h in range(AH):
                    pe.wait_ge(s_cv, 4 + h)
                    if h >= 2:
                        pe.wait_ge(s_far, h - 1)
                    nc.tensor.matmul(ps[h % 2][:, 0:384], view(arena, 4096 + P * h, P, rows=NB), onehot,
                                     start=True, stop=True).then_inc(cv_, 1)
                for h in range(AH):
                    last = nc.tensor.matmul(ps[2][:, h:h + 1], view(arena, 4096 + P * h, P, rows=NB), onehot[:, 0:1],
                                            start=True, stop=True)
                last.then_inc(cp_, 1)

        once.close()
        with nc.Fori(0, L) as l:
            with nc.Block() as block:
                @block.sync
                def _(sp):
                    for s in sems:
                        sp.sem_clear(s)

                @block.gpsimd
                def _(gp):
                    gp.dma_reset()
                    for s in pool_dma_sems:
                        gp.sem_clear(s)

            mem_a = ExitStack()

            def sba(name, shape):
                return mem_a.enter_context(nc.sbuf_tensor(name, shape, F32))

            arena = sba("arena", [P, 6 * SLOT])
            scratch = sba("scratch", [P, 7680])
            hT = sba("hT", [P, KD, S])
            mixg = sba("mixg", [P, GH, S])
            mixr = sba("mixr", [P, 5, S])
            sel = sba("sel", [P, NT, S])
            sq = sba("sq", [P, 2, S])
            rs = sba("rs", [P, 2, S])
            ik2 = sq[:, 1, :]
            prow = rs[0:NPC, 1, 0:P]

            def slot(i):
                return view(arena, i * SLOT, KD, 512)

            up = 3 * SLOT
            gq, gk, b = (view(arena, up + 1024 * i, 2, S) for i in range(3))
            st = view(arena, up + 1024, 3, 2, 2 * GV)
            gv = view(arena, up + 3072, NT, GH * GV)
            gr = view(arena, up + 4608, GH, S, rows=GV)
            AT = view(arena, up + 6656, NT, GH, P)
            qexp, kdec = view(arena, up + 8704, 2, S), view(arena, up + 9728, 2, S)
            kdecT = view(arena, up + 10752, NT, 2, P)
            lrT = view(arena, up + 11776, S, rows=RANK)
            cin = view(arena, up + 8704, 2, S + CW - 1)
            csig = view(arena, up + 8704 + 2 * (S + CW - 1), 2, S)
            xn = view(scratch, 0, 2, D)
            relu = view(scratch, 0, 4, S)
            ld, lq, lk = (view(scratch, 1024 * i, 2, S) for i in range(3))
            lg, bm, pT = (view(scratch, 1024 * i, 2, S) for i in range(3))
            dq, dk = view(scratch, 3072, 3, S), view(scratch, 4608, 3, S)
            dv = view(scratch, 6144, NT, AH * AD)
            iq = mixg[:, :, :]
            wog = view(arena, 0, GH, D, rows=GV)
            wor = view(arena, GH * D, 5, D)
            wckv = view(arena, up, KD, 512)
            wcq = view(arena, up + 4096, KD, 256)
            wco = view(arena, up + 6144, 2, D)
            memT = view(arena, up + 8192, KD, M)
            ckT = view(arena, up + 10240, 2, M)
            cv = view(arena, up + 10752, 2, XH * XD)
            cqT = view(arena, up + 11264, 2, S)
            mem = view(scratch, 2048, 2, D)
            clg, cpT = view(scratch, 4096, 2, M), view(scratch, 4608, 2, 2, P)
            coT = view(scratch, 5120, 2, S)
            oneP, oneB = view(scratch, 6144, 2, P), view(scratch, 6400, 2, 2 * NBC)
            selw = sel[:, :, :].rearrange("p n s -> p (n s)")
            rout = view(selw, 0, NT, 224)
            wr = view(selw, 1024, KD, NG + E)
            def layer(name):
                return A[name][bass.ds(l, 1)]

            PARAMS = [("gmix", "norm_mix", KD, P, 0), ("gx", "norm_x", KD, P, 0), ("gmem", "norm_mem", KD, P, 0),
                      ("gffn", "norm_ffn", KD, P, 0), ("onorm", "gla_onorm", 1, GV, 0),
                      ("clg", "conv_ln_g", 2, P, 0), ("clb", "conv_ln_b", 2, P, 0), ("cb", "conv_b", 2, P, 0)]
            HEADP = [("dqn", "dsa_qnorm"), ("dkn", "dsa_knorm"), ("cqn", "x_qnorm"), ("ckn", "x_knorm")]
            NPAR = len(PARAMS) + 2 * len(HEADP) + GH

            JOBS = [(0, 0, P, "T", "ik", 0), (0, 2 * ID + IH, RANK, "T", "lr", 0)]
            JOBS += [(0, 2 * ID, IH, "tok", "iw", i) for i in range(NT)]
            JOBS += [(1, P * i, P, "T", "iq", i) for i in range(4)]
            JOBS += [(2, P * i, P, "T", "ca", i) for i in range(2)] + [(2, CC + P * i, P, "T", "cg", i) for i in range(2)]
            JOBS += [(3, P * i, P, "T", "dq", i) for i in range(3)] + [(4, P * i, P, "T", "dk", i) for i in range(3)]
            JOBS += [(5, 0, AH * AD, "tok", "dv", i) for i in range(NT)]
            JOBS += [(6, P * i, P, "T", "gq", i) for i in range(2)] + [(6, 2 * P + P * i, P, "T", "gk", i) for i in range(2)]
            JOBS += [(7, 0, GH * GV, "tok", "gv", i) for i in range(NT)]
            JOBS += [(8, GV * i, GV, "T", "gr", i) for i in range(GH)]
            NJ = len(JOBS)

            def done(name):
                return max(n for n, j in enumerate(JOBS) if j[4] == name) + 1

            DEST = dict(ik=lambda i: ik2[:, :], lr=lambda i: lrT, iw=lambda i: iw[:, i, :], iq=lambda i: iq[:, i, :],
                        ca=lambda i: cin[:, i, CW - 1:], cg=lambda i: csig[:, i, :], dq=lambda i: dq[:, i, :],
                        dk=lambda i: dk[:, i, :], dv=lambda i: dv[:, i, :], gq=lambda i: gq[:, i, :],
                        gk=lambda i: gk[:, i, :], gv=lambda i: gv[:, i, :], gr=lambda i: gr[:, i, :])
            AFTER_IDX = done("iq")
            STEPS = [(i, h) for i in range(NT) for h in range(AH)]
            DOTS = [(i, h) for i in range(NT) for h in range(IH)]

            def merge(dve, do, v, c):
                dve.wait_ge(sN["lev_mm"], NT * v + c + 1)
                if v == 0 and c == 0:
                    dve.wait_ge(sN["at_zero"], 1)
                m = masks[:, v, :].unsqueeze(1).unsqueeze(1).to_broadcast([P, 2, 2, P])
                c0 = c - c % 2
                do(nc.vector.copy_predicated(AT[:, c0:c0 + 2, c % 2:GH:2, :], m,
                                             ps[4 + c][:, :].rearrange("p (c h t) -> p c h t", c=2, t=P)), "lev_cp")

            with nc.Block() as block:
                @block.sync
                def _(sp):
                    sp.wait_ge(sN["prow_zero"], 1)
                    for name, src, n, w, _ in PARAMS:
                        sp.dma_start(prow[PC[name]:PC[name] + n, 0:w], layer(src).rearrange("o (c p) -> (o c) p", p=w))\
                          .then_inc(s_par, 16)
                    for name, src in HEADP:
                        for half in (0, 64):
                            sp.dma_start(prow[PC[name]:PC[name] + 1, half:half + 64], layer(src)).then_inc(s_par, 16)
                    for h in range(GH):
                        sp.dma_start(prow[PC["ba"] + h // 2:PC["ba"] + h // 2 + 1, 64 * (h % 2):64 * (h % 2) + GK],
                                     layer("gla_ba")[:, GK * h:GK * h + GK]).then_inc(s_par, 16)
                    w_in = A["w_in"][bass.ds(l, 1)].rearrange("o (c p) n -> p (o c) n", p=P)
                    for n, parts in enumerate(CHUNKS):
                        if n >= NSLOT:
                            sp.wait_ge(sN["proj_done"], max(m for m, j in enumerate(JOBS) if j[0] == n - NSLOT) + 1)
                        for dst, col, width in parts:
                            sp.dma_start(slot(n % NSLOT)[:, :, dst:dst + width], w_in[:, :, col:col + width])\
                              .then_inc(s_w[n % NSLOT], 16)
                        if n == 0:
                            for h in range(GH):
                                sp.dma_start(wa2[:, h // 2, 64 * (h % 2):64 * (h % 2) + GK],
                                             layer("gla_wa2")[:, :, GK * h:GK * h + GK].rearrange("o r c -> (o r) c"))\
                                  .then_inc(s_wa2, 16)
                            sp.dma_start(rs[0:CW, 0, 0:CC], layer("conv_w").rearrange("o j c -> (o j) c")).then_inc(s_cwr, 16)

                @block.tensor
                def _(pe):
                    pe.wait_ge(s_par, 16 * NPAR)
                    nc.tensor.transpose(ps[7][:, 0:NPC], prow, ident[0:NPC, 0:NPC]).then_inc(sN["par_t"], 1)
                    for t in range(NT):
                        pe.wait_ge(sN["xn_ready"], t + 1)
                        for q in range(2):
                            n = 2 * t + q
                            if n >= 2:
                                pe.wait_ge(sN["hT_ready"], n - 1)
                            for c in range(4):
                                last = nc.tensor.transpose(ps[4 + q][:, P * c:P * c + P],
                                                           xn[:, t % 2, P * (4 * q + c):P * (4 * q + c) + P], ident)
                            last.then_inc(sN["tr_done"], 1)
                    pe.wait_ge(sN["hT_ready"], 8)

                    pe.wait_ge(s_cwr, 16)
                    for i in range(2):
                        last = nc.tensor.transpose(ps[6][:, CW * i:CW * i + CW], rs[0:CW, 0, P * i:P * i + P], ident[0:CW, 0:CW])
                    last.then_inc(sN["cw_t"], 1)

                    def project(n):
                        chunk, col, width, kind, name, i = JOBS[n]
                        k = chunk % NSLOT
                        first = JOBS.index(next(j for j in JOBS if j[0] == chunk))
                        if n == first:
                            parts = sum(len(CHUNKS[c]) for c in range(k, chunk + 1, NSLOT))
                            pe.wait_ge(s_w[k], 16 * parts)
                        if n >= 4:
                            pe.wait_ge(sN["proj_out"], n - 3)
                        w = slot(k)
                        for c in range(KD):
                            if kind == "T":
                                last = nc.tensor.matmul(ps[n % 4][0:width, :], w[:, c, col:col + width], hT[:, c, :],
                                                        start=(c == 0), stop=(c == KD - 1))
                            else:
                                last = nc.tensor.matmul(ps[n % 4][:, 0:width], hT[:, c, P * i:P * i + P],
                                                        w[:, c, col:col + width], start=(c == 0), stop=(c == KD - 1))
                        last.then_inc(sN["proj_done"], 1)

                    for n in range(AFTER_IDX):
                        project(n)
                    pe.wait_ge(sN["proj_out"], AFTER_IDX)
                    pe.wait_ge(sN["cw_out"], 1)
                    for n, (i, h) in enumerate(DOTS):
                        if n >= 4:
                            pe.wait_ge(sN["relu_done"], n - 3)
                        r = pair_rows(h, ID)
                        nc.tensor.matmul(ps[4 + n % 4][:, 0:P * (i + 1)], iq[r, h // 2, P * i:P * i + P],
                                         ik2[r, 0:P * (i + 1)], start=True, stop=True).then_inc(sN["dots_done"], 1)
                    for n in range(AFTER_IDX, NJ):
                        project(n)

                    pe.wait_ge(sN["relu_done"], len(DOTS))
                    for n in range(6):
                        pe.wait_ge(sN["sq_ready"], n + 1)
                        if n >= 2:
                            pe.wait_ge(sN["sums_root"], n - 1)
                        nc.tensor.matmul(ps[4 + n % 2][:, :], same_head, sq[:, n % 2, :], start=True, stop=True)\
                          .then_inc(sN["sum_done"], 1)
                    pe.wait_ge(s_wa2, 16 * GH)
                    for i in range(2):
                        nc.tensor.matmul(ps[6 + i][:, :], wa2[:, i, :], lrT, start=True, stop=True).then_inc(sN["a_done"], 1)
                    pe.wait_ge(sN["b_ready"], 2)
                    pe.wait_ge(sN["sums_root"], 6)
                    for v in range(NLEV + 1):
                        if v < NLEV:
                            pe.wait_ge(sN["lev_q"], v + 1)
                            pe.wait_ge(sN["lev_k"], v + 1)
                        qq, kk = (lq, lk) if v < NLEV else (gq, gk)
                        for m in range(4):
                            if v >= 1:
                                pe.wait_ge(sN["lev_cp"], 4 * (v - 1) + m + 1)
                            for c in (m - m % 2, m - m % 2 + 1):
                                for h in (m % 2, m % 2 + 2):
                                    r = pair_rows(h, GK)
                                    at = 2 * P * (c % 2) + P * (h // 2)
                                    last = nc.tensor.matmul(ps[4 + m][:, at:at + P], kk[r, h // 2, P * c:P * c + P],
                                                            qq[r, h // 2, P * c:P * c + P], start=True, stop=True)
                            last.then_inc(sN["lev_mm"], 1)
                    pe.wait_ge(sN["kdec_done"], 1)
                    pe.wait_ge(sN["lev_cp"], NT * (NLEV + 1))
                    for i in range(2):
                        for c in range(NT):
                            last = nc.tensor.transpose(ps[4 + i][:, P * c:P * c + P], kdec[:, i, P * c:P * c + P], ident)
                        last.then_inc(sN["kt_done"], 1)
                    pe.wait_ge(sN["kt_out"], 2)
                    pe.wait_ge(sN["proj_out"], NJ)
                    for c in range(3):
                        for i in range(2):
                            last = nc.tensor.matmul(ps[5 + c][:, 192 * i:192 * i + 192], kdecT[:, c, i, :],
                                                    gv[:, c, 192 * i:192 * i + 192], start=True, stop=True)
                        last.then_inc(sN["upd_done"], 1)
                    pe.wait_ge(sN["qexp_done"], 1)
                    for c in range(NT):
                        if c >= 1:
                            pe.wait_ge(sN["state_done"], c)
                        for h in range(GH):
                            r = pair_rows(h, GK)
                            o = ps[h][0:GV, P * c:P * c + P]
                            last = nc.tensor.matmul(o, gv[:, c, GV * h:GV * h + GV], AT[:, c, h, :], start=True, stop=(c == 0))
                            if c:
                                last = nc.tensor.matmul(o, st[r, c - 1, h // 2, GV * (h % 2):GV * (h % 2) + GV],
                                                        qexp[r, h // 2, P * c:P * c + P], start=False, stop=True)
                    last.then_inc(sN["o_done"], 1)
                    for h in range(GH):
                        pe.wait_ge(sN["osq"], h + 1)
                        if h == 0:
                            pe.wait_ge(sN["state_done"], 3)
                        if h >= 2:
                            pe.wait_ge(sN["oroot"], h - 1)
                        nc.tensor.matmul(ps[4 + h % 2][0:GV, :], ones[0:GV, 0:GV], sq[0:GV, h % 2, :], start=True, stop=True)\
                          .then_inc(sN["osum"], 1)
                    pe.wait_ge(sN["conv_done"], 1)
                    for i in range(2):
                        last = nc.tensor.matmul(ps[6][:, :], ones[:, :], mixr[:, 3 + i, :], start=(i == 0), stop=(i == 1))
                    last.then_inc(sN["mean_done"], 1)
                    pe.wait_ge(sN["csq"], 2)
                    for i in range(2):
                        last = nc.tensor.matmul(ps[7][:, :], ones[:, :], sq[:, i, :], start=(i == 0), stop=(i == 1))
                    last.then_inc(sN["var_done"], 1)
                    pe.wait_ge(sN["normed"], 6)
                    pe.wait_ge(sN["oroot"], 4)
                    pe.wait_ge(sN["croot"], 1)
                    pe.wait_ge(sN["odone"], 4)

                    def logits(n):
                        i, h = STEPS[n]
                        r = pair_rows(h, AD)
                        if n >= 2:
                            pe.wait_ge(sN["lg_out"], n - 1)
                        nc.tensor.matmul(ps[4 + n % 2][:, 0:P * (i + 1)], dq[r, h // 2, P * i:P * i + P],
                                         dk[r, h // 2, 0:P * (i + 1)], start=True, stop=True).then_inc(sN["lg_done"], 1)

                    def turn(n):
                        i, h = STEPS[n]
                        pe.wait_ge(sN["p_norm"], n + 1)
                        if n >= 2:
                            pe.wait_ge(sN["pt_out"], n - 1)
                        for j in range(i + 1):
                            last = nc.tensor.transpose(ps[6 + n % 2][:, P * j:P * j + P], lg[:, n % 2, P * j:P * j + P], ident)
                        last.then_inc(sN["pt_done"], 1)

                    def values(n):
                        i, h = STEPS[n]
                        pe.wait_ge(sN["pt_out"], n + 1)
                        for j in range(i + 1):
                            last = nc.tensor.matmul(ps[h // 2][pair_rows(h, AD), P * i:P * i + P],
                                                    dv[:, j, AD * h:AD * h + AD], pT[:, n % 2, P * j:P * j + P],
                                                    start=(j == 0), stop=(j == i))
                        last.then_inc(sN["pv_done"], 1)

                    logits(0)
                    logits(1)
                    for n in range(len(STEPS)):
                        turn(n)
                        if n + 2 < len(STEPS):
                            logits(n + 2)
                        if n >= 1:
                            values(n - 1)
                    values(len(STEPS) - 1)

                @block.scalar
                def _(act):
                    do = engine(act, ca_)
                    for t in range(NT):
                        if t >= 2:
                            act.wait_ge(sN["tr_done"], 2 * (t - 1))
                        do(nc.scalar.activation(xn[:, t % 2, :], x[:, t, :], ACT.Square, accum_out=small[:, t:t + 1]))
                        do(nc.scalar.activation(small[:, 4 + t:5 + t], small[:, t:t + 1], ACT.Sqrt, bias=epst[:, :],
                                                scale=1.0 / D), "root_done")

                    FUNC = dict(gr=ACT.Silu, cg=ACT.Sigmoid)

                    def evacuate(n):
                        chunk, col, width, kind, name, i = JOBS[n]
                        act.wait_ge(sN["proj_done"], n + 1)
                        if name == "gq" and i == 0:
                            act.wait_ge(sN["at_zero"], 1)
                        src = ps[n % 4][0:width, :] if kind == "T" else ps[n % 4][:, 0:width]
                        scale = GK ** -0.5 if name == "gq" else IH ** -0.5 if name == "iw" else 1.0
                        nc.scalar.activation(DEST[name](i), src, FUNC.get(name, ACT.Copy), scale=scale)\
                          .then_inc(sN["proj_out"], 1)

                    for n in range(AFTER_IDX):
                        evacuate(n)
                    for n, (i, h) in enumerate(DOTS):
                        act.wait_ge(sN["dots_done"], n + 1)
                        if n >= 4:
                            act.wait_ge(sN["relu_used"], n - 3)
                        nc.scalar.activation(relu[:, n % 4, 0:P * (i + 1)], ps[4 + n % 4][:, 0:P * (i + 1)], ACT.Relu,
                                             scale=ID ** -0.5).then_inc(sN["relu_done"], 1)
                    for n in range(AFTER_IDX, NJ):
                        evacuate(n)
                    act.wait_ge(sN["proj_out"], NJ)
                    for n in range(6):
                        t = (dq if n < 3 else dk)[:, n % 3, :]
                        if n >= 2:
                            act.wait_ge(sN["sum_done"], n - 1)
                        do(nc.scalar.activation(sq[:, n % 2, :], t, ACT.Square), "sq_ready", wait=False)
                        act.wait_ge(sN["sum_done"], n + 1)
                        if n >= 2:
                            act.wait_ge(sN["normed"], n - 1)
                        do(nc.scalar.activation(rs[:, n % 2, :], ps[4 + n % 2][:, :], ACT.Sqrt, bias=epst[:, :], scale=1.0 / AD),
                           "sums_root", wait=False)
                    for i in range(2):
                        act.wait_ge(sN["a_done"], i + 1)
                        act.wait_ge(sN["sig_abs"], i + 1)
                        do(nc.scalar.activation(ld[:, i, :], b[:, i, :], ACT.Abs))
                        do(nc.scalar.activation(ld[:, i, :], ld[:, i, :], ACT.Exp, scale=-1.0))
                        do(nc.scalar.activation(ld[:, i, :], ld[:, i, :], ACT.Ln, bias=ones[:, 0:1]), "sig_ln")
                    for v in range(NLEV):
                        act.wait_ge(sN["lev_d"], v + 1)
                        do(nc.scalar.activation(ld, ld, ACT.Abs))
                        do(nc.scalar.activation(ld, ld, ACT.Exp, scale=-1.0), "lev_e")
                    act.wait_ge(sN["lev_q"], NLEV)
                    act.wait_ge(sN["lev_k"], NLEV)
                    do(nc.scalar.activation(ld, b, ACT.Exp), "eb_done")
                    act.wait_ge(sN["el_done"], 1)
                    do(nc.scalar.activation(lq, lq, ACT.Exp, scale=-1.0), "er_done")
                    for i in range(2):
                        act.wait_ge(sN["kt_done"], i + 1)
                        do(nc.scalar.activation(kdecT[:, :, i, :], ps[4 + i][:, :].rearrange("p (c d) -> p c d", d=P), ACT.Copy),
                           "kt_out", wait=False)
                    act.wait_ge(sN["o_done"], 1)
                    for h in range(GH):
                        if h >= 2:
                            act.wait_ge(sN["osum"], h - 1)
                        do(nc.scalar.activation(sq[0:GV, h % 2, :], ps[h][0:GV, :], ACT.Square), "osq", wait=False)
                        act.wait_ge(sN["osum"], h + 1)
                        if h >= 2:
                            act.wait_ge(sN["odone"], h - 1)
                        do(nc.scalar.activation(rs[0:GV, h % 2, :], ps[4 + h % 2][0:GV, :], ACT.Sqrt, bias=epst[0:GV, :],
                                                scale=1.0 / GV), "oroot", wait=False)
                    for i in range(2):
                        act.wait_ge(sN["cen_done"], i + 1)
                        do(nc.scalar.activation(sq[:, i, :], mixr[:, 3 + i, :], ACT.Square), "csq", wait=False)
                    act.wait_ge(sN["var_done"], 1)
                    act.wait_ge(sN["odone"], 4)
                    do(nc.scalar.activation(rs[:, 0, :], ps[7][:, :], ACT.Sqrt, bias=epst[:, :], scale=1.0 / CC), "croot")
                    act.wait_ge(sN["cnorm"], 2)
                    for i in range(2):
                        do(nc.scalar.activation(mixr[:, 3 + i, :], mixr[:, 3 + i, :], ACT.Silu, scale=pc("clg", i),
                                                bias=pc("clb", i)), wait=False)

                    def exps(n):
                        i, h = STEPS[n]
                        act.wait_ge(sN["lg_out"], n + 1)
                        s = lg[:, n % 2, 0:P * (i + 1)]
                        nc.scalar.activation(s, s, ACT.Exp, bias=small[:, 8 + n % 2:9 + n % 2],
                                             accum_out=small[:, 10 + n % 2:11 + n % 2]).then_inc(sN["exp_done"], 1)

                    def turned(n):
                        i, h = STEPS[n]
                        act.wait_ge(sN["pt_done"], n + 1)
                        if n >= 2:
                            act.wait_ge(sN["pv_done"], n - 1)
                        nc.scalar.activation(pT[:, n % 2, 0:P * (i + 1)], ps[6 + n % 2][:, 0:P * (i + 1)], ACT.Copy)\
                          .then_inc(sN["pt_out"], 1)

                    exps(0)
                    for n in range(len(STEPS)):
                        if n + 1 < len(STEPS):
                            exps(n + 1)
                        turned(n)

                @block.vector
                def _(dve):
                    do = engine(dve, cv_)
                    do(nc.vector.memset(prow, 0.0), "prow_zero")
                    dve.wait_ge(sN["par_t"], 1)
                    do(nc.vector.tensor_copy(par[:, 0:NPC], ps[7][:, 0:NPC]))
                    for t in range(NT):
                        dve.wait_ge(sN["root_done"], t + 1)
                        do(nc.vector.reciprocal(small[:, 12 + t:13 + t], small[:, 4 + t:5 + t]))
                        do(nc.vector.tensor_scalar(xn[:, t % 2, :], x[:, t, :], small[:, 12 + t:13 + t], None, ALU.mult), "xn_ready")
                        for q in range(2):
                            dve.wait_ge(sN["tr_done"], 2 * t + q + 1)
                            g = par[:, PC["gmix"] + 4 * q:PC["gmix"] + 4 * q + 4].unsqueeze(2).to_broadcast([P, 4, P])
                            do(nc.vector.tensor_tensor(hT[:, 4 * q:4 * q + 4, P * t:P * t + P],
                                                       ps[4 + q][:, :].rearrange("p (c t) -> p c t", t=P), g, ALU.mult), "hT_ready",
                               wait=False)
                    dve.wait_ge(sN["cw_t"], 1)
                    do(nc.vector.tensor_copy(convw[:, :, 0:CW], ps[6][:, 0:2 * CW].rearrange("p (i j) -> p i j", j=CW)), "cw_out")
                    dve.wait_ge(sN["proj_out"], done("iw"))
                    for n, (i, h) in enumerate(DOTS):
                        s = sel[:, i, 0:P * (i + 1)]
                        dve.wait_ge(sN["relu_done"], n + 1)
                        r, w = relu[:, n % 4, 0:P * (i + 1)], iw[:, i, h:h + 1]
                        if h == 0:
                            ins = nc.vector.tensor_scalar(s, r, w, None, ALU.mult)
                        else:
                            ins = nc.vector.scalar_tensor_tensor(s, r, w, s, ALU.mult, ALU.add)
                        do(ins, "relu_used")
                    for i in range(NT):
                        dve.wait_ge(sN["causal_done"], i + 1)
                        s = sel[:, i, 0:P * (i + 1)]
                        if i == 0:
                            do(nc.vector.tensor_scalar(s, s, 0.9 * NEG, FAR, ALU.is_lt, ALU.mult))
                            continue
                        for _ in range(TOPK // 8):
                            do(nc.vector.max(m8[:, :], s))
                            do(nc.vector.match_replace(s, m8[:, :], s, TAKEN))
                        do(nc.vector.tensor_scalar(s, s, 0.5 * (NEG + TAKEN), FAR, ALU.is_gt, ALU.mult))
                    do(nc.vector.memset(small[:, 60:61], 0.0), "sel_done")
                    do(nc.vector.memset(cin[:, :, 0:CW - 1], 0.0))
                    dve.wait_ge(sN["proj_out"], done("cg"))
                    for i in range(2):
                        do(nc.vector.tensor_tensor(cin[:, i, CW - 1:], cin[:, i, CW - 1:], csig[:, i, :], ALU.mult))
                        o = mixr[:, 3 + i, :]
                        do(nc.vector.tensor_scalar(o, cin[:, i, 0:S], convw[:, i, 0:1], pc("cb", i), ALU.mult, ALU.add))
                        for j in range(1, CW):
                            do(nc.vector.scalar_tensor_tensor(o, cin[:, i, j:j + S], convw[:, i, j:j + 1], o, ALU.mult, ALU.add))
                    do(nc.vector.memset(small[:, 60:61], 0.0), "conv_done")
                    for n in range(6):
                        t = (dq if n < 3 else dk)[:, n % 3, :]
                        dve.wait_ge(sN["sums_root"], n + 1)
                        do(nc.vector.reciprocal(rs[:, n % 2, :], rs[:, n % 2, :]))
                        do(nc.vector.scalar_tensor_tensor(t, t, pc("dqn" if n < 3 else "dkn"), rs[:, n % 2, :], ALU.mult, ALU.mult),
                           "normed")
                    for i in range(2):
                        dve.wait_ge(sN["a_done"], i + 1)
                        do(nc.vector.tensor_scalar(b[:, i, :], ps[6 + i][:, :], pc("ba", i), None, ALU.add), "sig_abs")
                    for i in range(2):
                        dve.wait_ge(sN["sig_ln"], i + 1)
                        do(nc.vector.scalar_tensor_tensor(b[:, i, :], b[:, i, :], 0.0, ld[:, i, :], ALU.min, ALU.subtract))
                        do(nc.vector.tensor_scalar(b[:, i, :], b[:, i, :], 1.0 / 16.0, None, ALU.mult))
                        do(nc.vector.tensor_tensor_scan(lq[:, i, :], steps, b[:, i, :], 0.0, ALU.mult, ALU.add))
                        do(nc.vector.tensor_copy(b[:, i, :], lq[:, i, :]), "b_ready")
                    for v, half in enumerate(HALVES):
                        if v >= 1:
                            dve.wait_ge(sN["lev_k"], v)
                        bv = b.rearrange("p i t -> p (i t)").rearrange("p (n w) -> p n w", w=2 * half)
                        dvw = ld.rearrange("p i t -> p (i t)").rearrange("p (n w) -> p n w", w=2 * half)
                        do(nc.vector.tensor_tensor(dvw, bv, bv[:, :, half - 1:half].to_broadcast([P, 2 * S // (2 * half), 2 * half]),
                                                   ALU.subtract), "lev_d")
                        if v >= 1:
                            for c in range(NT):
                                merge(dve, do, v - 1, c)
                        dve.wait_ge(sN["lev_e"], v + 1)
                        do(nc.vector.tensor_tensor(lq, gq, ld, ALU.mult), "lev_q")
                    for v in (NLEV - 1, NLEV):
                        for c in range(NT):
                            merge(dve, do, v, c)
                    bc = b.rearrange("p i t -> p (i t)").rearrange("p (n w) -> p n w", w=P)
                    do(nc.vector.tensor_tensor(lq.rearrange("p i t -> p (i t)").rearrange("p (n w) -> p n w", w=P), bc,
                                               bc[:, :, P - 1:P].to_broadcast([P, 2 * NT, P]), ALU.subtract), "el_done")
                    dve.wait_ge(sN["eb_done"], 1)
                    do(nc.vector.tensor_tensor(qexp, gq, ld, ALU.mult), "qexp_done")
                    do(nc.vector.tensor_copy(ebl[:, :, :], ld.rearrange("p i (c t) -> p i c t", t=P)[:, :, :, P - 1]))
                    dve.wait_ge(sN["er_done"], 1)
                    do(nc.vector.tensor_tensor(kdec, gk, lq, ALU.mult), "kdec_done")
                    for c in range(3):
                        dve.wait_ge(sN["upd_done"], c + 1)
                        for i in range(2):
                            u = ps[5 + c][:, 192 * i:192 * i + 192]
                            if c == 0:
                                ins = nc.vector.tensor_copy(st[:, 0, i, :], u)
                            else:
                                ins = nc.vector.scalar_tensor_tensor(st[:, c, i, :], st[:, c - 1, i, :], ebl[:, i, c:c + 1], u,
                                                                     ALU.mult, ALU.add)
                            do(ins, "state_done" if i else None)
                    for h in range(GH):
                        dve.wait_ge(sN["oroot"], h + 1)
                        r = rs[0:GV, h % 2, :]
                        do(nc.vector.reciprocal(r, r))
                        do(nc.vector.scalar_tensor_tensor(r, ps[h][0:GV, :], pc("onorm", 0, GV), r, ALU.mult, ALU.mult))
                        do(nc.vector.tensor_tensor(mixg[0:GV, h, :], r, gr[:, h, :], ALU.mult), "odone")
                    dve.wait_ge(sN["mean_done"], 1)
                    for i in range(2):
                        do(nc.vector.scalar_tensor_tensor(mixr[:, 3 + i, :], ps[6][:, :], -1.0 / CC, mixr[:, 3 + i, :], ALU.mult,
                                                          ALU.add), "cen_done")
                    dve.wait_ge(sN["croot"], 1)
                    do(nc.vector.reciprocal(rs[:, 1, :], rs[:, 0, :]))
                    for i in range(2):
                        do(nc.vector.tensor_tensor(mixr[:, 3 + i, :], mixr[:, 3 + i, :], rs[:, 1, :], ALU.mult), "cnorm")

                    def masked(n):
                        i, h = STEPS[n]
                        w = P * (i + 1)
                        dve.wait_ge(sN["lg_done"], n + 1)
                        dve.wait_ge(sN["bm_done"], n + 1)
                        if n >= 2:
                            dve.wait_ge(sN["pt_done"], n - 1)
                        s = lg[:, n % 2, 0:w]
                        do(nc.vector.scalar_tensor_tensor(s, ps[4 + n % 2][:, 0:w], AD ** -0.5, bm[:, n % 2, 0:w], ALU.mult, ALU.add))
                        do(nc.vector.reduce_max(small[:, 16 + n % 2:17 + n % 2], s, AX))
                        do(nc.vector.tensor_scalar(small[:, 8 + n % 2:9 + n % 2], small[:, 16 + n % 2:17 + n % 2], -1.0, None,
                                                   ALU.mult), "lg_out")

                    def normalise(n):
                        i, h = STEPS[n]
                        s = lg[:, n % 2, 0:P * (i + 1)]
                        dve.wait_ge(sN["exp_done"], n + 1)
                        do(nc.vector.reciprocal(small[:, 18:19], small[:, 10 + n % 2:11 + n % 2]))
                        do(nc.vector.tensor_scalar(s, s, small[:, 18:19], None, ALU.mult), "p_norm")

                    masked(0)
                    for n in range(len(STEPS)):
                        if n + 1 < len(STEPS):
                            masked(n + 1)
                        normalise(n)
                    dve.wait_ge(sN["pv_done"], len(STEPS))
                    for i in range(3):
                        do(nc.vector.tensor_copy(mixr[:, i, :], ps[i][:, :]))

                @block.gpsimd
                def _(gp):
                    do = engine(gp, cp_)
                    do(nc.gpsimd.memset(AT, 0.0), "at_zero")
                    for i in range(NT):
                        gp.wait_ge(sN["relu_used"], IH * (i + 1))
                        s = sel[:, i, P * i:P * i + P]
                        do(nc.gpsimd.affine_select(out=s, in_=s, pattern=[[-1, P]], compare_op=ALU.is_ge, fill=NEG, base=0,
                                                   channel_multiplier=1), "causal_done")
                    for v in range(NLEV):
                        gp.wait_ge(sN["lev_e"], v + 1)
                        if v >= 1:
                            gp.wait_ge(sN["lev_mm"], NT * v)
                        else:
                            gp.wait_ge(sN["proj_out"], NJ)
                        do(nc.gpsimd.tensor_tensor(lk, gk, ld, ALU.mult), "lev_k")
                    gp.wait_ge(sN["sel_done"], 1)
                    gp.wait_ge(sN["kdec_done"], 1)
                    gp.wait_ge(sN["lev_mm"], NT * NLEV)
                    for n, (i, h) in enumerate(STEPS):
                        if n >= 2:
                            gp.wait_ge(sN["lg_out"], n - 1)
                        near = 2 if i else 1
                        w0 = P * (i + 1 - near)
                        if w0:
                            do(nc.gpsimd.tensor_scalar(bm[:, n % 2, 0:w0], sel[:, i, 0:w0], bfar[:, h:h + 1], None, ALU.add))
                        do(nc.gpsimd.tensor_tensor(bm[:, n % 2, w0:P * (i + 1)], sel[:, i, w0:P * (i + 1)],
                                                   toep[:, h, 2 * P - P * near:2 * P], ALU.add), "bm_done")

            XSTEPS = [(t, h) for t in range(NT) for h in range(XH)]
            HALF = [(t, q) for t in range(NT) for q in range(2)]

            def rows_squared(act, do, rows, nt, root, freed):
                for t in range(nt):
                    freed(act, t)
                    do(nc.scalar.activation(xn[:, t % 2, :], rows[:, t, :], ACT.Square, accum_out=small[:, t:t + 1]))
                    do(nc.scalar.activation(small[:, 4 + t:5 + t], small[:, t:t + 1], ACT.Sqrt, bias=epst[:, :], scale=1.0 / D), root)

            def rows_turned(pe, nt, ready, bank, tr, out):
                for t in range(nt):
                    pe.wait_ge(sN[ready], t + 1)
                    for q in range(2):
                        n = 2 * t + q
                        if n >= 2:
                            pe.wait_ge(sN[out], n - 1)
                        for c in range(4):
                            last = nc.tensor.transpose(ps[bank + q][:, P * c:P * c + P],
                                                       xn[:, t % 2, P * (4 * q + c):P * (4 * q + c) + P], ident)
                        last.then_inc(sN[tr], 1)

            def rows_normed(dve, do, rows, nt, root, ready, tr, bank, gain, dest, out, freed=None):
                for t in range(nt):
                    dve.wait_ge(sN[root], t + 1)
                    do(nc.vector.reciprocal(small[:, 12 + t:13 + t], small[:, 4 + t:5 + t]))
                    do(nc.vector.tensor_scalar(xn[:, t % 2, :], rows[:, t, :], small[:, 12 + t:13 + t], None, ALU.mult), ready)
                    for q in range(2):
                        dve.wait_ge(sN[tr], 2 * t + q + 1)
                        g = par[:, PC[gain] + 4 * q:PC[gain] + 4 * q + 4].unsqueeze(2).to_broadcast([P, 4, P])
                        do(nc.vector.tensor_tensor(dest[:, 4 * q:4 * q + 4, P * t:P * t + P],
                                                   ps[bank + q][:, :].rearrange("p (c t) -> p c t", t=P), g, ALU.mult), out)

            with nc.Block() as block:
                @block.sync
                def _(sp):
                    w = A["w_out"][bass.ds(l, 1)]
                    sp.dma_start(mem, A["mem"][0].rearrange("(n p) d -> p n d", p=P)).then_inc(sN["mem_in"], 16)
                    sp.dma_start(wog, w[:, 0:GH * GV, :].rearrange("o (h v) n -> v (o h) n", v=GV)).then_inc(sN["wo_in"], 16)
                    sp.dma_start(wor, w[:, GH * GV:D, :].rearrange("o (c p) n -> p (o c) n", p=P)).then_inc(sN["wo_in"], 16)
                    sp.dma_start(wckv, layer("w_ckv").rearrange("o (c p) n -> p (o c) n", p=P)).then_inc(sN["wckv_in"], 16)
                    sp.dma_start(wcq, layer("w_cq").rearrange("o (c p) n -> p (o c) n", p=P)).then_inc(sN["wcq_in"], 16)
                    sp.dma_start(wco, layer("w_co").rearrange("o (c p) n -> p (o c) n", p=P)).then_inc(sN["wco_in"], 16)
                    sp.dma_start(wr[:, :, 0:NG], layer("w_rg").rearrange("o (c p) n -> p (o c) n", p=P)).then_inc(sN["wr_in"], 16)
                    sp.dma_start(wr[:, :, NG:NG + E], layer("w_re").rearrange("o (c p) n -> p (o c) n", p=P)).then_inc(sN["wr_in"], 16)
                    sp.dma_start(blk[:, 0:NG], layer("b_rg")).then_inc(sN["rb_in"], 16)
                    sp.dma_start(blk[:, NG:NG + E], layer("b_re")).then_inc(sN["rb_in"], 16)
                    for t in range(NT):
                        sp.wait_ge(sN["f_xn"], t + 1)
                        sp.dma_start(hrows[P * t:P * t + P, :], xn[:, t % 2, :]).then_inc(s_hr[t], 16)
                    for t in range(NT):
                        sp.wait_ge(s_hr[t], 16)

                @block.tensor
                def _(pe):
                    rows_turned(pe, 2, "mm_xn", 2, "mm_tr", "mm_T")
                    pe.wait_ge(sN["wo_in"], 32)
                    for n, (t, q) in enumerate(HALF):
                        if n >= 2:
                            pe.wait_ge(sN["x_mid"], n - 1)
                        for c in range(GH + 5):
                            if c < GH:
                                a, w = mixg[0:GV, c, P * t:P * t + P], wog[:, c, 512 * q:512 * q + 512]
                            else:
                                a, w = mixr[:, c - GH, P * t:P * t + P], wor[:, c - GH, 512 * q:512 * q + 512]
                            last = nc.tensor.matmul(ps[n % 2][:, :], a, w, start=(c == 0), stop=(c == GH + 4))
                        last.then_inc(sN["op_done"], 1)
                    pe.wait_ge(sN["mm_T"], 4)
                    pe.wait_ge(sN["wckv_in"], 16)
                    for i in range(2):
                        for c in range(KD):
                            last = nc.tensor.matmul(ps[4][:, M * i:M * i + M], wckv[:, c, P * i:P * i + P], memT[:, c, :],
                                                    start=(c == 0), stop=(c == KD - 1))
                    last.then_inc(sN["cp_done"], 1)
                    for i in range(2):
                        for c in range(KD):
                            last = nc.tensor.matmul(ps[5][:, 256 * i:256 * i + 256], memT[:, c, P * i:P * i + P],
                                                    wckv[:, c, 256:512], start=(c == 0), stop=(c == KD - 1))
                    last.then_inc(sN["cp_done"], 1)
                    rows_turned(pe, NT, "xm_xn", 6, "xm_tr", "xm_hT")
                    pe.wait_ge(sN["xm_hT"], 8)
                    pe.wait_ge(sN["wcq_in"], 16)
                    for i in range(2):
                        for c in range(KD):
                            last = nc.tensor.matmul(ps[2 + i][:, :], wcq[:, c, P * i:P * i + P], hT[:, c, :],
                                                    start=(c == 0), stop=(c == KD - 1))
                        last.then_inc(sN["cp_done"], 1)
                    pe.wait_ge(sN["x_mid"], 8)
                    for n in range(3):
                        pe.wait_ge(sN["cn_sq"], n + 1)
                        if n >= 2:
                            pe.wait_ge(sN["cn_root"], n - 1)
                        nc.tensor.matmul(ps[n % 2][:, :], same_head, sq[:, n % 2, :], start=True, stop=True)\
                          .then_inc(sN["cn_sum"], 1)
                    pe.wait_ge(sN["cn_done"], 3)

                    def logits(n):
                        t, h = XSTEPS[n]
                        r = pair_rows(h, XD)
                        if n >= 2:
                            pe.wait_ge(sN["c_exp"], n - 1)
                        nc.tensor.matmul(ps[4 + n % 2][:, 0:M], cqT[r, h // 2, P * t:P * t + P], ckT[r, h // 2, :],
                                         start=True, stop=True).then_inc(sN["cl_done"], 1)

                    def values(n):
                        t, h = XSTEPS[n]
                        pe.wait_ge(sN["c_pto"], n + 1)
                        for j in range(2):
                            last = nc.tensor.matmul(ps[h // 2][pair_rows(h, XD), P * t:P * t + P],
                                                    cv[:, j, XD * h:XD * h + XD], cpT[:, n % 2, j, :], start=(j == 0), stop=(j == 1))
                        last.then_inc(sN["c_pv"], 1)

                    pe.wait_ge(sN["cp_out"], 1)
                    logits(0)
                    logits(1)
                    for n in range(len(XSTEPS)):
                        pe.wait_ge(sN["c_norm"], n + 1)
                        if n >= 2:
                            pe.wait_ge(sN["c_pto"], n - 1)
                        for j in range(2):
                            last = nc.tensor.transpose(ps[6 + n % 2][:, P * j:P * j + P], clg[:, n % 2, P * j:P * j + P], ident)
                        last.then_inc(sN["c_pt"], 1)
                        if n + 2 < len(XSTEPS):
                            logits(n + 2)
                        if n >= 1:
                            values(n - 1)
                    values(len(XSTEPS) - 1)
                    pe.wait_ge(sN["c_o"], 2)
                    pe.wait_ge(sN["wco_in"], 16)
                    for n, (t, q) in enumerate(HALF):
                        if n >= 2:
                            pe.wait_ge(sN["x_cross"], n - 1)
                        for c in range(2):
                            last = nc.tensor.matmul(ps[2 + n % 2][:, :], coT[:, c, P * t:P * t + P], wco[:, c, 512 * q:512 * q + 512],
                                                    start=(c == 0), stop=(c == 1))
                        last.then_inc(sN["co_done"], 1)
                    rows_turned(pe, NT, "f_xn", 6, "f_tr", "f_hT")
                    pe.wait_ge(sN["f_hT"], 8)
                    pe.wait_ge(sN["wr_in"], 32)
                    pe.wait_ge(sN["rb_in"], 32)
                    for t in range(NT):
                        o = ps[4][:, 32 * t:32 * t + NG + E]
                        for c in range(KD):
                            nc.tensor.matmul(o, hT[:, c, P * t:P * t + P], wr[:, c, :], start=(c == 0), stop=False)
                        last = nc.tensor.matmul(o, ones[0:1, :], blk[:, 0:NG + E], start=False, stop=True)
                    last.then_inc(sN["r_done"], 1)
                    pe.wait_ge(sN["r_hot"], 1)
                    for t in range(NT):
                        for j in range(t):
                            nc.tensor.matmul(ps[5][:, E * t:E * t + E], ones[:, :], rout[:, j, 80:96], start=(j == 0), stop=False)
                        nc.tensor.matmul(ps[5][:, E * t:E * t + E], before, rout[:, t, 80:96], start=(t == 0), stop=True)
                    for t in range(NT):
                        last = nc.tensor.matmul(ps[5][:, 64:64 + E], ones[:, :], rout[:, t, 80:96], start=(t == 0), stop=(t == NT - 1))
                    last.then_inc(sN["r_rank"], 1)
                    for n in range(2 * NT):
                        pe.wait_ge(sN["r_one"], n + 1)
                        last = nc.tensor.matmul(ps[4][:, 256:256 + 2 * NBC], oneP[:, n % 2, :], oneB[:, n % 2, :],
                                                start=(n == 0), stop=(n == 2 * NT - 1))
                        last.then_inc(sN["r_slots"], 1)

                @block.scalar
                def _(act):
                    do = engine(act, ca_)
                    act.wait_ge(sN["mem_in"], 16)
                    rows_squared(act, do, mem, 2, "mm_root", lambda e, t: None)

                    def freed_x(e, t):
                        e.wait_ge(sN["x_mid"], 2 * t + 2)
                        e.wait_ge(sN["mm_tr"], 4)
                        if t >= 2:
                            e.wait_ge(sN["xm_tr"], 2 * (t - 1))

                    rows_squared(act, do, x, NT, "xm_root", freed_x)
                    act.wait_ge(sN["cp_done"], 2)
                    do(nc.scalar.activation(cv, ps[5][:, :].rearrange("p (i n) -> p i n", i=2), ACT.Copy), "cp_out", wait=False)
                    for n in range(3):
                        src = ps[4] if n == 0 else ps[1 + n]
                        act.wait_ge(sN["cp_done"], 1 if n == 0 else n + 2)
                        if n >= 2:
                            act.wait_ge(sN["cn_sum"], n - 1)
                        do(nc.scalar.activation(sq[:, n % 2, :], src[:, :], ACT.Square), "cn_sq", wait=False)
                        act.wait_ge(sN["cn_sum"], n + 1)
                        if n >= 2:
                            act.wait_ge(sN["cn_done"], n - 1)
                        do(nc.scalar.activation(rs[:, n % 2, :], ps[n % 2][:, :], ACT.Sqrt, bias=epst[:, :], scale=1.0 / XD),
                           "cn_root", wait=False)

                    def exps(n):
                        act.wait_ge(sN["c_nm"], n + 1)
                        if n >= 2:
                            act.wait_ge(sN["c_pt"], n - 1)
                        nc.scalar.activation(clg[:, n % 2, :], ps[4 + n % 2][:, 0:M], ACT.Exp, bias=small[:, 20 + n % 2:21 + n % 2],
                                             scale=XD ** -0.5, accum_out=small[:, 22 + n % 2:23 + n % 2]).then_inc(sN["c_exp"], 1)

                    exps(0)
                    for n in range(len(XSTEPS)):
                        if n + 1 < len(XSTEPS):
                            exps(n + 1)
                        act.wait_ge(sN["c_pt"], n + 1)
                        if n >= 2:
                            act.wait_ge(sN["c_pv"], n - 1)
                        nc.scalar.activation(cpT[:, n % 2, :, :], ps[6 + n % 2][:, 0:2 * P].rearrange("p (j t) -> p j t", t=P),
                                             ACT.Copy).then_inc(sN["c_pto"], 1)
                    act.wait_ge(sN["c_pv"], len(XSTEPS))
                    for i in range(2):
                        do(nc.scalar.activation(coT[:, i, :], ps[i][:, :], ACT.Copy), "c_o", wait=False)

                    def freed_f(e, t):
                        e.wait_ge(sN["x_cross"], 2 * t + 2)
                        if t >= 2:
                            e.wait_ge(sN["f_tr"], 2 * (t - 1))
                            e.wait_ge(s_hr[t - 2], 16)

                    rows_squared(act, do, x, NT, "f_root", freed_f)
                    act.wait_ge(sN["r_lin"], 1)
                    do(nc.scalar.activation(rout[:, :, 24:28], rout[:, :, 24:28], ACT.Exp), "r_exp")
                    act.wait_ge(sN["r_lin"], 2)
                    do(nc.scalar.activation(rout[:, :, 44:45], rout[:, :, 44:45], ACT.Exp), "r_exp")

                @block.vector
                def _(dve):
                    do = engine(dve, cv_)
                    V = nc.vector
                    rows_normed(dve, do, mem, 2, "mm_root", "mm_xn", "mm_tr", 2, "gmem", memT, "mm_T")
                    for n, (t, q) in enumerate(HALF):
                        dve.wait_ge(sN["op_done"], n + 1)
                        xt = x[:, t, 512 * q:512 * q + 512]
                        do(V.tensor_tensor(xt, xt, ps[n % 2][:, :], ALU.add), "x_mid")
                    rows_normed(dve, do, x, NT, "xm_root", "xm_xn", "xm_tr", 6, "gx", hT, "xm_hT")
                    for n in range(3):
                        src, dst = (ps[4], ckT.rearrange("p i m -> p (i m)")) if n == 0 else (ps[1 + n], cqT[:, n - 1, :])
                        dve.wait_ge(sN["cn_root"], n + 1)
                        do(V.reciprocal(rs[:, n % 2, :], rs[:, n % 2, :]))
                        do(V.scalar_tensor_tensor(dst, src[:, :], pc("cqn" if n else "ckn"), rs[:, n % 2, :], ALU.mult, ALU.mult),
                           "cn_done")

                    def row_max(n):
                        dve.wait_ge(sN["cl_done"], n + 1)
                        do(V.reduce_max(small[:, 24:25], ps[4 + n % 2][:, 0:M], AX))
                        do(V.tensor_scalar(small[:, 20 + n % 2:21 + n % 2], small[:, 24:25], -XD ** -0.5, None, ALU.mult), "c_nm")

                    row_max(0)
                    for n in range(len(XSTEPS)):
                        if n + 1 < len(XSTEPS):
                            row_max(n + 1)
                        dve.wait_ge(sN["c_exp"], n + 1)
                        do(V.reciprocal(small[:, 25:26], small[:, 22 + n % 2:23 + n % 2]))
                        do(V.tensor_scalar(clg[:, n % 2, :], clg[:, n % 2, :], small[:, 25:26], None, ALU.mult), "c_norm")
                    for n, (t, q) in enumerate(HALF):
                        dve.wait_ge(sN["co_done"], n + 1)
                        xt = x[:, t, 512 * q:512 * q + 512]
                        do(V.tensor_tensor(xt, xt, ps[2 + n % 2][:, :], ALU.add), "x_cross")
                    rows_normed(dve, do, x, NT, "f_root", "f_xn", "f_tr", 6, "gffn", hT, "f_hT")

                    def R(a, b):
                        return rout[:, :, a:b]

                    def spread(ap, n):
                        return ap.to_broadcast([P, NT, n])

                    def first_largest(v, hot, m):
                        do(V.reduce_max(m, v, AX))
                        do(V.tensor_tensor(R(48, 52), v, spread(m, 4), ALU.is_equal))
                        do(V.tensor_tensor(R(48, 52), R(48, 52), rout[:, :, 220:224], ALU.mult))
                        do(V.reduce_max(R(52, 53), R(48, 52), AX))
                        do(V.tensor_tensor(hot, R(48, 52), spread(R(52, 53), 4), ALU.is_equal))

                    for t in range(NT):
                        do(V.tensor_scalar(rout[:, t, 220:224], iota[:, 0:4], -1.0, 8.0, ALU.mult, ALU.add))
                    dve.wait_ge(sN["r_done"], 1)
                    do(V.tensor_copy(R(0, NG + E), ps[4][:, 0:P].rearrange("p (t n) -> p t n", n=32)[:, :, 0:NG + E]))
                    first_largest(R(0, 4), R(20, 24), R(40, 41))
                    do(V.tensor_tensor(R(24, 28), R(0, 4), spread(R(40, 41), 4), ALU.subtract), "r_lin")
                    el4 = R(4, 20).rearrange("p t (g e) -> p t g e", e=EG)
                    w16 = R(112, 128).rearrange("p t (g e) -> p t g e", e=EG)
                    do(V.tensor_tensor(w16, el4, R(20, 24).unsqueeze(3).to_broadcast([P, NT, NG, EG]), ALU.mult))
                    do(V.tensor_reduce(R(28, 32), w16.rearrange("p t g e -> p t e g"), AX, ALU.add))
                    first_largest(R(28, 32), R(32, 36), R(42, 43))
                    do(V.scalar_tensor_tensor(R(54, 58), R(32, 36), NEG, R(28, 32), ALU.mult, ALU.add))
                    first_largest(R(54, 58), R(36, 40), R(43, 44))
                    do(V.tensor_tensor(R(44, 45), R(43, 44), R(42, 43), ALU.subtract), "r_lin")
                    dve.wait_ge(sN["r_exp"], 1)
                    do(V.reduce_sum(R(41, 42), R(24, 28), AX))
                    dve.wait_ge(sN["r_exp"], 2)
                    do(V.tensor_scalar(R(58, 59), R(44, 45), 1.0, None, ALU.add))
                    do(V.tensor_tensor(R(58, 59), R(58, 59), R(41, 42), ALU.mult))
                    do(V.reciprocal(R(136, 137), R(58, 59)))
                    do(V.tensor_tensor(R(137, 138), R(136, 137), R(44, 45), ALU.mult))
                    for k in range(2):
                        hot = R(140 + 16 * k, 156 + 16 * k).rearrange("p t (g e) -> p t g e", e=EG)
                        do(V.tensor_tensor(hot, R(20, 24).unsqueeze(3).to_broadcast([P, NT, NG, EG]),
                                           R(32 + 4 * k, 36 + 4 * k).unsqueeze(2).to_broadcast([P, NT, NG, EG]), ALU.mult))
                    do(V.tensor_tensor(R(80, 96), R(140, 156), R(156, 172), ALU.add), "r_hot")
                    dve.wait_ge(sN["r_rank"], 1)
                    cnt, nbk, cum, exc = (rout[:, 0, 172:188], rout[:, 1, 172:188], rout[:, 2, 172:188], rout[:, 3, 172:188])
                    do(V.tensor_copy(cnt, ps[5][:, 64:64 + E]))
                    do(V.tensor_copy(R(96, 112), ps[5][:, 0:64].rearrange("p (t e) -> p t e", e=E)))
                    do(V.tensor_scalar(nbk, cnt, 0.0, None, ALU.is_gt))
                    for k in range(1, S // P):
                        do(V.scalar_tensor_tensor(nbk, cnt, float(P * k), nbk, ALU.is_gt, ALU.add))
                    do(V.tensor_tensor_scan(cum, ones[:, 0:E], nbk, 0.0, ALU.mult, ALU.add))
                    do(V.tensor_tensor(exc, cum, nbk, ALU.subtract))
                    for k in range(2):
                        hot = R(140 + 16 * k, 156 + 16 * k)
                        do(V.tensor_tensor(R(112, 128), hot, R(96, 112), ALU.mult))
                        do(V.reduce_sum(R(128 + k, 129 + k), R(112, 128), AX))
                        do(V.tensor_tensor(R(112, 128), hot, exc.unsqueeze(1).to_broadcast([P, NT, E]), ALU.mult))
                        do(V.reduce_sum(R(130 + k, 131 + k), R(112, 128), AX))
                    do(V.tensor_scalar(R(132, 134), R(128, 130), float(P), None, ALU.is_ge))
                    for k in range(2, S // P):
                        do(V.scalar_tensor_tensor(R(132, 134), R(128, 130), float(P * k), R(132, 134), ALU.is_ge, ALU.add))
                    do(V.scalar_tensor_tensor(R(134, 136), R(132, 134), -float(P), R(128, 130), ALU.mult, ALU.add))
                    do(V.tensor_tensor(R(130, 132), R(130, 132), R(132, 134), ALU.add))
                    do(V.scalar_tensor_tensor(R(138, 140), R(130, 132), float(P), R(134, 136), ALU.mult, ALU.add))
                    do(V.tensor_copy(pair_slot[:, :, :], R(138, 140)))
                    for n in range(2 * NT):
                        t, k = n // 2, n % 2
                        if n >= 2:
                            dve.wait_ge(sN["r_slots"], n - 1)
                        do(V.tensor_scalar(oneP[:, n % 2, :], iota, rout[:, t, 134 + k:135 + k], None, ALU.is_equal))
                        do(V.tensor_scalar(oneB[:, n % 2, 0:NBC], iota[:, 0:NBC], rout[:, t, 130 + k:131 + k], tok[:, t:t + 1],
                                           ALU.is_equal, ALU.mult))
                        do(V.tensor_scalar(oneB[:, n % 2, NBC:2 * NBC], iota[:, 0:NBC], rout[:, t, 130 + k:131 + k],
                                           rout[:, t, 136 + k:137 + k], ALU.is_equal, ALU.mult), "r_one")
                    w = sq[0:1, 0, 0:NBC * E].rearrange("p (b e) -> p b e", e=E)
                    do(V.tensor_tensor(w, iota[0:1, 0:NBC].unsqueeze(2).to_broadcast([1, NBC, E]),
                                       cum[0:1, :].unsqueeze(1).to_broadcast([1, NBC, E]), ALU.is_ge))
                    do(V.reduce_sum(blk[:, 32:32 + NBC], w, AX))
                    do(V.tensor_scalar(blk[:, 32:32 + NBC], blk[:, 32:32 + NBC], float(E - 1), None, ALU.min))
                    tot = rout[0:1, 2, 187:188]
                    do(V.tensor_copy(blki[:, 0:NBC], blk[:, 32:32 + NBC]))
                    do(V.tensor_copy(blki[:, NBC:NBC + 1], tot))
                    dve.wait_ge(sN["r_slots"], 2 * NT)
                    do(V.tensor_copy(slots[:, :], ps[4][:, 256:256 + 2 * NBC]))
                    do(V.tensor_copy(slot_tok[:, :], slots[:, 0:NBC]))

            mem_a.close()

            KINDS = (("w_gate", KD, F), ("w_up", KD, F), ("w_down", F // P, D))
            mem_e = ExitStack()

            def sbe(name, shape, dt=F32):
                return mem_e.enter_context(nc.sbuf_tensor(name, shape, dt))

            raw = [sbe(f"raw_{n}", [P, c, w]) for n, c, w in KINDS]
            wh = [sbe(f"head_{n}", [P, c, w], F32R) for n, c, w in KINDS]
            wl = [sbe(f"rest_{n}", [P, c, w], F32R) for n, c, w in KINDS]
            xg = sbe("xg", [P, D])
            xh, xl = sbe("xg_head", [P, KD, P], F32R), sbe("xg_rest", [P, KD, P], F32R)
            he = sbe("he", [P, F])
            hh, hl = sbe("he_head", [P, F // P, P], F32R), sbe("he_rest", [P, F // P, P], F32R)
            yb = sbe("yb", [P, D])

            def block_count(eng):
                return eng.value_load(blki[0:1, NBC:NBC + 1], min_val=PAIRS // S, max_val=MAXB)

            with nc.Block() as block:
                @block.sync
                def _(sp):
                    def load(g, wait):
                        e = sp.value_load(blki[0:1, bass.ds(g, 1)] if wait else blki[0:1, 0:1], min_val=0, max_val=E - 1)
                        for q, (name, _, _) in enumerate(KINDS):
                            if wait:
                                sp.wait_ge(s_split[q], g)
                            src = A[name][bass.ds(l, 1), bass.ds(e, 1)].rearrange("o e (c p) n -> p (o e c) n", p=P)
                            sp.dma_start(raw[q][:, :, :], src).then_inc(s_raw[q], 16)

                    load(0, False)
                    with sp.Fori(1, block_count(sp)) as g:
                        load(g, True)

                @block.gpsimd
                def _(gp):
                    def gather():
                        gp.indirect_dma_start(out=xg[:, :], out_offset=None, in_=hrows,
                                              in_offset=bass.IndirectOffsetOnAxis(ap=idx[:, :], axis=0)).then_inc(s_ga, 16)

                    nc.gpsimd.tensor_copy(idx[:, :], slot_tok[:, 0:1]).then_inc(sN["idx"], 1)
                    gp.wait_ge(sN["idx"], 1)
                    gather()
                    with gp.Fori(1, block_count(gp)) as g:
                        gp.wait_ge(sN["x_free"], g)
                        gp.nop(nofuse=True)
                        nc.gpsimd.tensor_copy(idx[:, :], slot_tok[:, bass.ds(g, 1)]).then_inc(sN["idx"], 1)
                        gp.wait_ge(sN["idx"], g + 1)
                        gp.nop(nofuse=True)
                        gather()

                @block.tensor
                def _(pe):
                    def turn(q, mark):
                        for c in range(4):
                            last = nc.tensor.transpose(ps[4 + q][:, P * c:P * c + P], xg[:, P * (4 * q + c):P * (4 * q + c) + P], ident)
                        last.then_inc(sN[mark], 1)

                    def three_passes(out, a, b, n):
                        for c in range(n):
                            (ah, al), (bh, bl) = a(c), b(c)
                            nc.tensor.matmul(out, ah, bh, start=(c == 0), stop=False)
                            nc.tensor.matmul(out, ah, bl, start=False, stop=False)
                            last = nc.tensor.matmul(out, al, bh, start=False, stop=(c == n - 1))
                        return last

                    def gate_up(n):
                        pe.wait_ge(sN["blk_xl"], 2 * n)
                        for q in range(2):
                            pe.wait_ge(s_split[q], n)
                            three_passes(ps[q][:, :], lambda c: (xh[:, c, :], xl[:, c, :]),
                                         lambda c: (wh[q][:, c, :], wl[q][:, c, :]), KD).then_inc(s_used[q], 1)

                    def turn_h(n):
                        pe.wait_ge(sN["blk_h"], n)
                        for c in range(F // P):
                            last = nc.tensor.transpose(ps[6][:, P * c:P * c + P], he[:, P * c:P * c + P], ident)
                        last.then_inc(sN["blk_htr"], 1)

                    def down(n):
                        pe.wait_ge(sN["blk_hl"], n)
                        pe.wait_ge(s_split[2], n)
                        pe.wait_ge(sN["y_read"], n)
                        for q in range(2):
                            last = three_passes(ps[2 + q][:, :], lambda c: (hh[:, c, :], hl[:, c, :]),
                                                lambda c: (wh[2][:, c, 512 * q:512 * q + 512], wl[2][:, c, 512 * q:512 * q + 512]),
                                                F // P)
                        last.then_inc(s_used[2], 1)

                    pe.wait_ge(s_ga, 16)
                    turn(0, "blk_tr")
                    turn(1, "x_free")
                    gate_up(1)
                    with pe.Fori(1, block_count(pe)) as g:
                        pe.wait_ge(s_ga, 16 * g + 16)
                        turn(0, "blk_tr")
                        turn_h(g)
                        turn(1, "x_free")
                        down(g)
                        gate_up(g + 1)
                    turn_h(block_count(pe))
                    down(block_count(pe))

                @block.scalar
                def _(act):
                    act.sem_inc(s_ys, 16)
                    act.wait_ge(s_zero, 16)

                    def head(q, n, again=True):
                        act.wait_ge(s_raw[q], 16 * n)
                        if again:
                            act.wait_ge(s_used[q], n - 1)
                        nc.scalar.activation(wh[q][:, :, :], raw[q][:, :, :], ACT.Copy).then_inc(s_head[q], 1)

                    def rows_head(half, n, again=True):
                        act.wait_ge(sN["x_free" if half else "blk_tr"], n)
                        if again and not half:
                            act.wait_ge(s_used[1], n - 1)
                        for c in range(4 * half, 4 * half + 4):
                            last = nc.scalar.activation(xh[:, c, :], ps[4 + half][:, P * (c % 4):P * (c % 4) + P], ACT.Copy,
                                                        scale=pc("gffn", c))
                        last.then_inc(sN["blk_xh"], 1)

                    def silu(n):
                        act.wait_ge(s_used[0], n)
                        nc.scalar.activation(he[:, :], ps[0][:, :], ACT.Silu).then_inc(sN["blk_silu"], 1)

                    def h_head(n):
                        act.wait_ge(sN["blk_htr"], n)
                        nc.scalar.activation(hh[:, :, :], ps[6][:, :].rearrange("p (c t) -> p c t", t=P), ACT.Copy)                          .then_inc(sN["blk_hh"], 1)

                    def store(n):
                        act.wait_ge(sN["y_read"], n + 1)
                        act.dma_start(yrows[bass.ds(P * (n - 1), P), :], yb[:, :]).then_inc(s_ys, 16)

                    rows_head(0, 1, again=False)
                    rows_head(1, 1, again=False)
                    for q in range(3):
                        head(q, 1, again=False)
                    silu(1)
                    with act.Fori(1, block_count(act)) as g:
                        head(0, g + 1)
                        rows_head(0, g + 1)
                        h_head(g)
                        rows_head(1, g + 1)
                        head(1, g + 1)
                        store(g)
                        head(2, g + 1)
                        silu(g + 1)
                    h_head(block_count(act))
                    store(block_count(act))
                    act.wait_ge(s_ys, 16 * block_count(act) + 16)
                    act.nop(nofuse=True)

                @block.vector
                def _(dve):
                    dve.sem_inc(sN["y_read"], 1)

                    def rest(q, n):
                        dve.wait_ge(s_head[q], n)
                        nc.vector.tensor_tensor(wl[q][:, :, :], raw[q][:, :, :], wh[q][:, :, :].bitcast(F32), ALU.subtract)                          .then_inc(s_split[q], 1)

                    def rows_rest(half, n):
                        dve.wait_ge(sN["blk_xh"], 2 * n - 1 + half)
                        for c in range(4 * half, 4 * half + 4):
                            last = nc.vector.scalar_tensor_tensor(xl[:, c, :], ps[4 + half][:, P * (c % 4):P * (c % 4) + P], pc("gffn", c),
                                                                  xh[:, c, :].bitcast(F32), ALU.mult, ALU.subtract)
                        last.then_inc(sN["blk_xl"], 1)

                    def h_rest(n):
                        dve.wait_ge(sN["blk_hh"], n)
                        nc.vector.tensor_tensor(hl[:, :, :], ps[6][:, :].rearrange("p (c t) -> p c t", t=P), hh[:, :, :].bitcast(F32),
                                                ALU.subtract).then_inc(sN["blk_hl"], 1)

                    def gated(n):
                        dve.wait_ge(sN["blk_silu"], n)
                        dve.wait_ge(s_used[1], n)
                        nc.vector.tensor_tensor(he[:, :], he[:, :], ps[1][:, :], ALU.mult).then_inc(sN["blk_h"], 1)

                    def outputs(n):
                        nc.vector.tensor_copy(gate[:, :], slots[:, bass.ds(n + (NBC - 1), 1)]).then_inc(sN["gate_in"], 1)
                        dve.wait_ge(sN["gate_in"], n)
                        dve.wait_ge(s_used[2], n)
                        dve.wait_ge(s_ys, 16 * n)
                        for q in range(2):
                            last = nc.vector.tensor_scalar(yb[:, 512 * q:512 * q + 512], ps[2 + q][:, :], gate[:, 0:1], None, ALU.mult)
                        last.then_inc(sN["y_read"], 1)

                    rows_rest(0, 1)
                    rows_rest(1, 1)
                    for q in range(3):
                        rest(q, 1)
                    gated(1)
                    with dve.Fori(1, block_count(dve)) as g:
                        rows_rest(0, g + 1)
                        h_rest(g)
                        rows_rest(1, g + 1)
                        rest(0, g + 1)
                        rest(1, g + 1)
                        outputs(g)
                        rest(2, g + 1)
                        gated(g + 1)
                    h_rest(block_count(dve))
                    outputs(block_count(dve))
            mem_e.close()

            mem_c = ExitStack()
            ya = mem_c.enter_context(nc.sbuf_tensor("ya", [P, 4, D], F32))
            with nc.Block() as block:
                @block.gpsimd
                def _(gp):
                    for n in range(2 * NT):
                        t, k = n // 2, n % 2
                        if n >= 4:
                            gp.wait_ge(sN["y_added"], n - 3)
                        gp.indirect_dma_start(out=ya[:, n % 4, :], out_offset=None, in_=yrows,
                                              in_offset=bass.IndirectOffsetOnAxis(ap=pair_slot[:, t, k:k + 1], axis=0))\
                          .then_inc(s_yg[n % 4], 16)

                @block.vector
                def _(dve):
                    for n in range(2 * NT):
                        t, k = n // 2, n % 2
                        dve.wait_ge(s_yg[n % 4], 16 * (n // 4 + 1))
                        if k:
                            dve.wait_ge(sN["y_added"], n)
                        nc.vector.tensor_tensor(x[:, t, :], x[:, t, :], ya[:, n % 4, :], ALU.add).then_inc(sN["y_added"], 1)
            mem_c.close()

        with nc.Block() as block:
            @block.sync
            def _(sp):
                sp.dma_start(out[0].rearrange("(n p) d -> p n d", p=P), x[:, :, :]).then_inc(s_out, 16)
                sp.wait_ge(s_out, 16)


_INS = ["x", "mem", "rel_bias", "norm_mix", "w_in", "gla_wa2", "gla_ba", "gla_onorm", "dsa_qnorm", "dsa_knorm", "conv_w",
        "conv_b", "conv_ln_g", "conv_ln_b", "w_out", "norm_x", "norm_mem", "w_cq", "w_ckv", "x_qnorm", "x_knorm", "w_co",
        "norm_ffn", "w_rg", "b_rg", "w_re", "b_re", "w_gate", "w_up", "w_down"]


def kernel(**inputs):
    import concourse.bacc as _bacc
    from concourse.bass_utils import run_bass_kernel_spmd as _run

    nc = _bacc.Bacc("TRN2", target_bir_lowering=False, num_devices=1)
    arrays, handles = {}, {}
    cf, onehot, cmask = host_constants()
    for name, a in [(n, inputs[n]) for n in _INS] + [("cf", cf), ("onehot", onehot), ("cmask", cmask)]:
        a = np.ascontiguousarray(a)
        arrays[f"in_{name}"] = a
        handles[name] = nc.dram_tensor(f"in_{name}", a.shape, mybir.dt.from_np(a.dtype), kind="ExternalInput").ap()
    out = nc.dram_tensor("out_0", (1, S, D), F32, kind="ExternalOutput").ap()
    program(nc, handles, out)
    r = _run(nc, [arrays], core_ids=[0])
    return r.results[0]["out_0"]
```

```python
from contextlib import ExitStack

import concourse.bass as bass
from concourse import mybir
import numpy as np

F32 = mybir.dt.float32
I32 = mybir.dt.int32
U32 = mybir.dt.uint32
U8 = mybir.dt.uint8
F32R = mybir.dt.float32r
ALU = mybir.AluOpType
ACT = mybir.ActivationFunctionType
AX = mybir.AxisListType.X

P = 128
D, S, L, M = 1024, 512, 2, 256
KD = D // P
NT = S // P
GH, GK, GV, RANK = 4, 48, 96, 16
AH, AD = 6, 64
IH, ID = 8, 64
TOPK = S // 4
CC, CW = 256, 31
XH, XD = 4, 64
NB, MAXD = 32, 128
NG, EG, E, F = 4, 4, 16, 512
PAIRS = 2 * S
MAXB = E + (PAIRS - E) // P
MINB = PAIRS // P
NBC = MAXB + 1
EPS = 1e-6
SLOT = KD * 512
NSLOT = 3
NEG, TAKEN, FAR = -3.0e38, -3.4e38, -1.0e30
HALVES = [1, 2, 4, 8, 16, 32, 64]
NLEV = len(HALVES)

SIZES = dict(gq=GH * GK, gk=GH * GK, gv=GH * GV, lr=RANK, gr=GH * GV, dq=AH * AD, dk=AH * AD, dv=AH * AD,
             iq=IH * ID, ik=ID, iw=IH, ca=CC, cg=CC)
COL, _at = {}, 0
for _n, _w in SIZES.items():
    COL[_n] = _at
    _at += _w

CHUNKS = [
    [(0, COL["ik"], ID), (ID, COL["ik"], ID), (2 * ID, COL["lr"], RANK), (2 * ID + RANK, COL["iw"], IH)],
    [(0, COL["iq"], IH * ID)],
    [(0, COL["dq"], AH * AD)],
    [(0, COL["dk"], AH * AD)],
    [(0, COL["dv"], AH * AD)],
    [(0, COL["ca"], 2 * CC)],
    [(64 * h, COL["gq"] + GK * h, 64) for h in range(GH)] + [(256 + 64 * h, COL["gk"] + GK * h, 64) for h in range(GH)],
    [(0, COL["gv"], GH * GV)],
    [(0, COL["gr"], GH * GV)],
]
LOADS = [sum(len(c) for c in CHUNKS[:i + 1]) for i in range(len(CHUNKS))]


def host_constants():
    p, c = np.arange(P)[:, None], np.arange(P)[None, :]
    ident = (p == c).astype(np.float32)
    same_head = (p // 64 == c // 64).astype(np.float32)
    before = (p < c).astype(np.float32)
    iota = np.broadcast_to(c, (P, P)).astype(np.float32)
    dist = 255 - np.arange(384)
    d = np.maximum(dist, 1).astype(np.float32)
    large = NB // 2 + (np.log(d / np.float32(NB // 2)) / np.float32(np.log(MAXD / (NB // 2))) * (NB // 2)).astype(np.int32)
    bucket = np.where(dist < NB // 2, dist, np.minimum(large, NB - 1))
    onehot = (bucket[None, :] == np.arange(NB)[:, None]) & (dist >= 0)[None, :]
    onehot = onehot.astype(np.float32)
    steps = np.ones((P, S), np.float32)
    steps[:, ::P] = 0.0
    tok = (p + P * np.arange(NT)[None, :]).astype(np.float32)
    cf = np.concatenate([ident, same_head, before, iota, tok, steps], 1)
    masks = []
    for h in HALVES:
        masks.append((p // (2 * h) == c // (2 * h)) & ((c // h) % 2 == 1) & ((p // h) % 2 == 0))
    masks.append(p == c)
    return cf, onehot, np.stack(masks, 1).reshape(P, -1).astype(np.float32)


def program(nc, A, out):
    ctx = ExitStack()
    with ctx:
        def sb(name, shape, dt=F32):
            return ctx.enter_context(nc.sbuf_tensor(name, shape, dt))

        def sem(name):
            s = ctx.enter_context(nc.semaphore(name))
            (pool_dma_sems if name.startswith("pd_") else sems).append(s)
            return s

        def view(t, off, *shape, rows=P):
            n = int(np.prod(shape))
            ap = t[0:rows, off:off + n]
            names = "abcd"[:len(shape)]
            if len(shape) > 1:
                ap = ap.rearrange(f"p ({' '.join(names)}) -> p {' '.join(names)}",
                                  **{names[i]: shape[i] for i in range(1, len(shape))})
            return ap

        sems, pool_dma_sems = [], []

        x = sb("x", [P, NT, D])
        cf = sb("cf", [P, 4 * P + NT + S])
        cmask = sb("cmask", [P, (NLEV + 1) * P], U8)
        ones = sb("ones", [P, P])
        toep = sb("toep", [P, AH, 2 * P])
        bfar = sb("bfar", [P, AH])
        iw = sb("iw", [P, NT, IH])
        par = sb("par", [P, 64])
        convw = sb("convw", [P, 2, CW + 1])
        wa2 = sb("wa2", [RANK, 2, P])
        m8 = sb("m8", [P, 8])
        small = sb("small", [P, 64])
        epst = sb("epst", [P, 1])
        zero = sb("zero", [P, 256])
        ebl = sb("ebl", [P, 2, NT])
        slots = sb("slots", [P, 2 * NBC])
        slot_tok = sb("slot_tok", [P, NBC], U32)
        pair_slot = sb("pair_slot", [P, NT, 2], U32)
        blk = sb("blk", [1, 128])
        idx = sb("idx", [P, 1], U32)
        gate = sb("gate", [P, 1])
        blki = sb("blki", [1, 32], I32)

        ident, same_head = cf[:, 0:P], cf[:, P:2 * P]
        before, iota = cf[:, 2 * P:3 * P], cf[:, 3 * P:4 * P]
        tok = cf[:, 4 * P:4 * P + NT]
        steps = cf[:, 4 * P + NT:]
        masks = cmask[:, :].rearrange("p (l t) -> p l t", t=P)

        ps = [ctx.enter_context(nc.psum_tensor(f"ps{i}", [P, 512], F32)) for i in range(8)]

        skew = nc.dram_tensor("skew", [P * AH * 384 + 384], F32, kind="Internal").ap()
        hrows = nc.dram_tensor("hrows", [S, D], F32, kind="Internal").ap()
        yrows = nc.dram_tensor("yrows", [MAXB * P, D], F32, kind="Internal").ap()

        PC = dict(gmix=0, gx=8, gmem=16, gffn=24, ba=32, onorm=34, dqn=35, dkn=36, clg=37, clb=39, cqn=41, ckn=42, cb=43)
        NPC = 45

        def pc(name, i=0, rows=P):
            return par[0:rows, PC[name] + i:PC[name] + i + 1]

        once = ExitStack()
        s_const, s_x0, s_cv, s_zt, s_skw, s_toep, s_far = (once.enter_context(nc.semaphore(n)) for n in (
            "constants_in", "x_in", "c_dve", "zero_tile", "skew_written", "toep_in", "far_bias"))
        s_w = [sem(f"w_in_slot{i}") for i in range(NSLOT)]
        s_par, s_wa2, s_cwr = sem("params_in"), sem("wa2_in"), sem("conv_taps_in")
        cv_, ca_, cp_ = sem("dve_chain"), sem("act_chain"), sem("pool_chain")
        sN = {n: sem(n) for n in (
            "prow_zero", "par_t", "root_done", "xn_ready", "tr_done", "hT_ready", "proj_done", "proj_out", "dots_done",
            "relu_done", "relu_used", "causal_done", "conv_done", "sq_ready", "sum_done", "sums_root", "normed",
            "a_done", "sig_abs", "sig_ln", "b_ready", "lev_d", "lev_e", "lev_q", "lev_k", "lev_mm", "lev_cp", "at_zero",
            "eb_done", "el_done", "qexp_done", "kdec_done", "kt_done", "kt_out", "upd_done", "state_done", "o_done",
            "osq", "osum", "oroot", "odone", "mean_done", "cen_done", "csq", "var_done", "croot", "cnorm", "lg_done",
            "bm_done", "lg_out", "exp_done", "p_norm", "pt_done", "pt_out", "pv_done", "cw_t", "cw_out", "sel_done",
            "op_done", "x_mid", "xm_root", "xm_xn", "xm_tr", "xm_hT", "mm_root", "mm_xn", "mm_tr", "mm_T", "cp_done",
            "cp_out", "cn_sq", "cn_sum", "cn_root", "cn_done", "cl_done", "c_nm", "c_exp", "c_norm", "c_pt", "c_pto",
            "c_pv", "c_o", "co_done", "x_cross", "f_root", "f_xn", "f_tr", "f_hT", "r_done", "r_lin", "r_exp", "r_hot",
            "r_rank", "r_one", "r_slots", "blk_tr", "blk_silu", "blk_h", "blk_htr", "x_free", "mem_in", "wo_in",
            "wckv_in", "wcq_in", "wco_in", "wr_in", "rb_in", "idx", "y_read", "y_added", "er_done", "blk_xh", "blk_xl",
            "blk_hh", "blk_hl", "gate_in", "tile_out", "iw_t", "iw_out",)}
        s_ga = sem("pd_rows")
        s_yg = [sem(f"pd_ygather{i}") for i in range(4)]
        s_hr = [sem(f"hrows_stored{i}") for i in range(NT)]
        s_ys = sem("y_rows_stored")
        s_out = sem("out_stored")
        s_zero = ctx.enter_context(nc.semaphore("yrows_zeroed"))

        def pair_rows(h, n):
            return slice(64 * (h % 2), 64 * (h % 2) + n)

        count = {}

        def engine(eng, own):
            def do(ins, mark=None, wait=True):
                s = sN[mark] if mark else own
                count[s] = count.get(s, 0) + 1
                ins.then_inc(s, 1)
                if wait:
                    eng.wait_ge(s, count[s])
            return do

        def root(do, out, src, n, mark, wait=True):
            do(nc.scalar.activation(out, src, ACT.Sqrt, bias=epst[0:out.shape[0], :], scale=1.0 / n), mark, wait=wait)

        def inverse_roots(act, do, banks, n, summed, mark, rows=P, outs=None):
            for m, bank in enumerate(banks):
                act.wait_ge(sN[summed], m + 1)
                do(nc.scalar.activation(ps[bank][0:rows, :], ps[bank][0:rows, :], ACT.Ln, bias=epst[0:rows, :], scale=1.0 / n))
            for m, bank in enumerate(banks):
                out = outs[m][0:rows, :] if outs else ps[bank][0:rows, :]
                do(nc.scalar.activation(out, ps[bank][0:rows, :], ACT.Exp, scale=-0.5), mark, wait=False)

        arena = once.enter_context(nc.sbuf_tensor("tables", [P, 8192], F32))
        onehot = view(arena, 6144, 384, rows=NB)
        with nc.Block() as block:
            @block.sync
            def _(sp):
                sp.dma_start(cf[:, :], A["cf"]).then_inc(s_const, 16)
                sp.dma_start(view(arena, 7168, (NLEV + 1) * P), A["cmask"]).then_inc(s_const, 16)
                sp.dma_start(onehot, A["onehot"]).then_inc(s_const, 16)
                sp.dma_start(small[0:NB, 0:AH], A["rel_bias"]).then_inc(s_const, 16)
                sp.dma_start(x[:, :, :], A["x"][0].rearrange("(n p) d -> p n d", p=P)).then_inc(s_x0, 16)
                sp.wait_ge(s_far, 2 + AH)
                sp.dma_start(skew[0:P * AH * 384].rearrange("(p h j) -> p h j", h=AH, j=384),
                             view(arena, 0, AH, 384)).then_inc(s_skw, 16)
                sp.wait_ge(s_skw, 16)
                sp.dma_start(toep[:, :, :], bass.AP(tensor=skew.tensor, offset=P - 1,
                                                    ap=[[AH * 384 - 1, P], [384, AH], [1, 2 * P]])).then_inc(s_toep, 16)
                sp.wait_ge(s_toep, 16)
                sp.wait_ge(s_x0, 16)

            @block.scalar
            def _(act):
                act.wait_ge(s_zt, 1)
                act.dma_start(yrows.rearrange("(p n) (c d) -> p (n c) d", p=P, d=256),
                              zero[:, :].unsqueeze(1).to_broadcast([P, MAXB * D // 256, 256])).then_inc(s_zero, 16)

            @block.vector
            def _(dve):
                nc.vector.memset(zero[:, :], 0.0).then_inc(s_zt, 1)
                nc.vector.memset(ones[:, :], 1.0).then_inc(s_cv, 1)
                nc.vector.memset(epst[:, :], EPS).then_inc(s_cv, 1)
                nc.vector.memset(wa2[:, :, :], 0.0).then_inc(s_cv, 1)
                dve.wait_ge(s_const, 64)
                dve.wait_ge(s_cv, 3)
                for h in range(AH):
                    nc.vector.tensor_scalar(view(arena, 4096 + P * h, P, rows=NB), ones[0:NB, :], small[0:NB, h:h + 1],
                                            None, ALU.mult).then_inc(s_cv, 1)
                for h in range(AH):
                    dve.wait_ge(cv_, h + 1)
                    nc.vector.tensor_copy(view(arena, 384 * h, 384), ps[h % 2][:, 0:384]).then_inc(s_far, 1)
                dve.wait_ge(cp_, 1)
                nc.vector.tensor_copy(bfar[:, :], ps[2][:, 0:AH]).then_inc(s_far, 1)
                nc.vector.tensor_copy(cmask[:, :], view(arena, 7168, (NLEV + 1) * P)).then_inc(s_far, 1)

            @block.tensor
            def _(pe):
                pe.wait_ge(s_const, 64)
                for h in range(AH):
                    pe.wait_ge(s_cv, 4 + h)
                    if h >= 2:
                        pe.wait_ge(s_far, h - 1)
                    nc.tensor.matmul(ps[h % 2][:, 0:384], view(arena, 4096 + P * h, P, rows=NB), onehot,
                                     start=True, stop=True).then_inc(cv_, 1)
                for h in range(AH):
                    last = nc.tensor.matmul(ps[2][:, h:h + 1], view(arena, 4096 + P * h, P, rows=NB), onehot[:, 0:1],
                                            start=True, stop=True)
                last.then_inc(cp_, 1)

        once.close()
        s_used, s_head, s_split = ([sem(f"{n}_{q}") for q in ("gate", "up", "down")]
                                   for n in ("products_done", "head_done", "rest_done"))
        s_raw = [[sem(f"raw_in_{q}{j}") for j in range(2)] for q in ("gate", "up", "down")]
        s_split.append(sem("rest_done_down_first"))
        with nc.Fori(0, L) as l:
            with nc.Block() as block:
                @block.sync
                def _(sp):
                    for s in sems[0::4]:
                        sp.sem_clear(s)

                @block.scalar
                def _(act):
                    for s in sems[1::4]:
                        act.sem_clear(s)

                @block.vector
                def _(dve):
                    for s in sems[2::4]:
                        dve.sem_clear(s)

                @block.tensor
                def _(pe):
                    for s in sems[3::4]:
                        pe.sem_clear(s)

                @block.gpsimd
                def _(gp):
                    gp.dma_reset()
                    for s in pool_dma_sems:
                        gp.sem_clear(s)

            mem_a = ExitStack()

            def sba(name, shape):
                return mem_a.enter_context(nc.sbuf_tensor(name, shape, F32))

            arena = sba("arena", [P, 6 * SLOT])
            scratch = sba("scratch", [P, 7680])
            hT = sba("hT", [P, KD, S])
            mixg = sba("mixg", [P, GH, S])
            mixr = sba("mixr", [P, 5, S])
            sel = sba("sel", [P, NT, S])
            sq = sba("sq", [P, 2, S])
            rs = sba("rs", [P, 2, S])
            wide = [rs[:, 0, :], rs[:, 1, :], sq[:, 0, :], sq[:, 1, :]]
            ik2 = sq[:, 1, :]
            prow = rs[0:NPC, 1, 0:P]

            def slot(i):
                return view(arena, i * SLOT, KD, 512)

            up = 3 * SLOT
            gq, gk, b = (view(arena, up + 1024 * i, 2, S) for i in range(3))
            st = view(arena, up + 1024, 3, 2, 2 * GV)
            gv = view(arena, up + 3072, NT, GH * GV)
            gr = view(arena, up + 4608, GH, S, rows=GV)
            AT = view(arena, up + 6656, NT, GH, P)
            qexp, kdec = view(arena, up + 8704, 2, S), view(arena, up + 9728, 2, S)
            kdecT = view(arena, up + 10752, NT, 2, P)
            lrT = view(arena, up + 11776, S, rows=RANK)
            lrwT = view(arena, up + 11776, S, rows=RANK + IH)
            cin = view(arena, up + 8704, 2, S + CW - 1)
            csig = view(arena, up + 8704 + 2 * (S + CW - 1), 2, S)
            xn = view(scratch, 0, 2, D)
            relu = view(scratch, 0, 4, S)
            ld, lq, lk = (view(scratch, 1024 * i, 2, S) for i in range(3))
            lg, bm, pT = (view(scratch, 1024 * i, 2, S) for i in range(3))
            dq, dk = view(scratch, 3072, 3, S), view(scratch, 4608, 3, S)
            dv = view(scratch, 6144, NT, AH * AD)
            iq = mixg[:, :, :]
            wog = view(arena, 0, GH, D, rows=GV)
            wor = view(arena, GH * D, 5, D)
            wckv = view(scratch, 3072, KD, 512)
            wcq = view(arena, up + 4096, KD, 256)
            wco = view(arena, up + 6144, 2, D)
            memT = view(arena, up + 8192, KD, M)
            ckT = view(arena, up + 10240, 2, M)
            cv = view(arena, up + 10752, 2, XH * XD)
            cqT = view(arena, up + 11264, 2, S)
            mem = view(arena, (GH + 5) * D, 2, D)
            clg, cpT = view(arena, up, 2, M), view(arena, up + 512, 2, 2, P)
            coT = view(arena, up + 1024, 2, S)
            oneP, oneB = view(arena, up + 2048, 2, P), view(arena, up + 2304, 2, 2 * NBC)
            selw = sel[:, :, :].rearrange("p n s -> p (n s)")
            rout = view(selw, 0, NT, 224)
            wr = view(selw, 1024, KD, NG + E)
            lds = [ld, view(selw, 0, 2, S)]
            lqs = [lq, view(selw, 1024, 2, S)]
            lks = [lk, qexp]
            def layer(name):
                return A[name][bass.ds(l, 1)]

            PARAMS = [("gmix", "norm_mix", KD, P, 0), ("gx", "norm_x", KD, P, 0), ("gmem", "norm_mem", KD, P, 0),
                      ("gffn", "norm_ffn", KD, P, 0), ("onorm", "gla_onorm", 1, GV, 0),
                      ("clg", "conv_ln_g", 2, P, 0), ("clb", "conv_ln_b", 2, P, 0), ("cb", "conv_b", 2, P, 0)]
            HEADP = [("dqn", "dsa_qnorm"), ("dkn", "dsa_knorm"), ("cqn", "x_qnorm"), ("ckn", "x_knorm")]
            NPAR = len(PARAMS) + len(HEADP) + 1

            JOBS = [(0, 0, P, "T", "ik", 0), (0, 2 * ID, RANK + IH, "T", "lr", 0)]
            JOBS += [(1, P * i, P, "T", "iq", i) for i in range(4)]
            JOBS += [(2, P * i, P, "T", "dq", i) for i in range(3)] + [(3, P * i, P, "T", "dk", i) for i in range(3)]
            JOBS += [(4, 0, AH * AD, "tok", "dv", i) for i in range(NT)]
            JOBS += [(5, P * i, P, "T", "ca", i) for i in range(2)] + [(5, CC + P * i, P, "T", "cg", i) for i in range(2)]
            JOBS += [(6, P * i, P, "T", "gq", i) for i in range(2)] + [(6, 2 * P + P * i, P, "T", "gk", i) for i in range(2)]
            JOBS += [(7, 0, GH * GV, "tok", "gv", i) for i in range(NT)]
            JOBS += [(8, GV * i, GV, "T", "gr", i) for i in range(GH)]
            NJ = len(JOBS)

            def done(name):
                return max(n for n, j in enumerate(JOBS) if j[4] == name) + 1

            DEST = dict(ik=lambda i: ik2[:, :], lr=lambda i: lrwT, iq=lambda i: iq[:, i, :],
                        ca=lambda i: cin[:, i, CW - 1:], cg=lambda i: csig[:, i, :], dq=lambda i: dq[:, i, :],
                        dk=lambda i: dk[:, i, :], dv=lambda i: dv[:, i, :], gq=lambda i: gq[:, i, :],
                        gk=lambda i: gk[:, i, :], gv=lambda i: gv[:, i, :], gr=lambda i: gr[:, i, :])
            AFTER_IDX = done("iq")
            AFTER_DSA = done("dv")
            STEPS = [(i, h) for i in range(NT) for h in range(AH)]
            NS = len(STEPS)

            def parts_of(n):
                m = (NJ - AFTER_DSA) * KD
                return range(m * n // NS, m * (n + 1) // NS)

            def taps_of(n):
                first = NS * (done("cg") - AFTER_DSA) // (NJ - AFTER_DSA) + 1
                return range(max(0, 2 * CW * (n - first) // (NS - first)), max(0, 2 * CW * (n + 1 - first) // (NS - first)))

            QK_SUMS = [3, 4, 5, 6, 7, AFTER_DSA % 3]
            QK_NEXT = {n: (2 * n, 2 * n + 1) for n in range(3)}
            DOTS = [(i, h) for i in range(NT) for h in range(IH)]

            def merge(dve, do, v, c):
                dve.wait_ge(sN["lev_mm"], NT * v + c + 1)
                if v == 0 and c == 0:
                    dve.wait_ge(sN["at_zero"], 1)
                m = masks[:, v, :].unsqueeze(1).unsqueeze(1).to_broadcast([P, 2, 2, P])
                c0 = c - c % 2
                do(nc.vector.copy_predicated(AT[:, c0:c0 + 2, c % 2:GH:2, :], m,
                                             ps[4 + c][:, :].rearrange("p (c h t) -> p c h t", c=2, t=P)), "lev_cp")

            with nc.Block() as block:
                @block.sync
                def _(sp):
                    sp.wait_ge(sN["prow_zero"], 1)
                    for name, src, n, w, _ in PARAMS:
                        sp.dma_start(prow[PC[name]:PC[name] + n, 0:w], layer(src).rearrange("o (c p) -> (o c) p", p=w))\
                          .then_inc(s_par, 16)
                    for name, src in HEADP:
                        sp.dma_start(prow[PC[name]:PC[name] + 1, :].rearrange("o (a c) -> o a c", a=2),
                                     layer(src).unsqueeze(1).to_broadcast([1, 2, 64])).then_inc(s_par, 16)
                    sp.dma_start(prow[PC["ba"]:PC["ba"] + 2, :].rearrange("p (a c) -> p a c", a=2)[:, :, 0:GK],
                                 layer("gla_ba").rearrange("o (p a c) -> (o p) a c", p=2, a=2)).then_inc(s_par, 16)
                    w_in = A["w_in"][bass.ds(l, 1)].rearrange("o (c p) n -> p (o c) n", p=P)
                    for n, parts in enumerate(CHUNKS):
                        if n >= NSLOT:
                            sp.wait_ge(sN["proj_done"], max(m for m, j in enumerate(JOBS) if j[0] == n - NSLOT) + 1)
                        for dst, col, width in parts:
                            sp.dma_start(slot(n % NSLOT)[:, :, dst:dst + width], w_in[:, :, col:col + width])\
                              .then_inc(s_w[n % NSLOT], 16)
                        if n == 0:
                            for h in range(GH):
                                sp.dma_start(wa2[:, h // 2, 64 * (h % 2):64 * (h % 2) + GK],
                                             layer("gla_wa2")[:, :, GK * h:GK * h + GK].rearrange("o r c -> (o r) c"))\
                                  .then_inc(s_wa2, 16)
                            sp.dma_start(rs[0:CW, 0, 0:CC], layer("conv_w").rearrange("o j c -> (o j) c")).then_inc(s_cwr, 16)
                    sp.wait_ge(sN["proj_done"], NJ)
                    w = A["w_out"][bass.ds(l, 1)]
                    sp.dma_start(mem, A["mem"][0].rearrange("(n p) d -> p n d", p=P)).then_inc(sN["mem_in"], 16)
                    sp.dma_start(wog, w[:, 0:GH * GV, :].rearrange("o (h v) n -> v (o h) n", v=GV)).then_inc(sN["wo_in"], 16)
                    sp.dma_start(wor, w[:, GH * GV:D, :].rearrange("o (c p) n -> p (o c) n", p=P)).then_inc(sN["wo_in"], 16)
                    sp.wait_ge(sN["pv_done"], NS)
                    sp.dma_start(wckv, layer("w_ckv").rearrange("o (c p) n -> p (o c) n", p=P)).then_inc(sN["wckv_in"], 16)
                    sp.wait_ge(sN["mem_in"], 16)
                    sp.wait_ge(sN["wo_in"], 32)
                    sp.wait_ge(sN["wckv_in"], 16)

                @block.tensor
                def _(pe):
                    pe.wait_ge(s_par, 16 * NPAR)
                    nc.tensor.transpose(ps[7][:, 0:NPC], prow, ident[0:NPC, 0:NPC]).then_inc(sN["par_t"], 1)
                    for t in range(NT):
                        pe.wait_ge(sN["xn_ready"], t + 1)
                        for q in range(2):
                            n = 2 * t + q
                            if n >= 2:
                                pe.wait_ge(sN["hT_ready"], n - 1)
                            for c in range(4):
                                last = nc.tensor.transpose(ps[4 + q][:, P * c:P * c + P],
                                                           xn[:, t % 2, P * (4 * q + c):P * (4 * q + c) + P], ident)
                            last.then_inc(sN["tr_done"], 1)
                    pe.wait_ge(sN["hT_ready"], 8)

                    pe.wait_ge(s_cwr, 16)
                    for i in range(2):
                        last = nc.tensor.transpose(ps[6][:, CW * i:CW * i + CW], rs[0:CW, 0, P * i:P * i + P], ident[0:CW, 0:CW])
                    last.then_inc(sN["cw_t"], 1)

                    def project(n, chunks=range(KD)):
                        chunk, col, width, kind, name, i = JOBS[n]
                        k = chunk % NSLOT
                        first = JOBS.index(next(j for j in JOBS if j[0] == chunk))
                        if n == first and 0 in chunks:
                            parts = sum(len(CHUNKS[c]) for c in range(k, chunk + 1, NSLOT))
                            pe.wait_ge(s_w[k], 16 * parts)
                        if n >= 3 and 0 in chunks:
                            pe.wait_ge(sN["proj_out"], n - 2)
                        w = slot(k)
                        for c in chunks:
                            if kind == "T":
                                last = nc.tensor.matmul(ps[n % 3][0:width, :], w[:, c, col:col + width], hT[:, c, :],
                                                        start=(c == 0), stop=(c == KD - 1))
                            else:
                                last = nc.tensor.matmul(ps[n % 3][:, 0:width], hT[:, c, P * i:P * i + P],
                                                        w[:, c, col:col + width], start=(c == 0), stop=(c == KD - 1))
                        if KD - 1 in chunks:
                            last.then_inc(sN["proj_done"], 1)

                    for n in range(done("lr")):
                        project(n)
                    pe.wait_ge(s_wa2, 16 * GH)
                    pe.wait_ge(sN["proj_out"], done("lr"))
                    pe.wait_ge(sN["cw_out"], 1)
                    for i in range(2):
                        nc.tensor.matmul(ps[6 + i][:, :], wa2[:, i, :], lrT, start=True, stop=True).then_inc(sN["a_done"], 1)
                    for i in range(NT):
                        last = nc.tensor.transpose(ps[5][:, (RANK + IH) * i:(RANK + IH) * (i + 1)], lrwT[:, P * i:P * i + P],
                                                   ident[0:RANK + IH, 0:RANK + IH])
                    last.then_inc(sN["iw_t"], 1)
                    for n in range(done("lr"), AFTER_IDX):
                        project(n)
                    pe.wait_ge(sN["proj_out"], AFTER_IDX)
                    pe.wait_ge(sN["sig_abs"], 2)
                    pe.wait_ge(sN["iw_out"], 1)
                    for n, (i, h) in enumerate(DOTS):
                        if n >= 4:
                            pe.wait_ge(sN["relu_done"], n - 3)
                        r = pair_rows(h, ID)
                        nc.tensor.matmul(ps[4 + n % 4][:, 0:P * (i + 1)], iq[r, h // 2, P * i:P * i + P],
                                         ik2[r, 0:P * (i + 1)], start=True, stop=True).then_inc(sN["dots_done"], 1)
                    for n in range(AFTER_IDX, done("dk")):
                        project(n)
                    pe.wait_ge(sN["relu_done"], len(DOTS))
                    for m in range(NT):
                        project(done("dk") + m)
                        for n in QK_NEXT.get(m, ()):
                            pe.wait_ge(sN["sq_ready"], n + 1)
                            if n == 5:
                                pe.wait_ge(sN["proj_out"], AFTER_DSA - 2)
                            nc.tensor.matmul(ps[QK_SUMS[n]][:, :], same_head, sq[:, n % 2, :], start=True, stop=True)\
                              .then_inc(sN["sum_done"], 1)
                    pe.wait_ge(sN["normed"], 6)
                    pe.wait_ge(sN["proj_out"], AFTER_DSA)

                    def logits(n):
                        i, h = STEPS[n]
                        r = pair_rows(h, AD)
                        if n >= 2:
                            pe.wait_ge(sN["lg_out"], n - 1)
                        nc.tensor.matmul(ps[4 + n % 2][:, 0:P * (i + 1)], dq[r, h // 2, P * i:P * i + P],
                                         dk[r, h // 2, 0:P * (i + 1)], start=True, stop=True).then_inc(sN["lg_done"], 1)

                    def turn(n):
                        i, h = STEPS[n]
                        pe.wait_ge(sN["p_norm"], n + 1)
                        if n >= 2:
                            pe.wait_ge(sN["pt_out"], n - 1)
                        for j in range(i + 1):
                            last = nc.tensor.transpose(ps[6 + n % 2][:, P * j:P * j + P], lg[:, n % 2, P * j:P * j + P], ident)
                        last.then_inc(sN["pt_done"], 1)

                    def values(n):
                        i, h = STEPS[n]
                        pe.wait_ge(sN["pt_out"], n + 1)
                        if h == 0 and i:
                            pe.wait_ge(sN["tile_out"], i)
                        for j in range(i + 1):
                            last = nc.tensor.matmul(ps[3][pair_rows(h, AD), P * (h // 2):P * (h // 2) + P],
                                                    dv[:, j, AD * h:AD * h + AD], pT[:, n % 2, P * j:P * j + P],
                                                    start=(j == 0), stop=(j == i))
                        last.then_inc(sN["pv_done"], 1)

                    logits(0)
                    logits(1)
                    for n in range(len(STEPS)):
                        turn(n)
                        if n + 2 < len(STEPS):
                            logits(n + 2)
                        for m in parts_of(n):
                            project(AFTER_DSA + m // KD, range(m % KD, m % KD + 1))
                        if n >= 1:
                            values(n - 1)
                    values(len(STEPS) - 1)

                    pe.wait_ge(sN["conv_done"], 1)
                    pe.wait_ge(sN["proj_out"], NJ)
                    for i in range(2):
                        last = nc.tensor.matmul(ps[0][:, :], ones[:, :], mixr[:, 3 + i, :], start=(i == 0), stop=(i == 1))
                    last.then_inc(sN["mean_done"], 1)
                    for v in range(NLEV + 1):
                        if v == 1:
                            pe.wait_ge(sN["csq"], 2)
                            for i in range(2):
                                last = nc.tensor.matmul(ps[1][:, :], ones[:, :], sq[:, i, :], start=(i == 0), stop=(i == 1))
                            last.then_inc(sN["var_done"], 1)
                        if v < NLEV:
                            pe.wait_ge(sN["lev_q"], v + 1)
                            pe.wait_ge(sN["lev_k"], v + 1)
                        qq, kk = (lqs[v % 2], lks[v % 2]) if v < NLEV else (gq, gk)
                        for m in range(4):
                            if v >= 1:
                                pe.wait_ge(sN["lev_cp"], 4 * (v - 1) + m + 1)
                            for c in (m - m % 2, m - m % 2 + 1):
                                for h in (m % 2, m % 2 + 2):
                                    r = pair_rows(h, GK)
                                    at = 2 * P * (c % 2) + P * (h // 2)
                                    o, q = ps[4 + m][:, at:at + P], qq[r, h // 2, P * c:P * c + P]
                                    if v < NLEV:
                                        o, q = (a.rearrange("p (n w) -> p n w", w=2 * HALVES[v])[:, :, HALVES[v]:] for a in (o, q))
                                    last = nc.tensor.matmul(o, kk[r, h // 2, P * c:P * c + P], q, start=True, stop=True)
                            last.then_inc(sN["lev_mm"], 1)
                    pe.wait_ge(sN["kdec_done"], 1)
                    pe.wait_ge(sN["lev_cp"], NT * (NLEV + 1))
                    for i in range(2):
                        for c in range(NT):
                            last = nc.tensor.transpose(ps[4 + i][:, P * c:P * c + P], kdec[:, i, P * c:P * c + P], ident)
                        last.then_inc(sN["kt_done"], 1)
                    pe.wait_ge(sN["kt_out"], 2)
                    pe.wait_ge(sN["proj_out"], NJ)
                    for c in range(3):
                        for i in range(2):
                            last = nc.tensor.matmul(ps[5 + c][:, 192 * i:192 * i + 192], kdecT[:, c, i, :],
                                                    gv[:, c, 192 * i:192 * i + 192], start=True, stop=True)
                        last.then_inc(sN["upd_done"], 1)
                    pe.wait_ge(sN["qexp_done"], 1)
                    pe.wait_ge(sN["cnorm"], 2)
                    pe.wait_ge(sN["tile_out"], NT)
                    for c in range(NT):
                        if c >= 1:
                            pe.wait_ge(sN["state_done"], c)
                        for h in range(GH):
                            r = pair_rows(h, GK)
                            o = ps[h][0:GV, P * c:P * c + P]
                            last = nc.tensor.matmul(o, gv[:, c, GV * h:GV * h + GV], AT[:, c, h, :], start=True, stop=(c == 0))
                            if c:
                                last = nc.tensor.matmul(o, st[r, c - 1, h // 2, GV * (h % 2):GV * (h % 2) + GV],
                                                        qexp[r, h // 2, P * c:P * c + P], start=False, stop=True)
                    last.then_inc(sN["o_done"], 1)
                    for h in range(GH):
                        pe.wait_ge(sN["osq"], h + 1)
                        if h == 0:
                            pe.wait_ge(sN["state_done"], 3)
                        nc.tensor.matmul(ps[4 + h][0:GV, :], ones[0:GV, 0:GV], sq[0:GV, h % 2, :], start=True, stop=True)\
                          .then_inc(sN["osum"], 1)

                @block.scalar
                def _(act):
                    do = engine(act, ca_)
                    for t in range(NT):
                        if t >= 2:
                            act.wait_ge(sN["tr_done"], 2 * (t - 1))
                        do(nc.scalar.activation(xn[:, t % 2, :], x[:, t, :], ACT.Square, accum_out=small[:, t:t + 1]))
                        root(do, small[:, 4 + t:5 + t], small[:, t:t + 1], D, "root_done")

                    FUNC = dict(gr=ACT.Silu, cg=ACT.Sigmoid)

                    def evacuate(n):
                        chunk, col, width, kind, name, i = JOBS[n]
                        act.wait_ge(sN["proj_done"], n + 1)
                        if name == "gq" and i == 0:
                            act.wait_ge(sN["at_zero"], 1)
                        src = ps[n % 3][0:width, :] if kind == "T" else ps[n % 3][:, 0:width]
                        scale = GK ** -0.5 if name == "gq" else 1.0
                        nc.scalar.activation(DEST[name](i), src, FUNC.get(name, ACT.Copy), scale=scale)\
                          .then_inc(sN["proj_out"], 1)

                    for n in range(done("lr")):
                        evacuate(n)
                    for i in range(2):
                        act.wait_ge(sN["a_done"], i + 1)
                        act.wait_ge(sN["sig_abs"], i + 1)
                        do(nc.scalar.activation(ld[:, i, :], b[:, i, :], ACT.Abs))
                        do(nc.scalar.activation(ld[:, i, :], ld[:, i, :], ACT.Exp, scale=-1.0))
                        do(nc.scalar.activation(ld[:, i, :], ld[:, i, :], ACT.Ln, bias=ones[:, 0:1]), "sig_ln")
                    for n in range(done("lr"), AFTER_IDX):
                        evacuate(n)
                    act.wait_ge(sN["b_ready"], 2)
                    for n, (i, h) in enumerate(DOTS):
                        act.wait_ge(sN["dots_done"], n + 1)
                        if n >= 4:
                            act.wait_ge(sN["relu_used"], n - 3)
                        nc.scalar.activation(relu[:, n % 4, 0:P * (i + 1)], ps[4 + n % 4][:, 0:P * (i + 1)], ACT.Relu,
                                             scale=ID ** -0.5).then_inc(sN["relu_done"], 1)
                    for n in range(AFTER_IDX, done("dk")):
                        evacuate(n)
                    act.wait_ge(sN["proj_out"], done("dk"))
                    for m in range(NT):
                        for n in QK_NEXT.get(m, ()):
                            t = (dq if n < 3 else dk)[:, n % 3, :]
                            if n >= 2:
                                act.wait_ge(sN["sum_done"], n - 1)
                            do(nc.scalar.activation(sq[:, n % 2, :], t, ACT.Square), "sq_ready", wait=False)
                        evacuate(done("dk") + m)
                    inverse_roots(act, do, QK_SUMS, AD, "sum_done", "sums_root")
                    def exps(n):
                        i, h = STEPS[n]
                        act.wait_ge(sN["lg_out"], n + 1)
                        s = lg[:, n % 2, 0:P * (i + 1)]
                        nc.scalar.activation(s, s, ACT.Exp, bias=small[:, 8 + n % 2:9 + n % 2],
                                             accum_out=small[:, 10 + n % 2:11 + n % 2]).then_inc(sN["exp_done"], 1)

                    def turned(n):
                        i, h = STEPS[n]
                        act.wait_ge(sN["pt_done"], n + 1)
                        if n >= 2:
                            act.wait_ge(sN["pv_done"], n - 1)
                        nc.scalar.activation(pT[:, n % 2, 0:P * (i + 1)], ps[6 + n % 2][:, 0:P * (i + 1)], ACT.Copy)\
                          .then_inc(sN["pt_out"], 1)

                    def tile_output(i):
                        act.wait_ge(sN["pv_done"], AH * (i + 1))
                        nc.scalar.activation(mixr[:, 0:3, P * i:P * i + P], ps[3][:, 0:3 * P].rearrange("p (c t) -> p c t", t=P),
                                             ACT.Copy).then_inc(sN["tile_out"], 1)

                    exps(0)
                    for n in range(len(STEPS)):
                        if n + 1 < len(STEPS):
                            exps(n + 1)
                        turned(n)
                        for m in parts_of(n):
                            if m % KD == KD - 1:
                                evacuate(AFTER_DSA + m // KD)
                        if n and n % AH == 0:
                            tile_output(n // AH - 1)
                    tile_output(NT - 1)

                    for v in range(NLEV):
                        act.wait_ge(sN["lev_d"], v + 1)
                        d = lds[v % 2]
                        do(nc.scalar.activation(d, d, ACT.Abs))
                        do(nc.scalar.activation(d, d, ACT.Exp, scale=-1.0), "lev_e")
                        if v == 0:
                            for i in range(2):
                                act.wait_ge(sN["cen_done"], i + 1)
                                do(nc.scalar.activation(sq[:, i, :], mixr[:, 3 + i, :], ACT.Square), "csq", wait=False)
                        if v == 1:
                            act.wait_ge(sN["var_done"], 1)
                            inverse_roots(act, do, [1], CC, "var_done", "croot")
                        if v == 3:
                            act.wait_ge(sN["cnorm"], 2)
                            for i in range(2):
                                do(nc.scalar.activation(mixr[:, 3 + i, :], mixr[:, 3 + i, :], ACT.Silu, scale=pc("clg", i),
                                                        bias=pc("clb", i)), wait=False)
                    act.wait_ge(sN["lev_q"], NLEV)
                    act.wait_ge(sN["lev_k"], NLEV)
                    do(nc.scalar.activation(ld, b, ACT.Exp), "eb_done")
                    act.wait_ge(sN["el_done"], 1)
                    do(nc.scalar.activation(lq, lq, ACT.Exp, scale=-1.0), "er_done")
                    for i in range(2):
                        act.wait_ge(sN["kt_done"], i + 1)
                        do(nc.scalar.activation(kdecT[:, :, i, :], ps[4 + i][:, :].rearrange("p (c d) -> p c d", d=P), ACT.Copy),
                           "kt_out", wait=False)
                    act.wait_ge(sN["o_done"], 1)
                    for h in range(GH):
                        if h >= 2:
                            act.wait_ge(sN["osum"], h - 1)
                        do(nc.scalar.activation(sq[0:GV, h % 2, :], ps[h][0:GV, :], ACT.Square), "osq", wait=False)
                    inverse_roots(act, do, range(4, 4 + GH), GV, "osum", "oroot", rows=GV, outs=wide)

                @block.vector
                def _(dve):
                    do = engine(dve, cv_)
                    do(nc.vector.memset(prow, 0.0), "prow_zero")
                    dve.wait_ge(sN["par_t"], 1)
                    do(nc.vector.tensor_copy(par[:, 0:NPC], ps[7][:, 0:NPC]))
                    for t in range(NT):
                        dve.wait_ge(sN["root_done"], t + 1)
                        do(nc.vector.reciprocal(small[:, 12 + t:13 + t], small[:, 4 + t:5 + t]))
                        do(nc.vector.tensor_scalar(xn[:, t % 2, :], x[:, t, :], small[:, 12 + t:13 + t], None, ALU.mult), "xn_ready")
                        for q in range(2):
                            dve.wait_ge(sN["tr_done"], 2 * t + q + 1)
                            g = par[:, PC["gmix"] + 4 * q:PC["gmix"] + 4 * q + 4].unsqueeze(2).to_broadcast([P, 4, P])
                            do(nc.vector.tensor_tensor(hT[:, 4 * q:4 * q + 4, P * t:P * t + P],
                                                       ps[4 + q][:, :].rearrange("p (c t) -> p c t", t=P), g, ALU.mult), "hT_ready",
                               wait=False)
                    dve.wait_ge(sN["cw_t"], 1)
                    do(nc.vector.tensor_copy(convw[:, :, 0:CW], ps[6][:, 0:2 * CW].rearrange("p (i j) -> p i j", j=CW)), "cw_out")
                    for i in range(2):
                        dve.wait_ge(sN["a_done"], i + 1)
                        do(nc.vector.tensor_scalar(b[:, i, :], ps[6 + i][:, :], pc("ba", i), None, ALU.add), "sig_abs")
                    dve.wait_ge(sN["iw_t"], 1)
                    do(nc.vector.tensor_scalar(iw[:, :, :], ps[5][:, 0:NT * (RANK + IH)].rearrange("p (t c) -> p t c", t=NT)[:, :, RANK:],
                                               IH ** -0.5, None, ALU.mult), "iw_out")
                    for i in range(2):
                        dve.wait_ge(sN["sig_ln"], i + 1)
                        do(nc.vector.scalar_tensor_tensor(b[:, i, :], b[:, i, :], 0.0, ld[:, i, :], ALU.min, ALU.subtract))
                        do(nc.vector.tensor_scalar(b[:, i, :], b[:, i, :], 1.0 / 16.0, None, ALU.mult))
                        do(nc.vector.tensor_tensor_scan(lq[:, i, :], steps, b[:, i, :], 0.0, ALU.mult, ALU.add))
                        do(nc.vector.tensor_copy(b[:, i, :], lq[:, i, :]), "b_ready")
                    for n, (i, h) in enumerate(DOTS):
                        s = sel[:, i, 0:P * (i + 1)]
                        dve.wait_ge(sN["relu_done"], n + 1)
                        r, w = relu[:, n % 4, 0:P * (i + 1)], iw[:, i, h:h + 1]
                        if h == 0:
                            ins = nc.vector.tensor_scalar(s, r, w, None, ALU.mult)
                        else:
                            ins = nc.vector.scalar_tensor_tensor(s, r, w, s, ALU.mult, ALU.add)
                        do(ins, "relu_used")
                    for i in range(NT):
                        dve.wait_ge(sN["causal_done"], i + 1)
                        s = sel[:, i, 0:P * (i + 1)]
                        if i == 0:
                            do(nc.vector.tensor_scalar(s, s, 0.9 * NEG, FAR, ALU.is_lt, ALU.mult), "sel_done")
                            continue
                        for _ in range(TOPK // 8):
                            do(nc.vector.max(m8[:, :], s))
                            do(nc.vector.match_replace(s, m8[:, :], s, TAKEN))
                        do(nc.vector.tensor_scalar(s, s, 0.5 * (NEG + TAKEN), FAR, ALU.is_gt, ALU.mult), "sel_done")
                    for n in range(6):
                        t = (dq if n < 3 else dk)[:, n % 3, :]
                        dve.wait_ge(sN["sums_root"], n + 1)
                        do(nc.vector.scalar_tensor_tensor(t, t, pc("dqn" if n < 3 else "dkn"), ps[QK_SUMS[n]][:, :], ALU.mult, ALU.mult),
                           "normed")
                    def masked(n):
                        i, h = STEPS[n]
                        w = P * (i + 1)
                        dve.wait_ge(sN["lg_done"], n + 1)
                        dve.wait_ge(sN["bm_done"], n + 1)
                        if n >= 2:
                            dve.wait_ge(sN["pt_done"], n - 1)
                        s = lg[:, n % 2, 0:w]
                        do(nc.vector.scalar_tensor_tensor(s, ps[4 + n % 2][:, 0:w], AD ** -0.5, bm[:, n % 2, 0:w], ALU.mult, ALU.add))
                        do(nc.vector.reduce_max(small[:, 16 + n % 2:17 + n % 2], s, AX))
                        do(nc.vector.tensor_scalar(small[:, 8 + n % 2:9 + n % 2], small[:, 16 + n % 2:17 + n % 2], -1.0, None,
                                                   ALU.mult), "lg_out")

                    def normalise(n):
                        i, h = STEPS[n]
                        s = lg[:, n % 2, 0:P * (i + 1)]
                        dve.wait_ge(sN["exp_done"], n + 1)
                        do(nc.vector.reciprocal(small[:, 18:19], small[:, 10 + n % 2:11 + n % 2]))
                        do(nc.vector.tensor_scalar(s, s, small[:, 18:19], None, ALU.mult), "p_norm")

                    def conv_tap(m):
                        i, j = m // CW, m % CW
                        o = mixr[:, 3 + i, :]
                        if j == 0:
                            dve.wait_ge(sN["proj_out"], done("cg"))
                            do(nc.vector.tensor_tensor(cin[:, i, CW - 1:], cin[:, i, CW - 1:], csig[:, i, :], ALU.mult))
                            do(nc.vector.tensor_scalar(o, cin[:, i, 0:S], convw[:, i, 0:1], pc("cb", i), ALU.mult, ALU.add))
                        else:
                            do(nc.vector.scalar_tensor_tensor(o, cin[:, i, j:j + S], convw[:, i, j:j + 1], o, ALU.mult, ALU.add))

                    do(nc.vector.memset(cin[:, :, 0:CW - 1], 0.0))
                    masked(0)
                    for n in range(len(STEPS)):
                        if n + 1 < len(STEPS):
                            masked(n + 1)
                        normalise(n)
                        for m in taps_of(n):
                            conv_tap(m)
                    do(nc.vector.memset(small[:, 60:61], 0.0), "conv_done")
                    dve.wait_ge(sN["pv_done"], len(STEPS))
                    dve.wait_ge(sN["proj_out"], NJ)
                    def differences(v):
                        half = HALVES[v]
                        if v >= 2:
                            dve.wait_ge(sN["lev_k"], v - 1)
                        bv = b.rearrange("p i t -> p (i t)").rearrange("p (n w) -> p n w", w=2 * half)
                        dvw = lds[v % 2].rearrange("p i t -> p (i t)").rearrange("p (n w) -> p n w", w=2 * half)
                        do(nc.vector.tensor_tensor(dvw, bv, bv[:, :, half - 1:half].to_broadcast([P, 2 * S // (2 * half), 2 * half]),
                                                   ALU.subtract), "lev_d")

                    differences(0)
                    for v in range(NLEV):
                        if v + 1 < NLEV:
                            differences(v + 1)
                        dve.wait_ge(sN["lev_e"], v + 1)
                        do(nc.vector.tensor_tensor(lqs[v % 2], gq, lds[v % 2], ALU.mult), "lev_q")
                        if v == 0:
                            dve.wait_ge(sN["mean_done"], 1)
                            for i in range(2):
                                do(nc.vector.scalar_tensor_tensor(mixr[:, 3 + i, :], ps[0][:, :], -1.0 / CC, mixr[:, 3 + i, :],
                                                                  ALU.mult, ALU.add), "cen_done")
                        if v == 2:
                            dve.wait_ge(sN["croot"], 1)
                            for i in range(2):
                                do(nc.vector.tensor_tensor(mixr[:, 3 + i, :], mixr[:, 3 + i, :], ps[1][:, :], ALU.mult), "cnorm")
                        if v >= 1:
                            for c in range(NT):
                                merge(dve, do, v - 1, c)
                    for v in (NLEV - 1, NLEV):
                        for c in range(NT):
                            merge(dve, do, v, c)
                    bc = b.rearrange("p i t -> p (i t)").rearrange("p (n w) -> p n w", w=P)
                    do(nc.vector.tensor_tensor(lq.rearrange("p i t -> p (i t)").rearrange("p (n w) -> p n w", w=P), bc,
                                               bc[:, :, P - 1:P].to_broadcast([P, 2 * NT, P]), ALU.subtract), "el_done")
                    dve.wait_ge(sN["eb_done"], 1)
                    do(nc.vector.tensor_tensor(qexp, gq, ld, ALU.mult), "qexp_done")
                    do(nc.vector.tensor_copy(ebl[:, :, :], ld.rearrange("p i (c t) -> p i c t", t=P)[:, :, :, P - 1]))
                    dve.wait_ge(sN["er_done"], 1)
                    do(nc.vector.tensor_tensor(kdec, gk, lq, ALU.mult), "kdec_done")
                    for c in range(3):
                        dve.wait_ge(sN["upd_done"], c + 1)
                        for i in range(2):
                            u = ps[5 + c][:, 192 * i:192 * i + 192]
                            if c == 0:
                                ins = nc.vector.tensor_copy(st[:, 0, i, :], u)
                            else:
                                ins = nc.vector.scalar_tensor_tensor(st[:, c, i, :], st[:, c - 1, i, :], ebl[:, i, c:c + 1], u,
                                                                     ALU.mult, ALU.add)
                            do(ins, "state_done" if i else None)
                    for h in range(GH):
                        dve.wait_ge(sN["oroot"], h + 1)
                        r = wide[h][0:GV, :]
                        do(nc.vector.scalar_tensor_tensor(r, ps[h][0:GV, :], pc("onorm", 0, GV), r, ALU.mult, ALU.mult))
                        do(nc.vector.tensor_tensor(mixg[0:GV, h, :], r, gr[:, h, :], ALU.mult), "odone")

                @block.gpsimd
                def _(gp):
                    do = engine(gp, cp_)
                    do(nc.gpsimd.memset(AT, 0.0), "at_zero")
                    for i in range(NT):
                        gp.wait_ge(sN["relu_used"], IH * (i + 1))
                        s = sel[:, i, P * i:P * i + P]
                        do(nc.gpsimd.affine_select(out=s, in_=s, pattern=[[-1, P]], compare_op=ALU.is_ge, fill=NEG, base=0,
                                                   channel_multiplier=1), "causal_done")
                    for n, (i, h) in enumerate(STEPS):
                        if n >= 2:
                            gp.wait_ge(sN["lg_out"], n - 1)
                        if h == 0:
                            gp.wait_ge(sN["sel_done"], i + 1)
                        near = 2 if i else 1
                        w0 = P * (i + 1 - near)
                        if w0:
                            do(nc.gpsimd.tensor_scalar(bm[:, n % 2, 0:w0], sel[:, i, 0:w0], bfar[:, h:h + 1], None, ALU.add))
                        do(nc.gpsimd.tensor_tensor(bm[:, n % 2, w0:P * (i + 1)], sel[:, i, w0:P * (i + 1)],
                                                   toep[:, h, 2 * P - P * near:2 * P], ALU.add), "bm_done")
                    for v in range(NLEV):
                        gp.wait_ge(sN["lev_e"], v + 1)
                        if v >= 2:
                            gp.wait_ge(sN["lev_mm"], NT * (v - 1))
                        elif v == 0:
                            gp.wait_ge(sN["proj_out"], NJ)
                        do(nc.gpsimd.tensor_tensor(lks[v % 2], gk, lds[v % 2], ALU.mult), "lev_k")

            XSTEPS = [(t, h) for t in range(NT) for h in range(XH)]
            X_SUMS = [0, 1, 6]
            HALF = [(t, q) for t in range(NT) for q in range(2)]

            def rows_squared(act, do, rows, nt, mark, freed):
                for t in range(nt):
                    freed(act, t)
                    do(nc.scalar.activation(xn[:, t % 2, :], rows[:, t, :], ACT.Square, accum_out=small[:, t:t + 1]))
                    root(do, small[:, 4 + t:5 + t], small[:, t:t + 1], D, mark)

            def rows_turned(pe, nt, ready, bank, tr, out):
                for t in range(nt):
                    pe.wait_ge(sN[ready], t + 1)
                    for q in range(2):
                        n = 2 * t + q
                        if n >= 2:
                            pe.wait_ge(sN[out], n - 1)
                        for c in range(4):
                            last = nc.tensor.transpose(ps[bank + q][:, P * c:P * c + P],
                                                       xn[:, t % 2, P * (4 * q + c):P * (4 * q + c) + P], ident)
                        last.then_inc(sN[tr], 1)

            def rows_normed(dve, do, rows, nt, root, ready, tr, bank, gain, dest, out, freed=None):
                for t in range(nt):
                    dve.wait_ge(sN[root], t + 1)
                    do(nc.vector.reciprocal(small[:, 12 + t:13 + t], small[:, 4 + t:5 + t]))
                    do(nc.vector.tensor_scalar(xn[:, t % 2, :], rows[:, t, :], small[:, 12 + t:13 + t], None, ALU.mult), ready)
                    for q in range(2):
                        dve.wait_ge(sN[tr], 2 * t + q + 1)
                        g = par[:, PC[gain] + 4 * q:PC[gain] + 4 * q + 4].unsqueeze(2).to_broadcast([P, 4, P])
                        do(nc.vector.tensor_tensor(dest[:, 4 * q:4 * q + 4, P * t:P * t + P],
                                                   ps[bank + q][:, :].rearrange("p (c t) -> p c t", t=P), g, ALU.mult), out)

            with nc.Block() as block:
                @block.sync
                def _(sp):
                    sp.dma_start(wcq, layer("w_cq").rearrange("o (c p) n -> p (o c) n", p=P)).then_inc(sN["wcq_in"], 16)
                    sp.dma_start(wco, layer("w_co").rearrange("o (c p) n -> p (o c) n", p=P)).then_inc(sN["wco_in"], 16)
                    sp.dma_start(wr[:, :, 0:NG], layer("w_rg").rearrange("o (c p) n -> p (o c) n", p=P)).then_inc(sN["wr_in"], 16)
                    sp.dma_start(wr[:, :, NG:NG + E], layer("w_re").rearrange("o (c p) n -> p (o c) n", p=P)).then_inc(sN["wr_in"], 16)
                    sp.dma_start(blk[:, 0:NG], layer("b_rg")).then_inc(sN["rb_in"], 16)
                    sp.dma_start(blk[:, NG:NG + E], layer("b_re")).then_inc(sN["rb_in"], 16)
                    for t in range(NT):
                        sp.wait_ge(sN["f_xn"], t + 1)
                        sp.dma_start(hrows[P * t:P * t + P, :], xn[:, t % 2, :]).then_inc(s_hr[t], 16)
                    for t in range(NT):
                        sp.wait_ge(s_hr[t], 16)

                @block.tensor
                def _(pe):
                    rows_turned(pe, 2, "mm_xn", 2, "mm_tr", "mm_T")
                    pe.wait_ge(sN["wo_in"], 32)
                    for n, (t, q) in enumerate(HALF):
                        if n >= 2:
                            pe.wait_ge(sN["x_mid"], n - 1)
                        for c in range(GH + 5):
                            if c < GH:
                                a, w = mixg[0:GV, c, P * t:P * t + P], wog[:, c, 512 * q:512 * q + 512]
                            else:
                                a, w = mixr[:, c - GH, P * t:P * t + P], wor[:, c - GH, 512 * q:512 * q + 512]
                            last = nc.tensor.matmul(ps[n % 2][:, :], a, w, start=(c == 0), stop=(c == GH + 4))
                        last.then_inc(sN["op_done"], 1)
                    pe.wait_ge(sN["mm_T"], 4)
                    pe.wait_ge(sN["wckv_in"], 16)
                    for i in range(2):
                        for c in range(KD):
                            last = nc.tensor.matmul(ps[4][:, M * i:M * i + M], wckv[:, c, P * i:P * i + P], memT[:, c, :],
                                                    start=(c == 0), stop=(c == KD - 1))
                    last.then_inc(sN["cp_done"], 1)
                    for i in range(2):
                        for c in range(KD):
                            last = nc.tensor.matmul(ps[5][:, 256 * i:256 * i + 256], memT[:, c, P * i:P * i + P],
                                                    wckv[:, c, 256:512], start=(c == 0), stop=(c == KD - 1))
                    last.then_inc(sN["cp_done"], 1)
                    rows_turned(pe, NT, "xm_xn", 6, "xm_tr", "xm_hT")
                    pe.wait_ge(sN["xm_hT"], 8)
                    pe.wait_ge(sN["wcq_in"], 16)
                    for i in range(2):
                        for c in range(KD):
                            last = nc.tensor.matmul(ps[2 + i][:, :], wcq[:, c, P * i:P * i + P], hT[:, c, :],
                                                    start=(c == 0), stop=(c == KD - 1))
                        last.then_inc(sN["cp_done"], 1)
                    pe.wait_ge(sN["x_mid"], 8)
                    for n in range(3):
                        pe.wait_ge(sN["cn_sq"], n + 1)
                        nc.tensor.matmul(ps[X_SUMS[n]][:, :], same_head, sq[:, n % 2, :], start=True, stop=True)\
                          .then_inc(sN["cn_sum"], 1)
                    pe.wait_ge(sN["cn_done"], 3)

                    def logits(n):
                        t, h = XSTEPS[n]
                        r = pair_rows(h, XD)
                        if n >= 2:
                            pe.wait_ge(sN["c_exp"], n - 1)
                        nc.tensor.matmul(ps[4 + n % 2][:, 0:M], cqT[r, h // 2, P * t:P * t + P], ckT[r, h // 2, :],
                                         start=True, stop=True).then_inc(sN["cl_done"], 1)

                    def values(n):
                        t, h = XSTEPS[n]
                        pe.wait_ge(sN["c_pto"], n + 1)
                        for j in range(2):
                            last = nc.tensor.matmul(ps[h // 2][pair_rows(h, XD), P * t:P * t + P],
                                                    cv[:, j, XD * h:XD * h + XD], cpT[:, n % 2, j, :], start=(j == 0), stop=(j == 1))
                        last.then_inc(sN["c_pv"], 1)

                    pe.wait_ge(sN["cp_out"], 1)
                    logits(0)
                    logits(1)
                    for n in range(len(XSTEPS)):
                        pe.wait_ge(sN["c_norm"], n + 1)
                        if n >= 2:
                            pe.wait_ge(sN["c_pto"], n - 1)
                        for j in range(2):
                            last = nc.tensor.transpose(ps[6 + n % 2][:, P * j:P * j + P], clg[:, n % 2, P * j:P * j + P], ident)
                        last.then_inc(sN["c_pt"], 1)
                        if n + 2 < len(XSTEPS):
                            logits(n + 2)
                        if n >= 1:
                            values(n - 1)
                    values(len(XSTEPS) - 1)
                    pe.wait_ge(sN["c_o"], 2)
                    pe.wait_ge(sN["wco_in"], 16)
                    for n, (t, q) in enumerate(HALF):
                        if n >= 2:
                            pe.wait_ge(sN["x_cross"], n - 1)
                        for c in range(2):
                            last = nc.tensor.matmul(ps[2 + n % 2][:, :], coT[:, c, P * t:P * t + P], wco[:, c, 512 * q:512 * q + 512],
                                                    start=(c == 0), stop=(c == 1))
                        last.then_inc(sN["co_done"], 1)
                    rows_turned(pe, NT, "f_xn", 6, "f_tr", "f_hT")
                    pe.wait_ge(sN["f_hT"], 8)
                    pe.wait_ge(sN["wr_in"], 32)
                    pe.wait_ge(sN["rb_in"], 32)
                    for t in range(NT):
                        o = ps[4][:, 32 * t:32 * t + NG + E]
                        for c in range(KD):
                            nc.tensor.matmul(o, hT[:, c, P * t:P * t + P], wr[:, c, :], start=(c == 0), stop=False)
                        last = nc.tensor.matmul(o, ones[0:1, :], blk[:, 0:NG + E], start=False, stop=True)
                    last.then_inc(sN["r_done"], 1)
                    pe.wait_ge(sN["r_hot"], 1)
                    for t in range(NT):
                        for j in range(t):
                            nc.tensor.matmul(ps[5][:, E * t:E * t + E], ones[:, :], rout[:, j, 80:96], start=(j == 0), stop=False)
                        nc.tensor.matmul(ps[5][:, E * t:E * t + E], before, rout[:, t, 80:96], start=(t == 0), stop=True)
                    for t in range(NT):
                        last = nc.tensor.matmul(ps[5][:, 64:64 + E], ones[:, :], rout[:, t, 80:96], start=(t == 0), stop=(t == NT - 1))
                    last.then_inc(sN["r_rank"], 1)
                    for n in range(2 * NT):
                        pe.wait_ge(sN["r_one"], n + 1)
                        last = nc.tensor.matmul(ps[4][:, 256:256 + 2 * NBC], oneP[:, n % 2, :], oneB[:, n % 2, :],
                                                start=(n == 0), stop=(n == 2 * NT - 1))
                        last.then_inc(sN["r_slots"], 1)

                @block.scalar
                def _(act):
                    do = engine(act, ca_)
                    act.wait_ge(sN["mem_in"], 16)
                    rows_squared(act, do, mem, 2, "mm_root", lambda e, t: None)

                    def freed_x(e, t):
                        e.wait_ge(sN["x_mid"], 2 * t + 2)
                        e.wait_ge(sN["mm_tr"], 4)
                        if t >= 2:
                            e.wait_ge(sN["xm_tr"], 2 * (t - 1))

                    rows_squared(act, do, x, NT, "xm_root", freed_x)
                    act.wait_ge(sN["cp_done"], 2)
                    do(nc.scalar.activation(cv, ps[5][:, :].rearrange("p (i n) -> p i n", i=2), ACT.Copy), "cp_out", wait=False)
                    for n in range(3):
                        src = ps[4] if n == 0 else ps[1 + n]
                        act.wait_ge(sN["cp_done"], 1 if n == 0 else n + 2)
                        if n >= 2:
                            act.wait_ge(sN["cn_sum"], n - 1)
                        do(nc.scalar.activation(sq[:, n % 2, :], src[:, :], ACT.Square), "cn_sq", wait=False)
                    inverse_roots(act, do, X_SUMS, XD, "cn_sum", "cn_root", outs=wide)

                    def exps(n):
                        act.wait_ge(sN["c_nm"], n + 1)
                        if n >= 2:
                            act.wait_ge(sN["c_pt"], n - 1)
                        nc.scalar.activation(clg[:, n % 2, :], ps[4 + n % 2][:, 0:M], ACT.Exp, bias=small[:, 20 + n % 2:21 + n % 2],
                                             scale=XD ** -0.5, accum_out=small[:, 22 + n % 2:23 + n % 2]).then_inc(sN["c_exp"], 1)

                    exps(0)
                    for n in range(len(XSTEPS)):
                        if n + 1 < len(XSTEPS):
                            exps(n + 1)
                        act.wait_ge(sN["c_pt"], n + 1)
                        if n >= 2:
                            act.wait_ge(sN["c_pv"], n - 1)
                        nc.scalar.activation(cpT[:, n % 2, :, :], ps[6 + n % 2][:, 0:2 * P].rearrange("p (j t) -> p j t", t=P),
                                             ACT.Copy).then_inc(sN["c_pto"], 1)
                    act.wait_ge(sN["c_pv"], len(XSTEPS))
                    for i in range(2):
                        do(nc.scalar.activation(coT[:, i, :], ps[i][:, :], ACT.Copy), "c_o", wait=False)

                    def freed_f(e, t):
                        e.wait_ge(sN["x_cross"], 2 * t + 2)
                        if t >= 2:
                            e.wait_ge(sN["f_tr"], 2 * (t - 1))
                            e.wait_ge(s_hr[t - 2], 16)

                    rows_squared(act, do, x, NT, "f_root", freed_f)
                    act.wait_ge(sN["r_lin"], 1)
                    do(nc.scalar.activation(rout[:, :, 24:28], rout[:, :, 24:28], ACT.Exp), "r_exp")
                    act.wait_ge(sN["r_lin"], 2)
                    do(nc.scalar.activation(rout[:, :, 44:45], rout[:, :, 44:45], ACT.Exp), "r_exp")

                @block.vector
                def _(dve):
                    do = engine(dve, cv_)
                    V = nc.vector
                    rows_normed(dve, do, mem, 2, "mm_root", "mm_xn", "mm_tr", 2, "gmem", memT, "mm_T")
                    for n, (t, q) in enumerate(HALF):
                        dve.wait_ge(sN["op_done"], n + 1)
                        xt = x[:, t, 512 * q:512 * q + 512]
                        do(V.tensor_tensor(xt, xt, ps[n % 2][:, :], ALU.add), "x_mid")
                    rows_normed(dve, do, x, NT, "xm_root", "xm_xn", "xm_tr", 6, "gx", hT, "xm_hT")
                    for n in range(3):
                        src, dst = (ps[4], ckT.rearrange("p i m -> p (i m)")) if n == 0 else (ps[1 + n], cqT[:, n - 1, :])
                        dve.wait_ge(sN["cn_root"], n + 1)
                        do(V.scalar_tensor_tensor(dst, src[:, :], pc("cqn" if n else "ckn"), wide[n], ALU.mult, ALU.mult),
                           "cn_done")

                    def row_max(n):
                        dve.wait_ge(sN["cl_done"], n + 1)
                        do(V.reduce_max(small[:, 24:25], ps[4 + n % 2][:, 0:M], AX))
                        do(V.tensor_scalar(small[:, 20 + n % 2:21 + n % 2], small[:, 24:25], -XD ** -0.5, None, ALU.mult), "c_nm")

                    row_max(0)
                    for n in range(len(XSTEPS)):
                        if n + 1 < len(XSTEPS):
                            row_max(n + 1)
                        dve.wait_ge(sN["c_exp"], n + 1)
                        do(V.reciprocal(small[:, 25:26], small[:, 22 + n % 2:23 + n % 2]))
                        do(V.tensor_scalar(clg[:, n % 2, :], clg[:, n % 2, :], small[:, 25:26], None, ALU.mult), "c_norm")
                    for n, (t, q) in enumerate(HALF):
                        dve.wait_ge(sN["co_done"], n + 1)
                        xt = x[:, t, 512 * q:512 * q + 512]
                        do(V.tensor_tensor(xt, xt, ps[2 + n % 2][:, :], ALU.add), "x_cross")
                    rows_normed(dve, do, x, NT, "f_root", "f_xn", "f_tr", 6, "gffn", hT, "f_hT")

                    def R(a, b):
                        return rout[:, :, a:b]

                    def spread(ap, n):
                        return ap.to_broadcast([P, NT, n])

                    def first_largest(v, hot, m):
                        do(V.reduce_max(m, v, AX))
                        do(V.tensor_tensor(R(48, 52), v, spread(m, 4), ALU.is_equal))
                        do(V.tensor_tensor(R(48, 52), R(48, 52), rout[:, :, 220:224], ALU.mult))
                        do(V.reduce_max(R(52, 53), R(48, 52), AX))
                        do(V.tensor_tensor(hot, R(48, 52), spread(R(52, 53), 4), ALU.is_equal))

                    for t in range(NT):
                        do(V.tensor_scalar(rout[:, t, 220:224], iota[:, 0:4], -1.0, 8.0, ALU.mult, ALU.add))
                    dve.wait_ge(sN["r_done"], 1)
                    do(V.tensor_copy(R(0, NG + E), ps[4][:, 0:P].rearrange("p (t n) -> p t n", n=32)[:, :, 0:NG + E]))
                    first_largest(R(0, 4), R(20, 24), R(40, 41))
                    do(V.tensor_tensor(R(24, 28), R(0, 4), spread(R(40, 41), 4), ALU.subtract), "r_lin")
                    el4 = R(4, 20).rearrange("p t (g e) -> p t g e", e=EG)
                    w16 = R(112, 128).rearrange("p t (g e) -> p t g e", e=EG)
                    do(V.tensor_tensor(w16, el4, R(20, 24).unsqueeze(3).to_broadcast([P, NT, NG, EG]), ALU.mult))
                    do(V.tensor_reduce(R(28, 32), w16.rearrange("p t g e -> p t e g"), AX, ALU.add))
                    first_largest(R(28, 32), R(32, 36), R(42, 43))
                    do(V.scalar_tensor_tensor(R(54, 58), R(32, 36), NEG, R(28, 32), ALU.mult, ALU.add))
                    first_largest(R(54, 58), R(36, 40), R(43, 44))
                    do(V.tensor_tensor(R(44, 45), R(43, 44), R(42, 43), ALU.subtract), "r_lin")
                    dve.wait_ge(sN["r_exp"], 1)
                    do(V.reduce_sum(R(41, 42), R(24, 28), AX))
                    dve.wait_ge(sN["r_exp"], 2)
                    do(V.tensor_scalar(R(58, 59), R(44, 45), 1.0, None, ALU.add))
                    do(V.tensor_tensor(R(58, 59), R(58, 59), R(41, 42), ALU.mult))
                    do(V.reciprocal(R(136, 137), R(58, 59)))
                    do(V.tensor_tensor(R(137, 138), R(136, 137), R(44, 45), ALU.mult))
                    for k in range(2):
                        hot = R(140 + 16 * k, 156 + 16 * k).rearrange("p t (g e) -> p t g e", e=EG)
                        do(V.tensor_tensor(hot, R(20, 24).unsqueeze(3).to_broadcast([P, NT, NG, EG]),
                                           R(32 + 4 * k, 36 + 4 * k).unsqueeze(2).to_broadcast([P, NT, NG, EG]), ALU.mult))
                    do(V.tensor_tensor(R(80, 96), R(140, 156), R(156, 172), ALU.add), "r_hot")
                    dve.wait_ge(sN["r_rank"], 1)
                    cnt, nbk, cum, exc = (rout[:, 0, 172:188], rout[:, 1, 172:188], rout[:, 2, 172:188], rout[:, 3, 172:188])
                    do(V.tensor_copy(cnt, ps[5][:, 64:64 + E]))
                    do(V.tensor_copy(R(96, 112), ps[5][:, 0:64].rearrange("p (t e) -> p t e", e=E)))
                    do(V.tensor_scalar(nbk, cnt, 0.0, None, ALU.is_gt))
                    for k in range(1, S // P):
                        do(V.scalar_tensor_tensor(nbk, cnt, float(P * k), nbk, ALU.is_gt, ALU.add))
                    do(V.tensor_tensor_scan(cum, ones[:, 0:E], nbk, 0.0, ALU.mult, ALU.add))
                    do(V.tensor_tensor(exc, cum, nbk, ALU.subtract))
                    for k in range(2):
                        hot = R(140 + 16 * k, 156 + 16 * k)
                        do(V.tensor_tensor(R(112, 128), hot, R(96, 112), ALU.mult))
                        do(V.reduce_sum(R(128 + k, 129 + k), R(112, 128), AX))
                        do(V.tensor_tensor(R(112, 128), hot, exc.unsqueeze(1).to_broadcast([P, NT, E]), ALU.mult))
                        do(V.reduce_sum(R(130 + k, 131 + k), R(112, 128), AX))
                    do(V.tensor_scalar(R(132, 134), R(128, 130), float(P), None, ALU.is_ge))
                    for k in range(2, S // P):
                        do(V.scalar_tensor_tensor(R(132, 134), R(128, 130), float(P * k), R(132, 134), ALU.is_ge, ALU.add))
                    do(V.scalar_tensor_tensor(R(134, 136), R(132, 134), -float(P), R(128, 130), ALU.mult, ALU.add))
                    do(V.tensor_tensor(R(130, 132), R(130, 132), R(132, 134), ALU.add))
                    do(V.scalar_tensor_tensor(R(138, 140), R(130, 132), float(P), R(134, 136), ALU.mult, ALU.add))
                    do(V.tensor_copy(pair_slot[:, :, :], R(138, 140)))
                    for n in range(2 * NT):
                        t, k = n // 2, n % 2
                        if n >= 2:
                            dve.wait_ge(sN["r_slots"], n - 1)
                        do(V.tensor_scalar(oneP[:, n % 2, :], iota, rout[:, t, 134 + k:135 + k], None, ALU.is_equal))
                        do(V.tensor_scalar(oneB[:, n % 2, 0:NBC], iota[:, 0:NBC], rout[:, t, 130 + k:131 + k], tok[:, t:t + 1],
                                           ALU.is_equal, ALU.mult))
                        do(V.tensor_scalar(oneB[:, n % 2, NBC:2 * NBC], iota[:, 0:NBC], rout[:, t, 130 + k:131 + k],
                                           rout[:, t, 136 + k:137 + k], ALU.is_equal, ALU.mult), "r_one")
                    w = sq[0:1, 0, 0:NBC * E].rearrange("p (b e) -> p b e", e=E)
                    do(V.tensor_tensor(w, iota[0:1, 0:NBC].unsqueeze(2).to_broadcast([1, NBC, E]),
                                       cum[0:1, :].unsqueeze(1).to_broadcast([1, NBC, E]), ALU.is_ge))
                    do(V.reduce_sum(blk[:, 32:32 + NBC], w, AX))
                    do(V.tensor_scalar(blk[:, 32:32 + NBC], blk[:, 32:32 + NBC], float(E - 1), None, ALU.min))
                    tot = rout[0:1, 2, 187:188]
                    do(V.tensor_copy(blki[:, 0:NBC], blk[:, 32:32 + NBC]))
                    do(V.tensor_copy(blki[:, NBC:NBC + 1], tot))
                    do(V.tensor_scalar(blki[:, NBC + 1:NBC + 2], tot, -1.0, None, ALU.add))
                    dve.wait_ge(sN["r_slots"], 2 * NT)
                    do(V.tensor_copy(slots[:, :], ps[4][:, 256:256 + 2 * NBC]))
                    do(V.tensor_copy(slot_tok[:, :], slots[:, 0:NBC]))

            mem_a.close()

            KINDS = (("w_gate", KD, F), ("w_up", KD, F), ("w_down", F // P, D))
            mem_e = ExitStack()

            def sbe(name, shape, dt=F32):
                return mem_e.enter_context(nc.sbuf_tensor(name, shape, dt))

            raw = [sbe(f"raw_{n}", [P, c, w]) for n, c, w in KINDS]
            wh = [sbe(f"head_{n}", [P, c, w], F32R) for n, c, w in KINDS]
            wl = [sbe(f"rest_{n}", [P, c, w], F32R) for n, c, w in KINDS]
            xg = sbe("xg", [P, D])
            xh, xl = sbe("xg_head", [P, KD, P], F32R), sbe("xg_rest", [P, KD, P], F32R)
            he = sbe("he", [P, F])
            hh, hl = sbe("he_head", [P, F // P, P], F32R), sbe("he_rest", [P, F // P, P], F32R)
            yb = sbe("yb", [P, D])

            def part(q, j):
                n = KINDS[q][1] // 2
                return slice(n * j, n * j + n)

            def split(q, j, n):
                return (s_split[q], 2 * n + j) if q < 2 else (s_split[3 - j], n)

            def block_count(eng):
                return eng.value_load(blki[0:1, NBC:NBC + 1], min_val=MINB, max_val=MAXB)

            def last_two_out(eng):
                return eng.value_load(blki[0:1, NBC + 1:NBC + 2], min_val=MINB - 1, max_val=MAXB - 1)

            with nc.Block() as block:
                @block.sync
                def _(sp):
                    def load(q, n, before):
                        e = sp.value_load(blki[0:1, bass.ds(n - 1, 1)], min_val=0, max_val=E - 1)
                        src = A[KINDS[q][0]][bass.ds(l, 1), bass.ds(e, 1)].rearrange("o e (c p) n -> p (o e c) n", p=P)
                        for j in range(2):
                            if before is not None:
                                sp.wait_ge(*split(q, j, before))
                            sp.dma_start(raw[q][:, part(q, j), :], src[:, part(q, j), :]).then_inc(s_raw[q][j], 16)

                    load(0, 1, None)
                    load(1, 1, None)
                    load(0, 2, 1)
                    load(1, 2, 1)
                    load(2, 1, None)
                    with sp.Fori(1, last_two_out(sp)) as k:
                        load(0, k + 2, k + 1)
                        load(1, k + 2, k + 1)
                        load(2, k + 1, k)
                    load(2, block_count(sp), last_two_out(sp))

                @block.gpsimd
                def _(gp):
                    def gather():
                        gp.indirect_dma_start(out=xg[:, :], out_offset=None, in_=hrows,
                                              in_offset=bass.IndirectOffsetOnAxis(ap=idx[:, :], axis=0)).then_inc(s_ga, 16)

                    def rest(n):
                        gp.wait_ge(s_head[2], 2 * n)
                        c = part(2, 0)
                        nc.gpsimd.tensor_tensor(wl[2][:, c, :], raw[2][:, c, :], wh[2][:, c, :].bitcast(F32), ALU.subtract)\
                          .then_inc(s_split[3], 1)

                    def rows(n, again=True):
                        if again:
                            gp.wait_ge(sN["x_free"], n - 1)
                            gp.nop(nofuse=True)
                        nc.gpsimd.tensor_copy(idx[:, :], slot_tok[:, bass.ds(n - 1, 1)]).then_inc(sN["idx"], 1)
                        gp.wait_ge(sN["idx"], n)
                        gp.nop(nofuse=True)
                        gather()

                    rows(1, again=False)
                    rows(2)
                    with gp.Fori(1, last_two_out(gp)) as k:
                        rows(k + 2)
                        rest(k)
                    rest(last_two_out(gp))
                    rest(block_count(gp))

                @block.tensor
                def _(pe):
                    def turn(q, mark):
                        for c in range(4):
                            last = nc.tensor.transpose(ps[4 + q][:, P * c:P * c + P], xg[:, P * (4 * q + c):P * (4 * q + c) + P], ident)
                        last.then_inc(sN[mark], 1)

                    def three_passes(out, a, b, n, wait_half):
                        for c in range(n):
                            if c % (n // 2) == 0:
                                wait_half(2 * c // n)
                            (ah, al), (bh, bl) = a(c), b(c)
                            nc.tensor.matmul(out, ah, bh, start=(c == 0), stop=False)
                            nc.tensor.matmul(out, ah, bl, start=False, stop=False)
                            last = nc.tensor.matmul(out, al, bh, start=False, stop=(c == n - 1))
                        return last

                    def gate_up(n):
                        pe.wait_ge(sN["blk_xl"], 2 * n)
                        for q in range(2):
                            three_passes(ps[q][:, :], lambda c: (xh[:, c, :], xl[:, c, :]),
                                         lambda c: (wh[q][:, c, :], wl[q][:, c, :]), KD,
                                         lambda j: pe.wait_ge(*split(q, j, n))).then_inc(s_used[q], 1)

                    def turn_h(n):
                        pe.wait_ge(sN["blk_h"], n)
                        for c in range(F // P):
                            last = nc.tensor.transpose(ps[6][:, P * c:P * c + P], he[:, P * c:P * c + P], ident)
                        last.then_inc(sN["blk_htr"], 1)

                    def down(n):
                        pe.wait_ge(sN["blk_hl"], n)
                        pe.wait_ge(sN["y_read"], n)
                        for q in range(2):
                            last = three_passes(ps[2 + q][:, :], lambda c: (hh[:, c, :], hl[:, c, :]),
                                                lambda c: (wh[2][:, c, 512 * q:512 * q + 512], wl[2][:, c, 512 * q:512 * q + 512]),
                                                F // P, lambda j: pe.wait_ge(*split(2, j, n)))
                        last.then_inc(s_used[2], 1)

                    def turn_x(n):
                        pe.wait_ge(s_ga, 16 * n)
                        turn(0, "blk_tr")
                        turn(1, "x_free")

                    turn_x(1)
                    gate_up(1)
                    turn_x(2)
                    turn_h(1)
                    gate_up(2)
                    with pe.Fori(1, last_two_out(pe)) as k:
                        turn_x(k + 2)
                        down(k)
                        turn_h(k + 1)
                        gate_up(k + 2)
                    down(last_two_out(pe))
                    turn_h(block_count(pe))
                    down(block_count(pe))

                @block.scalar
                def _(act):
                    act.sem_inc(s_ys, 16)
                    for q in range(3):
                        act.sem_inc(s_head[q], 1)
                    act.wait_ge(s_zero, 16)

                    def head(q, n, before):
                        for j in range(2):
                            act.wait_ge(s_raw[q][j], 16 * n)
                            if before is not None:
                                act.wait_ge(s_used[q], before)
                            nc.scalar.activation(wh[q][:, part(q, j), :], raw[q][:, part(q, j), :], ACT.Copy)\
                              .then_inc(s_head[q], 1)

                    def rows_head(half, n, again=True):
                        act.wait_ge(sN["x_free" if half else "blk_tr"], n)
                        if again and not half:
                            act.wait_ge(s_used[1], n - 1)
                        for c in range(4 * half, 4 * half + 4):
                            last = nc.scalar.activation(xh[:, c, :], ps[4 + half][:, P * (c % 4):P * (c % 4) + P], ACT.Copy,
                                                        scale=pc("gffn", c))
                        last.then_inc(sN["blk_xh"], 1)

                    def silu(n):
                        act.wait_ge(s_used[0], n)
                        nc.scalar.activation(he[:, :], ps[0][:, :], ACT.Silu).then_inc(sN["blk_silu"], 1)

                    def h_head(n):
                        act.wait_ge(sN["blk_htr"], n)
                        nc.scalar.activation(hh[:, :, :], ps[6][:, :].rearrange("p (c t) -> p c t", t=P), ACT.Copy)                          .then_inc(sN["blk_hh"], 1)

                    def store(n):
                        act.wait_ge(sN["y_read"], n + 1)
                        act.dma_start(yrows[bass.ds(P * (n - 1), P), :], yb[:, :]).then_inc(s_ys, 16)

                    rows_head(0, 1, again=False)
                    rows_head(1, 1, again=False)
                    head(0, 1, None)
                    head(1, 1, None)
                    silu(1)
                    head(0, 2, 1)
                    rows_head(0, 2)
                    rows_head(1, 2)
                    head(1, 2, 1)
                    h_head(1)
                    head(2, 1, None)
                    silu(2)
                    with act.Fori(1, last_two_out(act)) as k:
                        head(0, k + 2, k + 1)
                        rows_head(0, k + 2)
                        rows_head(1, k + 2)
                        head(1, k + 2, k + 1)
                        h_head(k + 1)
                        head(2, k + 1, k)
                        store(k)
                        silu(k + 2)
                    h_head(block_count(act))
                    head(2, block_count(act), last_two_out(act))
                    store(last_two_out(act))
                    store(block_count(act))
                    act.wait_ge(s_ys, 16 * block_count(act) + 16)
                    act.nop(nofuse=True)

                @block.vector
                def _(dve):
                    dve.sem_inc(sN["y_read"], 1)
                    for q in range(2):
                        dve.sem_inc(s_split[q], 1)

                    def rest(q, j, n):
                        dve.wait_ge(s_head[q], 2 * n + j)
                        c = part(q, j)
                        nc.vector.tensor_tensor(wl[q][:, c, :], raw[q][:, c, :], wh[q][:, c, :].bitcast(F32), ALU.subtract)\
                          .then_inc(s_split[q], 1)

                    def rows_rest(half, n):
                        dve.wait_ge(sN["blk_xh"], 2 * n - 1 + half)
                        for c in range(4 * half, 4 * half + 4):
                            last = nc.vector.scalar_tensor_tensor(xl[:, c, :], ps[4 + half][:, P * (c % 4):P * (c % 4) + P], pc("gffn", c),
                                                                  xh[:, c, :].bitcast(F32), ALU.mult, ALU.subtract)
                        last.then_inc(sN["blk_xl"], 1)

                    def h_rest(n):
                        dve.wait_ge(sN["blk_hh"], n)
                        nc.vector.tensor_tensor(hl[:, :, :], ps[6][:, :].rearrange("p (c t) -> p c t", t=P), hh[:, :, :].bitcast(F32),
                                                ALU.subtract).then_inc(sN["blk_hl"], 1)

                    def gated(n):
                        dve.wait_ge(sN["blk_silu"], n)
                        dve.wait_ge(s_used[1], n)
                        nc.vector.tensor_tensor(he[:, :], he[:, :], ps[1][:, :], ALU.mult).then_inc(sN["blk_h"], 1)

                    def outputs(n):
                        dve.wait_ge(sN["y_read"], n)
                        nc.vector.tensor_copy(gate[:, :], slots[:, bass.ds(n + (NBC - 1), 1)]).then_inc(sN["gate_in"], 1)
                        dve.wait_ge(sN["gate_in"], n)
                        dve.wait_ge(s_used[2], n)
                        dve.wait_ge(s_ys, 16 * n)
                        for q in range(2):
                            last = nc.vector.tensor_scalar(yb[:, 512 * q:512 * q + 512], ps[2 + q][:, :], gate[:, 0:1], None, ALU.mult)
                        last.then_inc(sN["y_read"], 1)

                    def before_gated(n):
                        rest(0, 0, n)
                        rest(0, 1, n)
                        rows_rest(0, n)
                        rows_rest(1, n)
                        rest(1, 0, n)
                        rest(1, 1, n)

                    before_gated(1)
                    gated(1)
                    before_gated(2)
                    h_rest(1)
                    rest(2, 1, 1)
                    gated(2)
                    with dve.Fori(1, last_two_out(dve)) as k:
                        before_gated(k + 2)
                        outputs(k)
                        h_rest(k + 1)
                        rest(2, 1, k + 1)
                        gated(k + 2)
                    outputs(last_two_out(dve))
                    h_rest(block_count(dve))
                    rest(2, 1, block_count(dve))
                    outputs(block_count(dve))
            mem_e.close()

            mem_c = ExitStack()
            ya = mem_c.enter_context(nc.sbuf_tensor("ya", [P, 4, D], F32))
            with nc.Block() as block:
                @block.gpsimd
                def _(gp):
                    for n in range(2 * NT):
                        t, k = n // 2, n % 2
                        if n >= 4:
                            gp.wait_ge(sN["y_added"], n - 3)
                        gp.indirect_dma_start(out=ya[:, n % 4, :], out_offset=None, in_=yrows,
                                              in_offset=bass.IndirectOffsetOnAxis(ap=pair_slot[:, t, k:k + 1], axis=0))\
                          .then_inc(s_yg[n % 4], 16)

                @block.vector
                def _(dve):
                    for n in range(2 * NT):
                        t, k = n // 2, n % 2
                        dve.wait_ge(s_yg[n % 4], 16 * (n // 4 + 1))
                        if k:
                            dve.wait_ge(sN["y_added"], n)
                        nc.vector.tensor_tensor(x[:, t, :], x[:, t, :], ya[:, n % 4, :], ALU.add).then_inc(sN["y_added"], 1)
            mem_c.close()

        with nc.Block() as block:
            @block.sync
            def _(sp):
                sp.dma_start(out[0].rearrange("(n p) d -> p n d", p=P), x[:, :, :]).then_inc(s_out, 16)
                sp.wait_ge(s_out, 16)


_INS = ["x", "mem", "rel_bias", "norm_mix", "w_in", "gla_wa2", "gla_ba", "gla_onorm", "dsa_qnorm", "dsa_knorm", "conv_w",
        "conv_b", "conv_ln_g", "conv_ln_b", "w_out", "norm_x", "norm_mem", "w_cq", "w_ckv", "x_qnorm", "x_knorm", "w_co",
        "norm_ffn", "w_rg", "b_rg", "w_re", "b_re", "w_gate", "w_up", "w_down"]


def kernel(**inputs):
    import concourse.bacc as _bacc
    from concourse.bass_utils import run_bass_kernel_spmd as _run

    nc = _bacc.Bacc("TRN2", target_bir_lowering=False, num_devices=1)
    arrays, handles = {}, {}
    cf, onehot, cmask = host_constants()
    for name, a in [(n, inputs[n]) for n in _INS] + [("cf", cf), ("onehot", onehot), ("cmask", cmask)]:
        a = np.ascontiguousarray(a)
        arrays[f"in_{name}"] = a
        handles[name] = nc.dram_tensor(f"in_{name}", a.shape, mybir.dt.from_np(a.dtype), kind="ExternalInput").ap()
    out = nc.dram_tensor("out_0", (1, S, D), F32, kind="ExternalOutput").ap()
    program(nc, handles, out)
    r = _run(nc, [arrays], core_ids=[0])
    return r.results[0]["out_0"]
```
